# Optimizing a Trainium2 kernel written in Bass

```python
import math
import jax
import jax.numpy as jnp
from jax import lax
import numpy as np

D_MODEL = 1024
BATCH = 1
SEQ = 256
DEPTH = 2

GRID_W = 64
CTX_LEN = 256
BLOCK = 128
EPS = 1e-6
ROPE_THETA = 10000.0

A_HEADS = 8
A_KV_HEADS = 2
A_HEAD_DIM = 128
A_Q = A_HEADS * A_HEAD_DIM
A_KV = A_KV_HEADS * A_HEAD_DIM
B_WIDTH = 512
B_CONV = 31
EVEN_IN = A_Q + 2 * A_KV + 2 * B_WIDTH
EVEN_OUT = A_Q + B_WIDTH

C_HEADS = 16
C_KV_HEADS = 2
C_HEAD_DIM = 64
C_WINDOW = 128
C_Q = C_HEADS * C_HEAD_DIM
C_KV = C_KV_HEADS * C_HEAD_DIM
D_INNER = 1024
D_HEAD_DIM = 64
D_HEADS = D_INNER // D_HEAD_DIM
D_STATE = 128
D_GROUPS = 2
D_CONV = 5
D_CHUNK = 128
D_XBC = D_INNER + 2 * D_GROUPS * D_STATE
ODD_CTX_LO = C_Q
ODD_CTX_HI = C_Q + 2 * C_KV + D_XBC + 2 * D_HEADS
ODD_IN = ODD_CTX_HI + D_INNER
ODD_OUT = C_Q + D_INNER

FFN_HIDDEN = -(-8 * D_MODEL // (3 * 256)) * 256

kernel_name = 'hybrid_prefix_diffusion_trunk'

def rms_norm(x, g):
    xf = x.astype(jnp.float32)
    y = xf * lax.rsqrt(jnp.mean(xf * xf, axis=-1, keepdims=True) + EPS)
    return (y * g.astype(jnp.float32)).astype(x.dtype)

def layer_norm(x, g, b):
    xf = x.astype(jnp.float32)
    mu = jnp.mean(xf, axis=-1, keepdims=True)
    var = jnp.mean(jnp.square(xf - mu), axis=-1, keepdims=True)
    y = (xf - mu) * lax.rsqrt(var + EPS) * g.astype(jnp.float32) + b.astype(jnp.float32)
    return y.astype(x.dtype)

def modulate(h, shift, scale):
    return h * (1.0 + scale) + shift

def heads(t, d):
    return t.reshape(t.shape[:-1] + (t.shape[-1] // d, d))

def rope_tables(L, head_dim, dtype):
    ROWS = L // GRID_W
    row = jnp.repeat(jnp.arange(ROWS), GRID_W).astype(jnp.float32)
    col = jnp.tile(jnp.arange(GRID_W), ROWS).astype(jnp.float32)
    quarter = head_dim // 4
    inv = ROPE_THETA ** (-jnp.arange(quarter, dtype=jnp.float32) / quarter)
    ar = row[:, None] * inv
    ac = col[:, None] * inv
    ang = jnp.concatenate([ar, ar, ac, ac], axis=-1)
    return jnp.cos(ang).astype(dtype)[:, None, :], jnp.sin(ang).astype(dtype)[:, None, :]

def apply_rope(x, cos, sin):
    q = x.shape[-1] // 4
    xs = x.reshape(x.shape[:-1] + (2, 2, q))
    rot = jnp.stack([-xs[..., 1, :], xs[..., 0, :]], axis=-2).reshape(x.shape)
    return x * cos + rot * sin

def softmax_with_sink(s, sink):
    if sink is None:
        return jax.nn.softmax(s, axis=-1)
    hkv, g = s.shape[1], s.shape[2]
    col = jnp.broadcast_to(sink.astype(jnp.float32).reshape(hkv, g)[None, :, :, None, None], s.shape[:-1] + (1,))
    return jax.nn.softmax(jnp.concatenate([s, col], axis=-1), axis=-1)[..., :-1]

def dense_block_attention(q, k, v, sink=None):
    b, Lq, hq, d = q.shape
    hkv = k.shape[2]
    g = hq // hkv
    nb = Lq // BLOCK
    qb = jnp.moveaxis((q * d ** -0.5).reshape(b, nb, BLOCK, hkv, g, d), 1, 0)

    def one(qi):
        s = jnp.einsum('bqkgd,bskd->bkgqs', qi, k).astype(jnp.float32)
        p = softmax_with_sink(s, sink).astype(v.dtype)
        return jnp.einsum('bkgqs,bskd->bqkgd', p, v)

    o = lax.map(one, qb)
    return jnp.moveaxis(o, 0, 1).reshape(b, Lq, hq * d)

def banded_block_attention(q, k, v, k_ctx, v_ctx, sink):
    b, L, hq, d = q.shape
    hkv = k.shape[2]
    g = hq // hkv
    nb = L // BLOCK
    W = C_WINDOW
    span = BLOCK + 2 * W
    qb = jnp.moveaxis((q * d ** -0.5).reshape(b, nb, BLOCK, hkv, g, d), 1, 0)
    kp = jnp.pad(k, ((0, 0), (W, W), (0, 0), (0, 0)))
    vp = jnp.pad(v, ((0, 0), (W, W), (0, 0), (0, 0)))

    def one(args):
        qi, n = args
        start = n * BLOCK
        kb = lax.dynamic_slice_in_dim(kp, start, span, axis=1)
        vb = lax.dynamic_slice_in_dim(vp, start, span, axis=1)
        qpos = start + jnp.arange(BLOCK)
        kpos = start - W + jnp.arange(span)
        band = (jnp.abs(qpos[:, None] - kpos[None, :]) <= W) & ((kpos >= 0) & (kpos < L))[None, :]
        s_lat = jnp.where(band, jnp.einsum('bqkgd,bskd->bkgqs', qi, kb).astype(jnp.float32), -jnp.inf)
        s_ctx = jnp.einsum('bqkgd,bskd->bkgqs', qi, k_ctx).astype(jnp.float32)
        p = softmax_with_sink(jnp.concatenate([s_lat, s_ctx], axis=-1), sink).astype(v.dtype)
        return (jnp.einsum('bkgqs,bskd->bqkgd', p[..., :span], vb)
                + jnp.einsum('bkgqs,bskd->bqkgd', p[..., span:], v_ctx))

    o = lax.map(one, (qb, jnp.arange(nb)))
    return jnp.moveaxis(o, 0, 1).reshape(b, L, hq * d)

def depthwise_conv(x, w, bias):
    K = w.shape[0]
    pad = K // 2
    y = lax.conv_general_dilated(x, w.astype(x.dtype)[:, None, :], window_strides=(1,),
                                 padding=[(pad, K - 1 - pad)],
                                 dimension_numbers=('NWC', 'WIO', 'NWC'),
                                 feature_group_count=x.shape[-1])
    return y + bias.astype(x.dtype)

def conv_module(u, dw_w, dw_b, cn_g, cn_b):
    a, gte = jnp.split(u, 2, axis=-1)
    hdn = depthwise_conv(a * jax.nn.sigmoid(gte), dw_w, dw_b)
    return jax.nn.silu(layer_norm(hdn, cn_g, cn_b))

def ssm_inputs(xbc, dtr, conv_w, conv_b, dt_bias):
    b, n, _ = xbc.shape
    xbc = jax.nn.silu(depthwise_conv(xbc, conv_w, conv_b))
    xs, Bm, Cm = jnp.split(xbc, [D_INNER, D_INNER + D_GROUPS * D_STATE], axis=-1)
    dt = jax.nn.softplus(dtr.astype(jnp.float32).reshape(b, n, 2, D_HEADS) + dt_bias.astype(jnp.float32))
    return (heads(xs, D_HEAD_DIM), Bm.reshape(b, n, D_GROUPS, D_STATE),
            Cm.reshape(b, n, D_GROUPS, D_STATE), dt)

def ssd_scan(xdt, a, Bm, Cm, h0):
    b, L, H, P = xdt.shape
    G, N = Bm.shape[2], Bm.shape[3]
    hg = H // G
    Q = D_CHUNK
    nc = L // Q
    xdt = xdt.reshape(b, nc, Q, G, hg, P)
    acs = jnp.cumsum(a.reshape(b, nc, Q, G, hg), axis=2)
    Bm = Bm.reshape(b, nc, Q, G, N).astype(jnp.float32)
    Cm = Cm.reshape(b, nc, Q, G, N).astype(jnp.float32)
    lower = jnp.tril(jnp.ones((Q, Q), dtype=bool))[:, :, None, None]
    seg = acs[:, :, :, None] - acs[:, :, None, :]
    decay = jnp.exp(jnp.where(lower, seg, -jnp.inf))
    cb = jnp.einsum('bcign,bcjgn->bcijg', Cm, Bm)
    y = jnp.einsum('bcijgh,bcjghp->bcighp', cb[..., None] * decay, xdt)
    xw = xdt * jnp.exp(acs[:, :, -1:] - acs)[..., None]
    states = jnp.einsum('bcjgn,bcjghp->bcghpn', Bm, xw)
    chunk_decay = jnp.exp(acs[:, :, -1])

    def step(h, inp):
        s, dcy = inp
        return h * dcy[..., None, None] + s, h

    h_T, h_in = lax.scan(step, h0.reshape(b, G, hg, P, N),
                         (jnp.moveaxis(states, 1, 0), jnp.moveaxis(chunk_decay, 1, 0)))
    h_in = jnp.moveaxis(h_in, 0, 1)
    y = y + jnp.einsum('bcign,bcghpn->bcighp', Cm, h_in) * jnp.exp(acs)[..., None]
    return y.reshape(b, L, H, P), h_T.reshape(b, H, P, N)

def ssd_final_state(xdt, a, Bm):
    b, L, H, P = xdt.shape
    G, N = Bm.shape[2], Bm.shape[3]
    acs = jnp.cumsum(a, axis=1)
    xw = (xdt * jnp.exp(acs[:, -1:] - acs)[..., None]).reshape(b, L, G, H // G, P)
    return jnp.einsum('blgn,blghp->bghpn', Bm.astype(jnp.float32), xw).reshape(b, H, P, N)

def swiglu(h, w_in, w_out):
    gte, up = jnp.split(h @ w_in, 2, axis=-1)
    return (jax.nn.silu(gte) * up) @ w_out

def even_mixer(h, hc, w_in, w_out, q_g, k_g, dw_w, dw_b, cn_g, cn_b, need_ctx):
    b, L, _ = h.shape
    cos, sin = rope_tables(L, A_HEAD_DIM, h.dtype)
    cuts = [A_Q, A_Q + A_KV, A_Q + 2 * A_KV]
    q, k, v, glu = jnp.split(h @ w_in, cuts, axis=-1)
    if need_ctx:
        qc, kc, vc, gluc = jnp.split(hc @ w_in, cuts, axis=-1)
    else:
        kc, vc = jnp.split(hc @ w_in[:, A_Q:A_Q + 2 * A_KV], [A_KV], axis=-1)
    q = apply_rope(rms_norm(heads(q, A_HEAD_DIM), q_g), cos, sin)
    k = apply_rope(rms_norm(heads(k, A_HEAD_DIM), k_g), cos, sin)
    kc = rms_norm(heads(kc, A_HEAD_DIM), k_g)
    v, vc = heads(v, A_HEAD_DIM), heads(vc, A_HEAD_DIM)
    attn = dense_block_attention(q, jnp.concatenate([kc, k], axis=1), jnp.concatenate([vc, v], axis=1))
    conv = conv_module(glu, dw_w, dw_b, cn_g, cn_b)
    out = jnp.concatenate([attn, conv], axis=-1) @ w_out
    out_c = None
    if need_ctx:
        qc = rms_norm(heads(qc, A_HEAD_DIM), q_g)
        out_c = jnp.concatenate([dense_block_attention(qc, kc, vc),
                                 conv_module(gluc, dw_w, dw_b, cn_g, cn_b)], axis=-1) @ w_out
    return out, out_c

def odd_mixer(h, hc, w_in, w_out, q_g, k_g, sink, conv_w, conv_b, dt_bias, A_log, D_skip, gnorm_g, need_ctx):
    b, L, _ = h.shape
    f32 = jnp.float32
    cos, sin = rope_tables(L, C_HEAD_DIM, h.dtype)
    cuts = [C_Q, C_Q + C_KV, C_Q + 2 * C_KV, C_Q + 2 * C_KV + D_XBC, ODD_CTX_HI]
    q, k, v, xbc, dtr, z = jnp.split(h @ w_in, cuts, axis=-1)
    if need_ctx:
        qc, kc, vc, xbcc, dtrc, zc = jnp.split(hc @ w_in, cuts, axis=-1)
    else:
        kc, vc, xbcc, dtrc = jnp.split(hc @ w_in[:, ODD_CTX_LO:ODD_CTX_HI],
                                       [C_KV, 2 * C_KV, 2 * C_KV + D_XBC], axis=-1)
    q = apply_rope(rms_norm(heads(q, C_HEAD_DIM), q_g), cos, sin)
    k = apply_rope(rms_norm(heads(k, C_HEAD_DIM), k_g), cos, sin)
    kc = rms_norm(heads(kc, C_HEAD_DIM), k_g)
    v, vc = heads(v, C_HEAD_DIM), heads(vc, C_HEAD_DIM)
    attn = banded_block_attention(q, k, v, kc, vc, sink)
    A = -jnp.exp(A_log.astype(f32))
    xs, Bm, Cm, dt = ssm_inputs(xbc, dtr, conv_w, conv_b, dt_bias)
    xsc, Bc, Cc, dtc = ssm_inputs(xbcc, dtrc, conv_w, conv_b, dt_bias)
    Dk = D_skip.astype(f32)[:, None]
    y = Dk * xs.astype(f32)
    yc = Dk * xsc.astype(f32) if need_ctx else None
    for dirn in (0, 1):
        rev = (lambda t: jnp.flip(t, axis=1)) if dirn else (lambda t: t)
        xdt_c = rev(xsc.astype(f32) * dtc[..., dirn, :, None])
        a_c = rev(dtc[..., dirn, :] * A[dirn])
        if need_ctx:
            y_c, h_c = ssd_scan(xdt_c, a_c, rev(Bc), rev(Cc), jnp.zeros((b, D_HEADS, D_HEAD_DIM, D_STATE), f32))
            yc = yc + rev(y_c)
        else:
            h_c = ssd_final_state(xdt_c, a_c, rev(Bc))
        y_l, _ = ssd_scan(rev(xs.astype(f32) * dt[..., dirn, :, None]), rev(dt[..., dirn, :] * A[dirn]),
                          rev(Bm), rev(Cm), h_c)
        y = y + rev(y_l)
    ssm = rms_norm(y.reshape(b, L, D_INNER) * jax.nn.silu(z.astype(f32)), gnorm_g).astype(h.dtype)
    out = jnp.concatenate([attn, ssm], axis=-1) @ w_out
    out_c = None
    if need_ctx:
        qc = rms_norm(heads(qc, C_HEAD_DIM), q_g)
        ssm_c = rms_norm(yc.reshape(b, -1, D_INNER) * jax.nn.silu(zc.astype(f32)), gnorm_g).astype(h.dtype)
        out_c = jnp.concatenate([dense_block_attention(qc, kc, vc, sink), ssm_c], axis=-1) @ w_out
    return out, out_c

def setup_inputs(seed: int = 0) -> dict:
    key = jax.random.key(seed)
    ks = iter(jax.random.split(key, 40))
    f32 = jnp.float32
    D = D_MODEL
    NE = (DEPTH + 1) // 2
    NO = DEPTH // 2

    def nrm(shape, scale):
        return jax.random.normal(next(ks), shape, f32) * scale

    inp = {}
    inp['x'] = nrm((BATCH, SEQ, D), 1.0)
    inp['c'] = nrm((BATCH, D), 1.0)
    inp['ctx'] = nrm((BATCH, CTX_LEN, D), 1.0)
    inp['c_ctx'] = nrm((D,), 1.0)
    inp['mod_w'] = nrm((DEPTH, D, 6 * D), 0.5 * D ** -0.5)
    inp['mod_b'] = nrm((DEPTH, 6 * D), 0.01)
    inp['norm1_g'] = 1.0 + nrm((DEPTH, D), 0.05)
    inp['norm2_g'] = 1.0 + nrm((DEPTH, D), 0.05)
    inp['ffn_w_in'] = nrm((DEPTH, D, 2 * FFN_HIDDEN), D ** -0.5)
    inp['ffn_w_out'] = nrm((DEPTH, FFN_HIDDEN, D), FFN_HIDDEN ** -0.5)
    inp['ev_w_in'] = nrm((NE, D, EVEN_IN), D ** -0.5)
    inp['ev_w_out'] = nrm((NE, EVEN_OUT, D), EVEN_OUT ** -0.5)
    inp['ev_q_g'] = 1.0 + nrm((NE, A_HEAD_DIM), 0.05)
    inp['ev_k_g'] = 1.0 + nrm((NE, A_HEAD_DIM), 0.05)
    inp['ev_dw_w'] = nrm((NE, B_CONV, B_WIDTH), B_CONV ** -0.5)
    inp['ev_dw_b'] = nrm((NE, B_WIDTH), 0.01)
    inp['ev_cn_g'] = 1.0 + nrm((NE, B_WIDTH), 0.05)
    inp['ev_cn_b'] = nrm((NE, B_WIDTH), 0.01)
    inp['od_w_in'] = nrm((NO, D, ODD_IN), D ** -0.5)
    inp['od_w_out'] = nrm((NO, ODD_OUT, D), ODD_OUT ** -0.5)
    inp['od_q_g'] = 1.0 + nrm((NO, C_HEAD_DIM), 0.05)
    inp['od_k_g'] = 1.0 + nrm((NO, C_HEAD_DIM), 0.05)
    inp['od_sink'] = nrm((NO, C_HEADS), 0.5)
    inp['od_conv_w'] = nrm((NO, D_CONV, D_XBC), D_CONV ** -0.5)
    inp['od_conv_b'] = nrm((NO, D_XBC), 0.01)
    dt0 = jnp.exp(jax.random.uniform(next(ks), (NO, 2, D_HEADS), f32, math.log(1e-3), math.log(1e-1)))
    inp['od_dt_bias'] = dt0 + jnp.log(-jnp.expm1(-dt0))
    inp['od_A_log'] = jnp.log(jax.random.uniform(next(ks), (NO, 2, D_HEADS), f32, 1.0, 16.0))
    inp['od_D'] = 1.0 + nrm((NO, D_HEADS), 0.1)
    inp['od_gnorm_g'] = 1.0 + nrm((NO, D_INNER), 0.05)
    return inp

def reference(x, c, ctx, c_ctx, mod_w, mod_b, norm1_g, norm2_g, ffn_w_in, ffn_w_out,
              ev_w_in, ev_w_out, ev_q_g, ev_k_g, ev_dw_w, ev_dw_b, ev_cn_g, ev_cn_b,
              od_w_in, od_w_out, od_q_g, od_k_g, od_sink, od_conv_w, od_conv_b,
              od_dt_bias, od_A_log, od_D, od_gnorm_g):
    cx = ctx
    for l in range(DEPTH):
        need_ctx = l < DEPTH - 1
        i = l // 2
        sh1, sc1, g1, sh2, sc2, g2 = jnp.split((jax.nn.silu(c) @ mod_w[l] + mod_b[l])[:, None, :], 6, axis=-1)
        csh1, csc1, cg1, csh2, csc2, cg2 = jnp.split(jax.nn.silu(c_ctx) @ mod_w[l] + mod_b[l], 6)
        h = modulate(rms_norm(x, norm1_g[l]), sh1, sc1)
        hc = modulate(rms_norm(cx, norm1_g[l]), csh1, csc1)
        if l % 2 == 0:
            o, oc = even_mixer(h, hc, ev_w_in[i], ev_w_out[i], ev_q_g[i], ev_k_g[i], ev_dw_w[i], ev_dw_b[i],
                               ev_cn_g[i], ev_cn_b[i], need_ctx)
        else:
            o, oc = odd_mixer(h, hc, od_w_in[i], od_w_out[i], od_q_g[i], od_k_g[i], od_sink[i], od_conv_w[i],
                              od_conv_b[i], od_dt_bias[i], od_A_log[i], od_D[i], od_gnorm_g[i], need_ctx)
        x = x + g1 * o
        x = x + g2 * swiglu(modulate(rms_norm(x, norm2_g[l]), sh2, sc2), ffn_w_in[l], ffn_w_out[l])
        if need_ctx:
            cx = cx + cg1 * oc
            cx = cx + cg2 * swiglu(modulate(rms_norm(cx, norm2_g[l]), csh2, csc2), ffn_w_in[l], ffn_w_out[l])
    return x


_drawn_inputs = setup_inputs


def setup_inputs(seed=0):
    import zlib

    import numpy as np

    out = dict(_drawn_inputs(seed))
    spreads = {}
    factors = {'ctx': 2.688,
     'mod_b': 3.725,
     'norm1_g': 3.541,
     'ev_q_g': 8.0,
     'ev_k_g': 8.0,
     'ev_dw_b': 8.0,
     'ev_cn_g': 8.0,
     'ev_cn_b': 22.299,
     'od_q_g': 8.0,
     'od_k_g': 8.0,
     'od_sink': 8.0,
     'od_conv_b': 37.188,
     'od_D': 63.16,
     'od_gnorm_g': 5.23}
    for name, (base, spread) in spreads.items():
        noise = np.random.default_rng([zlib.crc32(name.encode()), seed]).standard_normal(out[name].shape)
        drawn = base * np.exp(spread * noise) if base else spread * noise
        out[name] = jnp.asarray(drawn.astype(out[name].dtype))
    for name, factor in factors.items():
        out[name] = (out[name] * factor).astype(out[name].dtype)
    return out
```

```python
import math
from contextlib import ExitStack

import numpy as np

import concourse.bass as bass
from concourse import mybir

F32 = mybir.dt.float32
F32R = mybir.dt.float32r
ALU = mybir.AluOpType
ACT = mybir.ActivationFunctionType
AX = mybir.AxisListType

P = 128
D = 1024
KD = D // P
LAT = 256
CTX = 256
T = LAT + CTX
TT = T // P
LT = LAT // P
DEPTH = 2
EPS = 1e-6
GRID_W = 64
THETA = 10000.0

A_HEADS, A_KV, A_HD = 8, 2, 128
B_WIDTH, B_CONV = 512, 31
BT = B_WIDTH // P
C_HEADS, C_HD, C_WINDOW = 16, 64, 128
S_HEADS, S_HD, S_STATE, S_GROUPS, S_CONV = 16, 64, 128, 2, 5
S_INNER = S_HEADS * S_HD
XBC_T = (S_INNER + 2 * S_GROUPS * S_STATE) // P
HG = S_HEADS // S_GROUPS
FFN = 2816
HALF = (12, 10)
BC = 256
RAW_SLOTS = 4
MOD_COLS = 2048
NEG = -1e30

CONST_COLS = {}


def _const_layout():
    at = 0
    for name, n in (("ident", P), ("ones", P), ("rotA", P), ("rotC", P), ("upto", P), ("from", P),
                    ("before", P), ("after", P), ("pair", P), ("headA", 32), ("headC", 32),
                    ("mask", 2 * P), ("cosA", LAT), ("sinA", LAT), ("cosC", LAT), ("sinC", LAT)):
        CONST_COLS[name] = (at, n)
        at += n
    return at


CONST_N = _const_layout()


def _rope(head_dim):
    rows = LAT // GRID_W
    row = np.repeat(np.arange(rows), GRID_W).astype(np.float32)
    col = np.tile(np.arange(GRID_W), rows).astype(np.float32)
    quarter = head_dim // 4
    inv = (np.float32(THETA) ** (-np.arange(quarter, dtype=np.float32) / np.float32(quarter))).astype(np.float32)
    ar, ac = row[:, None] * inv, col[:, None] * inv
    ang = np.concatenate([ar, ar, ac, ac], axis=-1)
    reps = P // head_dim
    return (np.tile(np.cos(ang).T.astype(np.float32), (reps, 1)),
            np.tile(np.sin(ang).T.astype(np.float32), (reps, 1)))


def _rot(head_dim):
    q = head_dim // 4
    m = np.zeros((P, P), np.float32)
    for o in range(P):
        if (o // q) % 2 == 0:
            m[o + q, o] = -1.0
        else:
            m[o - q, o] = 1.0
    return m


def constants():
    c = np.zeros((P, CONST_N), np.float32)
    k, i = np.arange(P)[:, None], np.arange(P)[None, :]

    def put(name, a):
        at, n = CONST_COLS[name]
        c[:, at:at + n] = a

    put("ident", np.eye(P))
    put("ones", 1.0)
    put("rotA", _rot(A_HD))
    put("rotC", _rot(C_HD))
    put("upto", k <= i)
    put("from", k >= i)
    put("before", k < i)
    put("after", k > i)
    put("pair", (k // C_HD) == (i // C_HD))
    j = np.arange(32)[None, :]
    put("headA", np.broadcast_to(j == 15, (P, 32)))
    put("headC", ((j == 15) & (k < C_HD)) | ((j == 16) & (k >= C_HD)))
    put("mask", np.concatenate([np.where(i <= k, 0.0, NEG), np.where(i >= k, 0.0, NEG)], axis=1))
    for name, hd in (("A", A_HD), ("C", C_HD)):
        cos, sin = _rope(hd)
        put("cos" + name, cos)
        put("sin" + name, sin)
    return c


MODB, N1G, N2G = 0, 96, 112
DWB, CNG, CNB, CVB, GNG, CVEC, AQG, AKG, CQG, CKG, CVW = 128, 132, 136, 140, 152, 160, 176, 177, 178, 179, 180
DWW = 240
VEC_N = 364
SH1, SC1, G1, SH2, SC2, G2 = 0, 8, 16, 24, 32, 40


class Chain:

    def __init__(self, eng, sem):
        self.eng, self.sem, self.n, self.it, self.per = eng, sem, 0, None, 0

    def __call__(self, ins):
        ins.then_inc(self.sem, 1)
        self.n += 1
        self.eng.wait_ge(self.sem, self.n if self.it is None else self.it * self.per + self.n)

    def enter(self, it, per):
        self.it, self.per, self.n0 = it, per, self.n

    def leave(self, times):
        assert self.n - self.n0 == self.per, (self.n - self.n0, self.per)
        self.n = self.n0 + self.per * times
        self.it = None


def at(base, it=None, per=0):
    return base if it is None or per == 0 else it * per + base


def build_trunk(nc, a, out):
    with ExitStack() as ctx:
        def sem(name):
            return ctx.enter_context(nc.semaphore(name))

        def psum(name, shape):
            return ctx.enter_context(nc.psum_tensor(name, shape, F32))

        base = (nc.sbuf_base + 31) // 32 * 32
        room = nc.sbuf_usable_end - base - 32
        ctx.enter_context(nc.sbuf_tensor("arena", [P, room // 4], F32))
        place = [base]

        def region(size):
            start = place[0]
            place[0] += (size + 31) // 32 * 32
            assert place[0] <= base + room, (place[0], base + room)
            return start

        def view(name, shape, offset, dtype=F32):
            return nc.alloc_sbuf_tensor_at(name, [P] + list(shape), dtype, offset=offset)

        r_x, r_h, r_big = region(KD * T * 4), region(2 * KD * T * 4), region(2 * 12 * T * 4)
        r_raw, r_split = region(RAW_SLOTS * 8192), region(4 * 8192)
        r_const, r_misc = region(CONST_N * 4), region(29632)
        X = view("X", [KD, T], r_x)
        Hhi = view("Hhi", [KD, T], r_h, F32R)
        Hlo = view("Hlo", [KD, T], r_h + KD * T * 4, F32R)
        hid_hi = view("hid_hi", [12, T], r_big, F32R)
        hid_lo = view("hid_lo", [12, T], r_big + 12 * T * 4, F32R)
        mixC_hi = view("mixC_hi", [16, LAT], r_big, F32R)
        mixC_lo = view("mixC_lo", [16, LAT], r_big + 16 * LAT * 4, F32R)
        raw = view("raw", [RAW_SLOTS, 2048], r_raw)
        w_hi = view("w_hi", [2, 2048], r_split, F32R)
        w_lo = view("w_lo", [2, 2048], r_split + 16384, F32R)
        const = view("const", [CONST_N], r_const)
        modc = view("modc", [512], region(2048))
        vec = view("vec", [VEC_N], region(VEC_N * 4))
        cvec = view("cvec", [KD, 32], region(1024))
        mod = view("mod", [DEPTH, 48, 2], region(768))
        gain = view("gain", [4, KD, 2], region(256))
        rows = view("rows", [96], region(384))
        qsc = view("qsc", [TT, 16], region(256))
        sm = view("sm", [3, 8], region(96))
        ysum = view("ysum", [4], region(32))
        epsc = view("epsc", [1], region(32))
        DTB, ALOG, DSK, SINK = rows[:, 0:32], rows[:, 32:64], rows[:, 64:80], rows[:, 80:96]
        assert VEC_N == DWW + B_CONV * BT

        xin = view("xin", [TT, D], r_h)
        vrow = view("vrow", [3, P], r_big)
        n_sq = view("n_sq", [2, T], r_big + 2048)
        n_rt = view("n_rt", [T], r_big + 6144)
        n_rs = view("n_rs", [T], r_big + 8192)
        n_t = view("n_t", [T], r_big + 10240)
        n_h = view("n_h", [2, T], r_big + 12288)
        QK = view("QK", [A_KV + A_HEADS, T], r_misc)
        U = view("U", [BT, 2, LAT + B_CONV - 1], r_misc + 20480)
        sgate = view("sgate", [BT, T], r_big)
        sqA = view("sqA", [2, 2, T], r_big + 8192)
        ptap = view("ptap", [T], r_big + 20480)
        ropeT = view("ropeT", [2, LAT], r_big + 32768 - 2048)
        V = view("V", [TT, A_KV * A_HD], r_big + 8 * T * 4)
        Y = view("Y", [BT, T], r_big + 20 * T * 4)
        prob = view("prob", [3, T], r_h)
        probT = view("probT", [2, T], r_h + 6144)
        yc = view("yc", [BT, T], r_h + 10240)
        yq = view("yq", [2, T], r_h + 18432)
        l_rt = view("l_rt", [T], r_h + 22528)
        yz = view("yz", [2, T], r_h + 24576)
        qrow = view("qrow", [T], r_h + 28672)
        krt = view("krt", [2, T], r_big + 24576)
        Q = view("Q", [KD, LAT], r_misc)
        Kc = view("Kc", [T], r_misc + 8192)
        K2 = view("K2", [2, T], r_misc + 10240)
        Vc = view("Vc", [TT, 2 * C_HD], r_misc + 14336)
        Z = view("Z", [LT, S_INNER], r_misc + 16384)
        dts = view("dts", [8, TT * 32], r_misc + 24576)
        dt_, da = dts[:, 6, :], dts[:, 7, :]
        XB = view("XB", [XBC_T, 2, LAT + S_CONV - 1], r_big)
        r_xc = r_big + 24960
        XC = view("XC", [10, T], r_xc)
        Cc = view("Cc", [S_GROUPS, LAT], r_xc + 10 * T * 4)
        XS = view("XS", [TT, S_INNER], r_h)
        XDT = view("XDT", [LT, 2, S_INNER], r_h + 16384)
        state = view("state", [8, 512], r_big)
        XW = view("XW", [2, S_INNER], r_big + 16384)
        seg = view("seg", [4, 512], r_big + 16384)
        Btok = view("Btok", [TT, S_GROUPS * S_STATE], r_big + 25088)
        rx = view("rx", [2, 512], r_big + 25088)
        ytmp = view("ytmp", [512], r_big + 29184)
        Ys = view("Ys", [LT, S_INNER], r_big + 32768)
        EX = view("EX", [12, 16], region(768))
        PL = view("PL", [4, 16], region(256))
        DW = view("DW", [6, 16], region(384))
        CB = X[:, :, LAT:LAT + P]
        sqQ = [X[:, 2 * i:2 * i + 2, LAT:T] for i in range(2)]
        sqK = X[:, 4:6, LAT:T]
        kroot = X[:, 6:8, LAT:T]
        qrowC = X[0:16, 4, LAT:T]
        ptapC = dts[:, 1:5, :].rearrange("p n c -> p (n c)").rearrange("p (s t) -> p s t", s=2)
        ropeC = modc[:, :].rearrange("p (s t) -> p s t", s=2)
        probC = view("probC", [3, T], r_h + 16384)
        probTC = view("probTC", [2, T], r_h + 22528)
        f_gate = view("f_gate", [2, T], r_misc)
        f_h = view("f_h", [2, T], r_misc + 4096)
        otile = view("otile", [LT, D], r_h)

        def cst(name, lo=0, hi=None, p0=0, p1=P):
            s, n = CONST_COLS[name]
            return const[p0:p1, s + lo:s + (n if hi is None else hi)]

        acc = psum("acc", [P, 4, 512])
        pmod = psum("pmod", [P, 512])
        p5 = psum("p5", [P, 512])
        p6 = psum("p6", [P, 512])
        p7 = psum("p7", [P, 512])
        sbank = [acc[:, 0, :], acc[:, 1, :], p7[:, :]]
        po = [p5, p6]
        stbank = [acc[:, 0, :], acc[:, 1, :], acc[:, 2, :], acc[:, 3, :], p5[:, :], p6[:, :], pmod[:, :], p7[:, :]]

        S = {}

        def s(name):
            if name not in S:
                S[name] = sem(name)
            return S[name]

        raw_loaded = [s(f"raw_loaded{i}") for i in range(RAW_SLOTS)]
        hi_split, lo_split, block_done = s("hi_split"), s("lo_split"), s("block_done")
        mod_used, read_act, read_dve = s("mod_used"), s("read_act"), s("read_dve")

        def tiles(w):
            return w.rearrange("(k p) n -> p k n", p=P)

        ev_in, ev_out = tiles(a["ev_w_in"][0]), tiles(a["ev_w_out"][0])
        od_in, od_out = tiles(a["od_w_in"][0]), tiles(a["od_w_out"][0])
        ffn_in = [tiles(a["ffn_w_in"][l]) for l in range(DEPTH)]
        ffn_out = [tiles(a["ffn_w_out"][l]) for l in range(DEPTH)]
        GLU_A, GLU_G = A_HEADS * A_HD + 2 * A_KV * A_HD, A_HEADS * A_HD + 2 * A_KV * A_HD + B_WIDTH
        blocksA = ([("g", ev_in, GLU_G + BC * i) for i in range(2)] + [("a", ev_in, GLU_A + BC * i) for i in range(2)]
                   + [("k", ev_in, A_HEADS * A_HD), ("v", ev_in, A_HEADS * A_HD + A_KV * A_HD)]
                   + [("q", ev_in, BC * i) for i in range(4)])
        C_Q = C_HEADS * C_HD
        C_X = C_Q + 4 * C_HD
        C_DT = C_X + XBC_T * P
        blocksC = ([("x", od_in, C_X + BC * i) for i in range(6)] + [("dt", od_in, C_DT), ("kv", od_in, C_Q)]
                   + [("q", od_in, BC * i) for i in range(4)] + [("z", od_in, C_DT + 32 + BC * i) for i in range(4)])
        stream = [("mod", 0, 0, k) for k in range(KD)]
        for n, (_, src, col) in enumerate(blocksA):
            stream.append(("w", src, 0, KD, col, BC))
            if 1 <= n <= 8:
                stream.append(("mod", 0, 1, n - 1))
        ev_out_blocks = [("w", ev_out, 6 * (n % 2), 6, BC * (n // 2), BC) for n in range(8)]
        stream.append(ev_out_blocks[0])
        for l, j in ((0, 2), (1, 0), (1, 1), (1, 2)):
            stream += [("mod", l, j, k) for k in range(KD)]
        stream += ev_out_blocks[1:]
        FF = []
        NW = lambda: sum(i[0] == "w" for i in stream)

        def add_ffn(l):
            FF.append((len(stream), NW()))
            for half, nt in enumerate(HALF):
                t0 = sum(HALF[:half])
                for p_ in range(nt // 2):
                    for side in range(2):
                        stream.append(("w", ffn_in[l], 0, KD, side * FFN + P * t0 + BC * p_, BC))
                for m in range(4):
                    for part in range(2):
                        stream.append(("w", ffn_out[l], t0 + part * nt // 2, nt // 2, BC * m, BC))

        add_ffn(0)
        C_IN = NW()
        stream += [("w", src, 0, KD, col, 32 if kind == "dt" else BC) for kind, src, col in blocksC]
        C_OUT = NW()
        stream += [("w", od_out, 8 * (n % 2), 8, BC * (n // 2), BC) for n in range(8)]
        add_ffn(1)
        A_OUT = len(blocksA)
        w_raw = [r for r, i in enumerate(stream) if i[0] == "w"]
        m_raw = [r for r, i in enumerate(stream) if i[0] == "mod"]
        w_index = {r: n for n, r in enumerate(w_raw)}
        m_index = {r: n for n, r in enumerate(m_raw)}

        def raw_block(r, kt, cols=BC):
            return raw[:, r % RAW_SLOTS, 0:kt * cols].rearrange("p (k n) -> p k n", k=kt)

        def split_block(w, kt, cols=BC):
            return [x[:, w % 2, 0:kt * cols].rearrange("p (k n) -> p k n", k=kt) for x in (w_hi, w_lo)]

        block = ctx.enter_context(nc.Block())

        @block.sync
        def _(sp):
            for t in range(TT):
                src = (a["x"] if t < LT else a["ctx"])[0]
                if t % LT == 0:
                    sp.dma_start(xin[:, t:t + LT, :], src.rearrange("(t p) d -> p t d", p=P)).then_inc(s("x_loaded"), 16)

            def free(r):
                if r < RAW_SLOTS:
                    return
                last = r - RAW_SLOTS
                if last in m_index:
                    sp.wait_ge(mod_used, m_index[last] + 1)
                else:
                    sp.wait_ge(lo_split, w_index[last] + 1)

            def load(r):
                item = stream[r]
                free(r)
                if item[0] == "mod":
                    _, l, j, k = item
                    sp.dma_start(raw[:, r % RAW_SLOTS, :],
                                 a["mod_w"][l, k * P:(k + 1) * P, j * MOD_COLS:(j + 1) * MOD_COLS])\
                        .then_inc(raw_loaded[r % RAW_SLOTS], 16)
                else:
                    _, src, k0, kt, col, cols = item
                    sp.dma_start(raw_block(r, kt, cols), src[:, k0:k0 + kt, col:col + cols])\
                        .then_inc(raw_loaded[r % RAW_SLOTS], 16)

            def load_loop(r, w, times, where):
                with sp.Fori(0, times) as it:
                    for q in range(4):
                        sp.wait_ge(lo_split, at(w + q - RAW_SLOTS + 1, it, 4))
                        src, kt = where(q, it)
                        sp.dma_start(raw_block(r + q, kt), src).then_inc(raw_loaded[(r + q) % RAW_SLOTS], 16)

            def load_ffn(l):
                r, w = FF[l]
                for half, nt in enumerate(HALF):
                    t0 = sum(HALF[:half])
                    n_in = nt // 4
                    load_loop(r, w, n_in, lambda q, it: (
                        ffn_in[l][:, :, bass.ds(it * (2 * BC) + ((q % 2) * FFN + P * t0 + BC * (q // 2)), BC)], KD))
                    r, w = r + 4 * n_in, w + 4 * n_in
                    for _ in range(nt % 4):
                        load(r)
                        r, w = r + 1, w + 1
                    load_loop(r, w, 2, lambda q, it: (
                        ffn_out[l][:, t0 + (q % 2) * nt // 2:t0 + (q % 2 + 1) * nt // 2,
                                   bass.ds(it * (2 * BC) + BC * (q // 2), BC)], nt // 2))
                    r, w = r + 8, w + 8
                return r

            for r in range(FF[0][0]):
                load(r)
            r = load_ffn(0)
            while r < FF[1][0]:
                load(r)
                r += 1
            load_ffn(1)
            for c in range(LT):
                sp.wait_ge(s("out_act"), c + 1)
                sp.wait_ge(s("out_dve"), c + 1)
                sp.dma_start(out[0, c * P:(c + 1) * P, :], otile[:, c, :]).then_inc(s("out_stored"), 16)
            sp.wait_ge(s("out_stored"), 16 * LT)

        def splitters(eng, kind):
            def split(w, it=None, first_only=False):
                r = w_raw[w]
                kt, cols = (8, BC) if it is not None else (stream[r][3], stream[r][5])
                n = kt * cols
                if kind == "hi":
                    eng.wait_ge(raw_loaded[r % RAW_SLOTS], at(16 * (r // RAW_SLOTS + 1), it, 16))
                    if w >= 2:
                        eng.wait_ge(block_done, at(w - 1, it, 4))
                    nc.scalar.activation(w_hi[:, w % 2, 0:n], raw[:, r % RAW_SLOTS, 0:n], ACT.Copy).then_inc(hi_split, 1)
                else:
                    eng.wait_ge(hi_split, at(w + 1, it, 4))
                    nc.vector.tensor_tensor(w_lo[:, w % 2, 0:n], raw[:, r % RAW_SLOTS, 0:n],
                                            w_hi[:, w % 2, 0:n].bitcast(F32), ALU.subtract).then_inc(lo_split, 1)
            return split

        def conv_C(i):
            if i < 10:
                return (XC[:, i, :].rearrange("p (s t) -> p s t", s=2), lambda tap: XB[:, i, :, tap:tap + LAT])
            return Cc[:, i - 10, :], lambda tap: XB[:, i, 0, tap:tap + LAT]

        def cvw(tap, i):
            return vec[:, CVW + XBC_T * tap + i:CVW + XBC_T * tap + i + 1]


        reads = {"act": 0, "dve": 0}
        A_READS, C_READS = [], []
        for kind, _, _ in blocksA:
            who = {"g": "act", "a": "dve", "k": "act", "v": "dve", "q": "act"}[kind]
            reads[who] += 1
            A_READS.append((who, reads[who]))
        after_A_in = dict(reads)
        reads["dve"] += 4
        FFN_READS = []

        def ffn_reads():
            res = []
            for nt in HALF:
                res.append(dict(reads))
                reads["act"] += nt // 2
                reads["dve"] += nt // 2
                res.append(dict(reads))
                reads["dve"] += 4
            FFN_READS.append(res)

        ffn_reads()
        for kind, _, _ in blocksC:
            who = {"x": "act", "dt": "dve", "kv": "act", "q": "act", "z": "act"}[kind]
            reads[who] += 1
            C_READS.append((who, reads[who]))
        after_C_in = dict(reads)
        reads["dve"] += 4
        ffn_reads()

        @block.gpsimd
        def _(pool):
            step = Chain(pool, s("pool_step"))
            nc.gpsimd.memset(U[:, :, :, :], 0.0).then_inc(s("pads_A"), 1)

            def norm_lo(n, t):
                for f in range(KD):
                    pool.wait_ge(s("h_hi"), KD * n + f + 1)
                    nc.gpsimd.tensor_tensor(Hlo[:, f, 0:t], n_h[:, f % 2, 0:t], Hhi[:, f, 0:t].bitcast(F32),
                                            ALU.subtract).then_inc(s("h_lo"), 1)

            norm_lo(0, T)
            pool.wait_ge(read_dve, 2)
            pool.wait_ge(s("vec_ready"), 1)
            i = BT - 1
            y = Y[:, i, :].rearrange("p (s t) -> p s t", s=2)
            z = ptap[:, :].rearrange("p (s t) -> p s t", s=2)
            step(nc.gpsimd.tensor_scalar(y, U[:, i, :, 0:LAT], vec[:, DWW + i:DWW + i + 1],
                                         vec[:, DWB + i:DWB + i + 1], ALU.mult, ALU.add))
            for tap in range(1, B_CONV):
                col = DWW + tap * BT + i
                step(nc.gpsimd.tensor_scalar(z, U[:, i, :, tap:tap + LAT], vec[:, col:col + 1], 0.0, ALU.mult, ALU.add))
                step(nc.gpsimd.tensor_tensor(y, y, z, ALU.add))
            nc.gpsimd.memset(ptap[:, 0:1], 0.0).then_inc(s("conv_pool"), 1)
            norm_lo(1, T)
            norm_lo(2, T)
            pool.wait_ge(s("h_lo"), 3 * KD)
            nc.gpsimd.memset(XB[:, :, :, 0:2], 0.0).then_inc(s("pads_C"), 1)
            nc.gpsimd.memset(XB[:, :, :, 2 + LAT:4 + LAT], 0.0).then_inc(s("pads_C"), 1)
            pool.wait_ge(s("pads_C"), 2)
            for i in range(8, XBC_T):
                pool.wait_ge(read_act, C_READS[i // 2][1])
                o, src = conv_C(i)
                z = ptapC[:, 0:2, :] if i < 10 else ptapC[:, 0, :]
                step(nc.gpsimd.tensor_scalar(o, src(0), cvw(0, i), vec[:, CVB + i:CVB + i + 1], ALU.mult, ALU.add))
                for tap in range(1, S_CONV):
                    step(nc.gpsimd.tensor_scalar(z, src(tap), cvw(tap, i), 0.0, ALU.mult, ALU.add))
                    ins = nc.gpsimd.tensor_tensor(o, o, z, ALU.add)
                    if tap < S_CONV - 1:
                        step(ins)
                ins.then_inc(s("conv_C_pool"), 1)
                pool.wait_ge(s("conv_C_pool"), i - 7)
            pool.wait_ge(s("xw_used"), 6)
            for k, (c, g, d, hg) in enumerate(SEG):
                if k >= 2:
                    pool.wait_ge(s("R_mm"), k - 1)
                at_ = 32 * c + 16 * d + 8 * g + 4 * hg
                nc.gpsimd.tensor_tensor(rx[:, k % 2, :].rearrange("p (h i) -> p h i", h=4),
                                        cst(("upto", "from")[d]).unsqueeze(1).to_broadcast([P, 4, P]),
                                        dts[:, 7, at_:at_ + 4].unsqueeze(2).to_broadcast([P, 4, P]), ALU.mult)\
                    .then_inc(s("rx_ready"), 1)
            norm_lo(3, LAT)

        @block.scalar
        def _(act):
            step = Chain(act, s("act_step"))
            split = splitters(act, "hi")
            A = nc.scalar.activation

            act.dma_start(const[:, :], a["const"]).then_inc(s("const_loaded"), 16)
            small = []

            def row(slot, r0, n, src):
                small.append(act.dma_start(vrow[r0:r0 + n, slot, :], src).then_inc(s("small_loaded"), 16))

            row(0, MODB, 96, a["mod_b"].rearrange("l (f p) -> (l f) p", p=P))
            row(0, N1G, 16, a["norm1_g"].rearrange("l (f p) -> (l f) p", p=P))
            row(0, N2G, 16, a["norm2_g"].rearrange("l (f p) -> (l f) p", p=P))
            fold = lambda x: x.rearrange("l (f p) -> (l f) p", p=P)
            row(1, DWB - 128, 4, fold(a["ev_dw_b"]))
            row(1, CNG - 128, 4, fold(a["ev_cn_g"]))
            row(1, CNB - 128, 4, fold(a["ev_cn_b"]))
            row(1, CVB - 128, 12, fold(a["od_conv_b"]))
            row(1, GNG - 128, 8, fold(a["od_gnorm_g"]))
            row(1, CVEC - 128, 8, fold(a["c"]))
            row(1, CVEC - 128 + 8, 8, a["c_ctx"].rearrange("(f p) -> f p", p=P))
            row(1, AQG - 128, 1, a["ev_q_g"])
            row(1, AKG - 128, 1, a["ev_k_g"])
            for r0, name in ((CQG, "od_q_g"), (CKG, "od_k_g")):
                for half in range(2):
                    act.dma_start(vrow[r0 - 128:r0 - 127, 1, half * C_HD:(half + 1) * C_HD], a[name])\
                        .then_inc(s("small_loaded"), 16)
                    small.append(0)
            row(1, CVW - 128, 60, a["od_conv_w"][0].rearrange("t (f p) -> (t f) p", p=P))
            row(2, 0, 124, a["ev_dw_w"][0].rearrange("t (f p) -> (t f) p", p=P))
            for lo, n, src in ((0, 32, a["od_dt_bias"]), (32, 32, a["od_A_log"])):
                act.dma_start(rows[:, lo:lo + n], src.rearrange("l d h -> l (d h)").partition_broadcast(P)[:, 0, :])\
                    .then_inc(s("rows_loaded"), 16)
            for lo, n, src in ((64, 16, a["od_D"]), (80, 16, a["od_sink"])):
                act.dma_start(rows[:, lo:lo + n], src.partition_broadcast(P)[:, 0, :]).then_inc(s("rows_loaded"), 16)

            for f in range(1, KD, 2):
                act.wait_ge(s("xT_done"), f + 1)
                A(X[:, f, :], acc[:, f % 4, :], ACT.Copy).then_inc(s("xT_act"), 1)
            act.wait_ge(s("vec_ready"), 1)
            act.wait_ge(s("cvec_zero"), 1)
            A(cvec[:, :, 0:2], vec[:, CVEC:CVEC + 16].rearrange("p (v k) -> p k v", v=2), ACT.Silu)\
                .then_inc(s("cvec_ready"), 1)

            def norm(n, t, updates=0):
                if n:
                    act.wait_ge(read_dve, updates)
                for f in range(KD):
                    if n == 0:
                        act.wait_ge(s("xT_dve"), f // 2 + 1)
                        act.wait_ge(s("xT_act"), (f + 1) // 2) if f else None
                    if f >= 2:
                        act.wait_ge(s("ss_mm"), KD * n + f - 1)
                    A(n_sq[:, f % 2, 0:t], X[:, f, 0:t], ACT.Square).then_inc(s("sq_ready"), 1)
                act.wait_ge(s("ss_mm"), KD * (n + 1))
                A(n_rt[:, 0:t], p5[:, 0:t], ACT.Sqrt, scale=1.0 / D, bias=epsc[:, 0:1]).then_inc(s("rt_ready"), 1)
                for f in range(KD):
                    act.wait_ge(s("h_ready"), KD * n + f + 1)
                    A(Hhi[:, f, 0:t], n_h[:, f % 2, 0:t], ACT.Copy).then_inc(s("h_hi"), 1)

            norm(0, T)

            split(0)
            nk = 0
            for n, (kind, _, _) in enumerate(blocksA):
                split(n + 1)
                lo = 2 * (n % 2)
                if kind in ("g", "k", "q"):
                    act.wait_ge(block_done, n + 1)
                if kind == "g":
                    A(sgate[:, 2 * n:2 * n + 2, :], acc[:, lo:lo + 2, :], ACT.Sigmoid).then_inc(read_act, 1)
                if kind in ("k", "q"):
                    if nk >= 2:
                        act.wait_ge(s("aux_done"), nk - 1)
                    if nk == 0:
                        act.wait_ge(s("h_lo"), KD)
                    step(A(sqA[:, nk % 2, :, :], acc[:, lo:lo + 2, :], ACT.Square))
                    g0 = AKG if kind == "k" else AQG
                    A(QK[:, 2 * nk:2 * nk + 2, :], acc[:, lo:lo + 2, :], ACT.Copy,
                      scale=vec[:, g0:g0 + 1]).then_inc(read_act, 1)
                    nk += 1
                if nk == 2 and kind == "q":
                    act.wait_ge(s("aux_done"), 1)
                    for h in range(A_KV):
                        A(krt[:, h, :], (p5, p7)[h][:, :], ACT.Sqrt, scale=1.0 / A_HD, bias=epsc[:, 0:1])\
                            .then_inc(s("krt_ready"), 1)
            act.wait_ge(s("qrow_T"), 1)
            A(qsc[:, :, :], p6[:, 0:64].rearrange("p (t h) -> p t h", t=TT), ACT.Sqrt, scale=1.0 / A_HD,
              bias=epsc[:, 0:1]).then_inc(s("qsc_root"), 1)

            def attention(layer, units, O_hi, tile_units, pr, prT, nk_of, qcol, sink=None):
                n0 = layer * 32

                def out_hi(tile):
                    act.wait_ge(s("pv_done"), n0 + tile_units * (tile + 1))
                    w = tile_units * P if layer == 0 else LAT
                    A(O_hi[:, tile, 0:w], po[tile % 2][:, 0:w], ACT.Copy).then_inc(s("o_hi"), 1)

                def exp(u):
                    n = n0 + u
                    act.wait_ge(s("nb_ready"), n + 1)
                    if u >= 3:
                        act.wait_ge(s("pT_done"), n - 2)
                    c0, nkt = nk_of(u)
                    A(pr[:, u % 3, c0 * P:T], sbank[u % 3][:, c0 * P:T], ACT.Exp, scale=qcol(u),
                      bias=sm[:, u % 3, 1:2], accum_out=sm[:, u % 3, 2:3]).then_inc(s("exp_done"), 1)
                    if sink is not None:
                        A(sm[:, u % 3, 3:4], sink(u), ACT.Exp, bias=sm[:, u % 3, 1:2]).then_inc(s("sink_done"), 1)

                exp(0)
                for u in range(units):
                    if u + 1 < units:
                        exp(u + 1)
                    copy_T(u, n0 + u, nk_of, prT)
                    if u % tile_units == 1 and u > tile_units:
                        out_hi(u // tile_units - 1)
                out_hi(units // tile_units - 1)

            def copy_T(u, n, nk_of, prT):
                act.wait_ge(s("pT_done"), n + 1)
                if u >= 2:
                    act.wait_ge(s("pv_done"), n - 1)
                w = nk_of(u)[1] * P
                A(prT[:, u % 2, 0:w], acc[:, 2 + u % 2, 0:w], ACT.Copy).then_inc(s("pT_copied"), 1)

            attention(0, 32, hid_hi, 4, prob, probT, lambda u: (0, 4) if u % 4 < 2 else (2, 2),
                      lambda u: qsc[:, u % 4, u // 4:u // 4 + 1])

            for i in range(BT):
                act.wait_ge(s("yc_ready"), i + 1)
                if i >= 2:
                    act.wait_ge(s("var_mm"), i - 1)
                A(yq[:, i % 2, :], yc[:, i, :], ACT.Square).then_inc(s("yq_ready"), 1)
            act.wait_ge(s("var_mm"), BT)
            A(l_rt[:, :], pmod[:, :], ACT.Sqrt, scale=1.0 / B_WIDTH, bias=epsc[:, 0:1]).then_inc(s("lrt_ready"), 1)
            for i in range(BT):
                act.wait_ge(s("yn_ready"), i + 1)
                if i >= 2:
                    act.wait_ge(s("mixA_lo"), i - 1)
                step(A(yz[:, i % 2, :], yc[:, i, :], ACT.Silu, scale=vec[:, CNG + i:CNG + i + 1],
                       bias=vec[:, CNB + i:CNB + i + 1]))
                A(hid_hi[:, 8 + i, :], yz[:, i % 2, :], ACT.Copy).then_inc(s("mixA_hi"), 1)

            for n in range(8):
                split(A_OUT + n + 1)
            norm(1, T, after_A_in['dve'] + 4)

            def ffn(l, t):
                w = FF[l][1]
                npair = 0
                for half, nt in enumerate(HALF):
                    def gate(w, q, it, pair, per):
                        split(w + q + 1, it)
                        act.wait_ge(block_done, at(w + q + 1, it, 4))
                        act.wait_ge(read_dve, at(FFN_READS[l][2 * half]["dve"] + pair, it, per))
                        A(f_gate[:, :, 0:t], acc[:, 0:2, 0:t], ACT.Silu).then_inc(read_act, 1)

                    def up(w, q, it, pair, per, hcol):
                        split(w + q + 1, it)
                        act.wait_ge(read_dve, at(FFN_READS[l][2 * half]["dve"] + pair + 1, it, per))
                        A(hcol, f_h[:, :, 0:t], ACT.Copy).then_inc(s("hid_hi_done"), 1)

                    n_in = nt // 4
                    with act.Fori(0, n_in) as it:
                        for p_ in range(2):
                            gate(w, 2 * p_, it, p_, 2)
                            up(w, 2 * p_ + 1, it, p_, 2, hid_hi[:, bass.ds(it * 4 + 2 * p_, 2), 0:t])
                    w += 4 * n_in
                    if nt % 4:
                        p_ = nt // 2 - 1
                        gate(w, 0, None, p_, 0)
                        up(w, 1, None, p_, 0, hid_hi[:, 2 * p_:2 * p_ + 2, 0:t])
                        w += 2
                    times = 2
                    if l == 1 and half == 1:
                        times = 1
                    with act.Fori(0, times) as it:
                        for q in range(4):
                            split(w + q + 1, it)
                    if times == 1:
                        for q in range(4, 7):
                            split(w + q + 1)
                    w += 8

            ffn(0, T)

            norm(2, T, FFN_READS[0][3]["dve"] + 4)
            w = C_IN
            nq = 0
            for n, (kind, _, _) in enumerate(blocksC):
                split(w + n + 1)
                lo = 2 * (n % 2)
                if kind != "dt":
                    act.wait_ge(block_done, w + n + 1)
                if kind == "x":
                    if n == 0:
                        act.wait_ge(s("pads_C"), 2)
                    if n < 5:
                        for i in range(2):
                            ins = A(XB[:, 2 * n + i, :, 2:2 + LAT], acc[:, lo + i, :].rearrange("p (s t) -> p s t", s=2),
                                    ACT.Copy)
                            if i:
                                ins.then_inc(read_act, 1)
                            else:
                                step(ins)
                    else:
                        A(XB[:, 10:12, 0, 2:2 + LAT], acc[:, lo:lo + 2, 0:LAT], ACT.Copy).then_inc(read_act, 1)
                elif kind == "kv":
                    step(A(sqK, acc[:, lo, :].rearrange("p (s t) -> p s t", s=2), ACT.Square))
                    step(A(Kc[:, :], acc[:, lo, :], ACT.Copy, scale=vec[:, CKG:CKG + 1]))
                    A(Vc[:, :, :], acc[:, lo + 1, :].rearrange("p (t n) -> p t n", t=TT), ACT.Copy).then_inc(read_act, 1)
                elif kind == "q":
                    if nq >= 2:
                        act.wait_ge(s("aux_done"), 5 + nq)
                    step(A(sqQ[nq % 2], acc[:, lo:lo + 2, 0:LAT], ACT.Square))
                    A(Q[:, 2 * nq:2 * nq + 2, :], acc[:, lo:lo + 2, 0:LAT], ACT.Copy, scale=vec[:, CQG:CQG + 1])\
                        .then_inc(read_act, 1)
                    if nq == 0:
                        act.wait_ge(s("aux_done"), 6)
                        A(kroot, p5[:, :].rearrange("p (s t) -> p s t", s=2), ACT.Sqrt, scale=1.0 / C_HD, bias=epsc[:, 0:1])\
                            .then_inc(s("krt_ready"), 1)
                    nq += 1
                elif kind == "z":
                    c0 = BC * (n - 12)
                    A(Z[:, :, c0:c0 + BC], acc[:, lo:lo + 2, 0:BC], ACT.Silu).then_inc(read_act, 1)
            act.wait_ge(s("qrow_T"), 2)
            A(qsc[:, 0:LT, :], p6[:, 0:32].rearrange("p (t h) -> p t h", t=LT), ACT.Sqrt, scale=1.0 / C_HD,
              bias=epsc[:, 0:1]).then_inc(s("qsc_root"), 1)
            for i in range(XBC_T):
                act.wait_ge(s("conv_C_dve") if i < 8 else s("conv_C_pool"), i + 1 if i < 8 else i - 7)
                o = XC[:, i, :] if i < 10 else Cc[:, i - 10, :]
                A(o, o, ACT.Silu).then_inc(s("xc_ready"), 1)
            act.wait_ge(read_dve, C_READS[6][1])
            step(A(dts[:, 1, :], dts[:, 0, :], ACT.Abs))
            step(A(dts[:, 1, :], dts[:, 1, :], ACT.Exp, scale=-1.0))
            act.wait_ge(s("rows_loaded"), 64)
            A(dts[:, 2, 0:32], ALOG, ACT.Exp).then_inc(s("spexp_ready"), 1)
            act.wait_ge(s("cum_mm"), 1)
            step(A(PL[:, :, :], p7[:, 64:128].rearrange("p (n h) -> p n h", n=4), ACT.Copy))
            A(EX[:, :, :], p7[:, 0:192].rearrange("p (n h) -> p n h", n=12), ACT.Exp).then_inc(s("ex_ready"), 1)
            for k in range(1, 8, 2):
                act.wait_ge(s("xsT_done"), k + 1)
                A(XS[:, k // 2, (k % 2) * 512:(k % 2) * 512 + 512], acc[:, k % 4, :], ACT.Copy).then_inc(s("xs_act"), 1)
            for k in range(4):
                act.wait_ge(s("xw_used"), (2, 3, 5, 6)[k])
                A(state[:, 2 * k + 1, :], stbank[2 * k + 1], ACT.Copy).then_inc(s("state_act"), 1)
            for k in range(16):
                act.wait_ge(s("seg_ready"), k + 1)
                A(seg[:, k % 4, :], seg[:, k % 4, :], ACT.Exp).then_inc(s("decay_ready"), 1)
            act.wait_ge(s("yg_ready"), 1)
            for c in range(LT):
                ins = A(XDT[:, c, 0, :], Ys[:, c, :], ACT.Square, accum_out=ysum[:, c:c + 1])
                step(ins)
            A(ysum[:, 2:4], ysum[:, 0:2], ACT.Sqrt, scale=1.0 / S_INNER, bias=epsc[:, 0:1]).then_inc(s("yrt_ready"), 1)
            for k in range(4):
                act.wait_ge(s("yT_done"), k + 1)
                for i in range(2):
                    f = 2 * k + i
                    ins = A(mixC_hi[:, 8 + f, :], acc[:, k % 4, i * LAT:(i + 1) * LAT], ACT.Copy,
                            scale=vec[:, GNG + f:GNG + f + 1])
                    ins.then_inc(s("mixC_hi_done"), 1)
            attention(1, 32, mixC_hi, 4, probC, probTC, lambda u: (0, 4),
                      lambda u: qsc[:, (u // 2) % 2, 2 * (u // 4) + u % 2:2 * (u // 4) + u % 2 + 1],
                      lambda u: SINK[:, 2 * (u // 4) + u % 2:2 * (u // 4) + u % 2 + 1])
            for n in range(8):
                split(C_OUT + n + 1)
            norm(3, LAT, after_C_in["dve"] + 4)
            ffn(1, LAT)
            for k in range(1, 4, 2):
                act.wait_ge(s("oT_done"), k + 1)
                A(otile[:, k // 2, 512:1024], acc[:, k % 4, :], ACT.Copy).then_inc(s("out_act"), 1)

        @block.vector
        def _(dve):
            step = Chain(dve, s("dve_step"))
            split = splitters(dve, "lo")
            V_ = nc.vector

            V_.memset(epsc[:, :], EPS).then_inc(s("cvec_zero"), 1)
            V_.memset(cvec[:, :, :], 0.0).then_inc(s("cvec_zero"), 1)
            dve.wait_ge(s("vec_T"), 1)
            V_.tensor_copy(vec[:, :], p7[:, 0:VEC_N]).then_inc(s("vec_ready"), 1)
            for f in range(0, KD, 2):
                dve.wait_ge(s("xT_done"), f + 1)
                V_.tensor_copy(X[:, f, :], acc[:, f % 4, :]).then_inc(s("xT_dve"), 1)

            GROUPS = [(l, j) for l in range(DEPTH) for j in range(3)]

            def mod_copy(n):
                dve.wait_ge(mod_used, KD * (n + 1))
                V_.tensor_copy(modc[:, :], pmod[:, :]).then_inc(s("modc_ready"), 1)

            def mod_final(n):
                l, j = GROUPS[n]
                dve.wait_ge(s("modT_done"), n + 1)
                for v in range(2):
                    src = pmod[:, :].rearrange("p (b g c) -> p g b c", b=4, g=4)[:, :, :, v]
                    b0 = MODB + 48 * l + 16 * j
                    step(V_.tensor_tensor(mod[:, l, 16 * j:16 * j + 16, v].rearrange("p (g b) -> p g b", g=4), src,
                                          vec[:, b0:b0 + 16].rearrange("p (g b) -> p g b", g=4), ALU.add))
                norm_of = {0: (2 * l, SC1, N1G), 2: (2 * l + 1, SC2, N2G)}.get(j)
                if norm_of:
                    k, sc, g0 = norm_of
                    for v in range(2):
                        step(V_.scalar_tensor_tensor(out=gain[:, k, :, v], in0=mod[:, l, sc:sc + KD, v], scalar=1.0,
                                                     in1=vec[:, g0 + KD * l:g0 + KD * (l + 1)], op0=ALU.add,
                                                     op1=ALU.mult))
                V_.memset(ysum[:, 0:1], 0.0).then_inc(s("mod_ready"), 1)

            mod_copy(0)
            mod_final(0)

            def norm(n, t):
                l, k = n // 2, n
                sh = (SH1, SH2)[n % 2]
                dve.wait_ge(s("rt_ready"), n + 1)
                step(V_.reciprocal(n_rs[:, 0:t], n_rt[:, 0:t]))
                for f in range(KD):
                    if f:
                        dve.wait_ge(s("h_ready"), KD * n + f)
                    step(V_.tensor_tensor(n_t[:, 0:t], X[:, f, 0:t], n_rs[:, 0:t], ALU.mult))
                    if f >= 2:
                        dve.wait_ge(s("h_lo"), KD * n + f - 1)
                    for v in range(t // LAT):
                        ins = V_.tensor_scalar(n_h[:, f % 2, v * LAT:(v + 1) * LAT], n_t[:, v * LAT:(v + 1) * LAT],
                                               gain[:, k, f, v:v + 1], mod[:, l, sh + f, v:v + 1], ALU.mult, ALU.add)
                    ins.then_inc(s("h_ready"), 1)

            norm(0, T)

            def rope(out2, rot, tmp, cos, sin, n):
                step(V_.tensor_tensor(tmp, rot, sin, ALU.mult))
                step(V_.tensor_tensor(out2, out2, cos, ALU.mult))
                V_.tensor_tensor(out2, out2, tmp, ALU.add).then_inc(s("rope_done"), 1)

            def both(x):
                return x.unsqueeze(1).to_broadcast([P, 2, LAT])

            taps = [(tap, i) for tap in range(B_CONV) for i in range(BT - 1)]

            def conv_taps(count):
                for _ in range(min(count, len(taps))):
                    tap, i = taps.pop(0)
                    y = Y[:, i, :].rearrange("p (s t) -> p s t", s=2)
                    col = vec[:, DWW + tap * BT + i:DWW + tap * BT + i + 1]
                    if tap == 0:
                        ins = V_.tensor_scalar(y, U[:, i, :, 0:LAT], col, vec[:, DWB + i:DWB + i + 1], ALU.mult,
                                               ALU.add)
                    else:
                        dve.wait_ge(s("conv_dve"), (BT - 1) * (tap - 1) + i + 1)
                        ins = V_.scalar_tensor_tensor(out=y, in0=U[:, i, :, tap:tap + LAT], scalar=col, in1=y,
                                                      op0=ALU.mult, op1=ALU.add)
                    ins.then_inc(s("conv_dve"), 1)

            split(0)
            dve.wait_ge(s("pads_A"), 1)
            nk = 0
            for n, (kind, _, _) in enumerate(blocksA):
                split(n + 1)
                lo = 2 * (n % 2)
                if kind == "a":
                    i0 = 2 * (n - 2)
                    dve.wait_ge(block_done, n + 1)
                    dve.wait_ge(read_act, A_READS[n - 2][1])
                    for i in range(2):
                        ins = V_.tensor_tensor(U[:, i0 + i, :, B_CONV // 2:B_CONV // 2 + LAT],
                                               acc[:, lo + i, :].rearrange("p (s t) -> p s t", s=2),
                                               sgate[:, i0 + i, :].rearrange("p (s t) -> p s t", s=2), ALU.mult)
                    ins.then_inc(read_dve, 1)
                if kind == "v":
                    dve.wait_ge(block_done, n + 1)
                    V_.tensor_copy(V[:, :, :].rearrange("p (b t) n -> p b (t n)", b=2), acc[:, lo:lo + 2, :])\
                        .then_inc(read_dve, 1)
                if n == 4:
                    dve.wait_ge(read_dve, 2)
                if n >= 4:
                    conv_taps(8)
                if n >= 5 and n != 6:
                    dve.wait_ge(s("aux_done"), nk + 1)
                    rope(QK[:, 2 * nk:2 * nk + 2, 0:LAT], p6[:, :].rearrange("p (s t) -> p s t", s=2), ropeT[:, :, :],
                         both(cst("cosA")), both(cst("sinA")), nk)
                    nk += 1
                if n == 7:
                    for h in range(A_KV):
                        dve.wait_ge(s("krt_ready"), h + 1)
                        step(V_.reciprocal(krt[:, h, :], krt[:, h, :]))
                        V_.tensor_tensor(QK[:, h, :], QK[:, h, :], krt[:, h, :], ALU.mult).then_inc(s("k_scaled"), 1)
                        dve.wait_ge(s("k_scaled"), h + 1)
            mod_copy(1)
            dve.wait_ge(s("aux_done"), 5)
            rope(QK[:, 8:10, 0:LAT], p6[:, :].rearrange("p (s t) -> p s t", s=2), ropeT[:, :, :], both(cst("cosA")),
                 both(cst("sinA")), 4)
            V_.tensor_copy(qrow[0:16, :], p7[0:16, :]).then_inc(s("qrow_ready"), 1)
            dve.wait_ge(s("qsc_root"), 1)
            step(V_.reciprocal(qsc[:, :, :], qsc[:, :, :]))
            V_.tensor_scalar(qsc[:, :, :], qsc[:, :, :], A_HD ** -0.5, None, ALU.mult).then_inc(s("qsc_ready"), 1)
            dve.wait_ge(s("qsc_ready"), 1)
            mod_final(1)

            def attention(layer, O_hi, O_lo, pr, nk_of, qcol, sink=None):
                n0 = 32 * layer

                def row_max(u):
                    c0 = nk_of(u)[0]
                    dve.wait_ge(s("s_done"), n0 + u + 1)
                    step(V_.reduce_max(sm[:, u % 3, 0:1], sbank[u % 3][:, c0 * P:T], AX.X))
                    if sink is None:
                        V_.tensor_scalar(sm[:, u % 3, 1:2], sm[:, u % 3, 0:1], qcol(u), -1.0, ALU.mult, ALU.mult)\
                            .then_inc(s("nb_ready"), 1)
                    else:
                        step(V_.tensor_scalar(sm[:, u % 3, 5:6], sm[:, u % 3, 0:1], qcol(u), sink(u), ALU.mult,
                                              ALU.max))
                        V_.tensor_scalar(sm[:, u % 3, 1:2], sm[:, u % 3, 5:6], -1.0, None, ALU.mult)\
                            .then_inc(s("nb_ready"), 1)

                def normalise(u):
                    c0 = nk_of(u)[0]
                    dve.wait_ge(s("exp_done"), n0 + u + 1)
                    total = sm[:, u % 3, 2:3]
                    if sink is not None:
                        dve.wait_ge(s("sink_done"), u + 1)
                        step(V_.tensor_tensor(sm[:, u % 3, 6:7], total, sm[:, u % 3, 3:4], ALU.add))
                        total = sm[:, u % 3, 6:7]
                    step(V_.reciprocal(sm[:, u % 3, 4:5], total))
                    V_.tensor_scalar(pr[:, u % 3, c0 * P:T], pr[:, u % 3, c0 * P:T], sm[:, u % 3, 4:5], None, ALU.mult)\
                        .then_inc(s("p_norm"), 1)

                def out_lo(tile):
                    dve.wait_ge(s("o_hi"), 8 * layer + tile + 1)
                    w = T if layer == 0 else LAT
                    V_.tensor_tensor(O_lo[:, tile, 0:w], po[tile % 2][:, 0:w], O_hi[:, tile, 0:w].bitcast(F32),
                                     ALU.subtract).then_inc(s("o_lo"), 1)

                row_max(0)
                row_max(1)
                for u in range(32):
                    normalise(u)
                    if u + 2 < 32:
                        row_max(u + 2)
                    if layer == 0:
                        conv_taps(2)
                    if layer == 0 and u % 8 == 4:
                        mod_copy(2 + u // 8)
                    if layer == 0 and u % 8 == 6:
                        mod_final(2 + u // 8)
                    if u % 4 == 1 and u > 4:
                        out_lo(u // 4 - 1)
                out_lo(7)

            attention(0, hid_hi, hid_lo, prob, lambda u: (0, 4) if u % 4 < 2 else (2, 2),
                      lambda u: qsc[:, u % 4, u // 4:u // 4 + 1])

            dve.wait_ge(s("mu_mm"), 1)
            for i in range(BT):
                V_.scalar_tensor_tensor(out=yc[:, i, :], in0=p7[:, :], scalar=-1.0 / B_WIDTH, in1=Y[:, i, :],
                                        op0=ALU.mult, op1=ALU.add).then_inc(s("yc_ready"), 1)
            dve.wait_ge(s("lrt_ready"), 1)
            step(V_.reciprocal(l_rt[:, :], l_rt[:, :]))
            for i in range(BT):
                V_.tensor_tensor(yc[:, i, :], yc[:, i, :], l_rt[:, :], ALU.mult).then_inc(s("yn_ready"), 1)
            for i in range(BT):
                dve.wait_ge(s("mixA_hi"), i + 1)
                V_.tensor_tensor(hid_lo[:, 8 + i, :], yz[:, i % 2, :], hid_hi[:, 8 + i, :].bitcast(F32),
                                 ALU.subtract).then_inc(s("mixA_lo"), 1)

            def update(l, g0, pair, m, t, it=None):
                for i in range(2):
                    for v in range(t // LAT):
                        cols = slice(v * LAT, (v + 1) * LAT)
                        if it is None:
                            xs, gt = X[:, m + i, cols], mod[:, l, g0 + m + i, v:v + 1]
                        else:
                            xs = X[:, bass.ds(it * 4 + (m + i), 1), cols].rearrange("p a t -> p (a t)")
                            gt = mod[:, l, bass.ds(it * 4 + (g0 + m + i), 1), v:v + 1].rearrange("p a v -> p (a v)")
                        ins = V_.scalar_tensor_tensor(out=xs, in0=acc[:, 2 * pair + i, cols], scalar=gt, in1=xs,
                                                      op0=ALU.mult, op1=ALU.add)
                ins.then_inc(read_dve, 1)

            def out_projection(w, l, t):
                for n in range(8):
                    split(w + n + 1)
                    if n % 2:
                        dve.wait_ge(block_done, w + n + 1)
                        update(l, G1, (n // 2) % 2, 2 * (n // 2), t)

            out_projection(A_OUT, 0, T)
            norm(1, T)

            def ffn(l, t):
                w = FF[l][1]
                hid = sum(HALF) // 2 * l
                for half, nt in enumerate(HALF):
                    R = FFN_READS[l][2 * half]

                    def up(w, q, it, pair, per, hi, lo):
                        split(w + q + 1, it)
                        dve.wait_ge(block_done, at(w + q + 1, it, 4))
                        dve.wait_ge(read_act, at(R["act"] + pair + 1, it, per))
                        V_.tensor_tensor(f_h[:, :, 0:t], acc[:, 2:4, 0:t], f_gate[:, :, 0:t], ALU.mult)\
                            .then_inc(read_dve, 1)
                        dve.wait_ge(s("hid_hi_done"), at(hid + pair + 1, it, per))
                        V_.tensor_tensor(lo, f_h[:, :, 0:t], hi.bitcast(F32), ALU.subtract).then_inc(s("hid_lo_done"), 1)

                    n_in = nt // 4
                    with dve.Fori(0, n_in) as it:
                        for p_ in range(2):
                            split(w + 2 * p_ + 1, it)
                            cols = bass.ds(it * 4 + 2 * p_, 2)
                            up(w, 2 * p_ + 1, it, p_, 2, hid_hi[:, cols, 0:t], hid_lo[:, cols, 0:t])
                    w += 4 * n_in
                    if nt % 4:
                        p_ = nt // 2 - 1
                        split(w + 1)
                        up(w, 1, None, p_, 0, hid_hi[:, 2 * p_:2 * p_ + 2, 0:t], hid_lo[:, 2 * p_:2 * p_ + 2, 0:t])
                        w += 2
                    hid += nt // 2
                    last = l == DEPTH - 1 and half == 1
                    with dve.Fori(0, 1 if last else 2) as it:
                        for q in range(4):
                            split(w + q + 1, it)
                            if q % 2:
                                dve.wait_ge(block_done, at(w + q + 1, it, 4))
                                update(l, G2, q // 2, 2 * (q // 2), t, it)
                    if last:
                        for q in range(4, 8):
                            if q < 7:
                                split(w + q + 1)
                            if q % 2:
                                dve.wait_ge(block_done, w + q + 1)
                                update(l, G2, (q // 2) % 2, 2 * (q // 2), t)
                    w += 8

            ffn(0, T)

            norm(2, T)
            w = C_IN
            for n, (kind, _, _) in enumerate(blocksC):
                split(w + n + 1)
                if kind == "dt":
                    dve.wait_ge(block_done, w + n + 1)
                    dve.wait_ge(s("rows_loaded"), 64)
                    V_.tensor_tensor(dts[:, 0, :].rearrange("p (t h) -> p t h", t=TT),
                                     acc[:, 0, 0:TT * 32].rearrange("p (t h) -> p t h", t=TT),
                                     DTB.unsqueeze(1).to_broadcast([P, TT, 32]), ALU.add).then_inc(read_dve, 1)
                if n == 8:
                    dve.wait_ge(s("aux_done"), 6)
                    rope(Kc[:, 0:LAT], p6[:, 0:LAT], modc[:, 0:LAT], cst("cosC"), cst("sinC"), 5)
                    dve.wait_ge(s("krt_ready"), 3)
                    step(V_.reciprocal(kroot, kroot))
                    kv = Kc[:, :].rearrange("p (s t) -> p s t", s=2)
                    dve.wait_ge(s("rope_done"), 6)
                    step(V_.tensor_tensor(kv, kv, kroot, ALU.mult))
                    for g in range(2):
                        for e in range(2):
                            ins = V_.tensor_copy(K2[64 * e:64 * e + 64, g, :], Kc[64 * g:64 * g + 64, :])
                    ins.then_inc(s("k2_ready"), 1)
                if 1 <= n <= 4:
                    dve.wait_ge(read_act, C_READS[n - 1][1])
                    dve.wait_ge(s("pads_C"), 2)
                    for tap in range(S_CONV):
                        for i in (2 * n - 2, 2 * n - 1):
                            o, src = conv_C(i)
                            if tap == 0:
                                ins = V_.tensor_scalar(o, src(0), cvw(0, i), vec[:, CVB + i:CVB + i + 1], ALU.mult,
                                                       ALU.add)
                            else:
                                ins = V_.scalar_tensor_tensor(out=o, in0=src(tap), scalar=cvw(tap, i), in1=o,
                                                              op0=ALU.mult, op1=ALU.add)
                            if tap == S_CONV - 1:
                                ins.then_inc(s("conv_C_dve"), 1)
                            else:
                                step(ins)
                if 9 <= n <= 12:
                    nq = n - 9
                    dve.wait_ge(s("aux_done"), 7 + nq)
                    rope(Q[:, 2 * nq:2 * nq + 2, :], p6[:, :].rearrange("p (s t) -> p s t", s=2), ropeC, both(cst("cosC")),
                         both(cst("sinC")), 6 + nq)
            V_.tensor_copy(qrowC, p7[0:16, 0:LAT]).then_inc(s("qrow_ready"), 1)
            dve.wait_ge(s("qsc_root"), 2)
            step(V_.reciprocal(qsc[:, 0:LT, :], qsc[:, 0:LT, :]))
            V_.tensor_scalar(qsc[:, 0:LT, :], qsc[:, 0:LT, :], C_HD ** -0.5, None, ALU.mult).then_inc(s("qsc_ready"), 1)

            dve.wait_ge(s("spexp_ready"), 1)
            DTR, e, z2, q, tmp = dts[:, 0, :], dts[:, 1, :], dts[:, 4, :], dts[:, 5, :], dts[:, 3, :]
            step(V_.tensor_scalar(tmp, e, 2.0, None, ALU.add))
            step(V_.reciprocal(tmp, tmp))
            step(V_.tensor_tensor(e, e, tmp, ALU.mult))
            step(V_.tensor_tensor(z2, e, e, ALU.mult))
            step(V_.tensor_scalar(q, z2, 1.0 / 15, None, ALU.mult))
            for odd in (13, 11, 9, 7, 5, 3):
                step(V_.scalar_tensor_tensor(out=q, in0=q, scalar=1.0 / odd, in1=z2, op0=ALU.add, op1=ALU.mult))
            step(V_.scalar_tensor_tensor(out=q, in0=q, scalar=1.0, in1=e, op0=ALU.add, op1=ALU.mult))
            step(V_.tensor_scalar(tmp, DTR, 0.0, None, ALU.max))
            step(V_.scalar_tensor_tensor(out=dt_, in0=q, scalar=2.0, in1=tmp, op0=ALU.mult, op1=ALU.add))
            by_tile = lambda x: x.rearrange("p (t h) -> p t h", t=TT)
            V_.scalar_tensor_tensor(out=by_tile(da), in0=by_tile(dt_), scalar=-1.0,
                                    in1=dts[:, 2, 0:32].unsqueeze(1).to_broadcast([P, TT, 32]), op0=ALU.mult,
                                    op1=ALU.mult).then_inc(s("da_ready"), 1)
            dt_of = lambda t, d: dts[:, 6, 32 * t + 16 * d:32 * t + 16 * d + 16]
            for k in range(0, 8, 2):
                dve.wait_ge(s("xsT_done"), k + 1)
                V_.tensor_copy(XS[:, k // 2, (k % 2) * 512:(k % 2) * 512 + 512], acc[:, k % 4, :]).then_inc(s("xs_dve"), 1)
            for k in range(2):
                dve.wait_ge(s("bT_done"), k + 1)
                V_.tensor_copy(Btok[:, 2 * k:2 * k + 2, :], po[k][:, :].rearrange("p (t n) -> p t n", t=2))\
                    .then_inc(s("btok_ready"), 1)
            dve.wait_ge(s("cb_mm"), 1)
            pcb = pmod[:, :].rearrange("p (n i) -> p n i", n=4)
            for d, tri in ((0, "upto"), (1, "from")):
                V_.tensor_tensor(CB[:, 4 * d:4 * d + 4, :], pcb, cst(tri).unsqueeze(1).to_broadcast([P, 4, P]),
                                 ALU.mult).then_inc(s("cb_ready"), 1)
            per_head = lambda x: x.unsqueeze(2).to_broadcast([P, x.shape[1], S_HD])
            split_heads = lambda x: x.rearrange("p (h n) -> p h n", n=S_HD)
            dve.wait_ge(s("xs_dve"), 4)
            dve.wait_ge(s("xs_act"), 4)
            dve.wait_ge(s("ex_ready"), 1)
            SRC = ((2, 0, 0), (3, 0, 1), (0, 0, 10), (2, 1, 2), (3, 1, 3), (1, 1, 11))
            for n, (t, d, k) in enumerate(SRC):
                ins = V_.tensor_tensor(DW[:, n, :], dt_of(t, d), EX[:, k, :], ALU.mult)
            step(ins)
            for n, (t, d, k) in enumerate(SRC):
                if n >= 2:
                    dve.wait_ge(s("xw_used"), n - 1)
                V_.tensor_tensor(split_heads(XW[:, n % 2, :]), split_heads(XS[:, t, :]), per_head(DW[:, n, :]),
                                 ALU.mult).then_inc(s("xw_ready"), 1)
            for c in range(LT):
                for d in range(2):
                    V_.tensor_tensor(split_heads(XDT[:, c, d, :]), split_heads(XS[:, c, :]), per_head(dt_of(c, d)),
                                     ALU.mult).then_inc(s("xdt_ready"), 1)
                V_.tensor_tensor(split_heads(Ys[:, c, :]), split_heads(XS[:, c, :]), per_head(DSK), ALU.mult)\
                    .then_inc(s("ys_step"), 1)
            for k in range(4):
                dve.wait_ge(s("xw_used"), (2, 3, 5, 6)[k])
                V_.tensor_copy(state[:, 2 * k, :], stbank[2 * k]).then_inc(s("state_dve"), 1)
            dve.wait_ge(s("ys_step"), 2)

            def segments(k):
                c, g, d, hg = SEG[k]
                dve.wait_ge(s("R_mm"), k + 1)
                if k >= 4:
                    dve.wait_ge(s("intra_mm"), k - 3)
                for h in range(4):
                    col = PL[:, 2 * d + c, 8 * g + 4 * hg + h:8 * g + 4 * hg + h + 1]
                    ins = V_.tensor_scalar(seg[:, k % 4, h * P:(h + 1) * P], po[k % 2][:, h * P:(h + 1) * P], col, 0.0,
                                           ALU.subtract, ALU.min)
                ins.then_inc(s("seg_ready"), 1)

            segments(0)
            segments(1)
            for k in range(16):
                c, g, d, hg = SEG[k]
                dve.wait_ge(s("decay_ready"), k + 1)
                sv = seg[:, k % 4, :].rearrange("p (h i) -> p h i", h=4)
                V_.tensor_tensor(sv, sv, CB[:, 4 * d + 2 * c + g, :].unsqueeze(1).to_broadcast([P, 4, P]), ALU.mult)\
                    .then_inc(s("m_ready"), 1)
                if k < 12:
                    c, st, ex = INTER[k // 2]
                    g = k % 2
                    dve.wait_ge(s("inter_mm"), k + 1)
                    step(V_.tensor_tensor(split_heads(ytmp[:, :]), split_heads((pmod, p7)[k % 2][:, :]),
                                          per_head(EX[:, ex, 8 * g:8 * g + 8]), ALU.mult))
                    yg = Ys[:, c, g * 512:(g + 1) * 512]
                    V_.tensor_tensor(yg, yg, ytmp[:, :], ALU.add).then_inc(s("inter_read"), 1)
                    dve.wait_ge(s("inter_read"), k + 1)
                if k + 2 < 16:
                    segments(k + 2)
            dve.wait_ge(s("intra_mm"), 16)
            for c in range(LT):
                for g in range(2):
                    yg = Ys[:, c, g * 512:(g + 1) * 512]
                    ins = V_.tensor_tensor(yg, yg, acc[:, 2 * c + g, :], ALU.add)
            step(ins)
            V_.tensor_tensor(Ys[:, :, :], Ys[:, :, :], Z[:, :, :], ALU.mult).then_inc(s("yg_ready"), 1)
            dve.wait_ge(s("yrt_ready"), 1)
            step(V_.reciprocal(ysum[:, 2:4], ysum[:, 2:4]))
            for c in range(LT):
                V_.tensor_scalar(Ys[:, c, :], Ys[:, c, :], ysum[:, 2 + c:3 + c], None, ALU.mult)\
                    .then_inc(s("yn_C"), 1)
            for f in range(8):
                dve.wait_ge(s("mixC_hi_done"), f // 2 * 2 + 2)
                V_.scalar_tensor_tensor(out=mixC_lo[:, 8 + f, :], in0=acc[:, f // 2, (f % 2) * LAT:(f % 2 + 1) * LAT],
                                        scalar=vec[:, GNG + f:GNG + f + 1], in1=mixC_hi[:, 8 + f, :].bitcast(F32),
                                        op0=ALU.mult, op1=ALU.subtract).then_inc(s("mixC_lo_done"), 1)
            attention(1, mixC_hi, mixC_lo, probC, lambda u: (0, 4),
                      lambda u: qsc[:, (u // 2) % 2, 2 * (u // 4) + u % 2:2 * (u // 4) + u % 2 + 1],
                      lambda u: SINK[:, 2 * (u // 4) + u % 2:2 * (u // 4) + u % 2 + 1])
            out_projection(C_OUT, 1, LAT)
            norm(3, LAT)
            ffn(1, LAT)
            for c in range(LT):
                dve.wait_ge(s("oT_done"), 2 * c + 1)
                V_.tensor_copy(otile[:, c, 0:512], acc[:, 2 * c, :]).then_inc(s("out_dve"), 1)

        @block.tensor
        def _(pe):
            mm = nc.tensor.matmul
            ident = cst("ident")

            def T_(o, x, n=P):
                return nc.tensor.transpose(o, x, cst("ident", 0, n, 0, n))

            pe.wait_ge(s("const_loaded"), 16)
            pe.wait_ge(s("small_loaded"), 16 * SMALLS)
            T_(p7[:, 0:128], vrow[:, 0, :])
            T_(p7[:, 128:240], vrow[0:112, 1, :], 112)
            T_(p7[:, 240:364], vrow[0:124, 2, :], 124).then_inc(s("vec_T"), 1)
            pe.wait_ge(s("x_loaded"), 32)
            for f in range(KD):
                if f >= 4:
                    pe.wait_ge(s("xT_act") if f % 2 else s("xT_dve"), (f - 4) // 2 + 1)
                for t in range(TT):
                    ins = T_(acc[:, f % 4, t * P:(t + 1) * P], xin[:, t, f * P:(f + 1) * P])
                ins.then_inc(s("xT_done"), 1)

            def mod_unit(m):
                n, k = m // KD, m % KD
                r = m_raw[m]
                pe.wait_ge(raw_loaded[r % RAW_SLOTS], 16 * (r // RAW_SLOTS + 1))
                if m == 0:
                    pe.wait_ge(s("cvec_ready"), 1)
                if k == 0 and n:
                    pe.wait_ge(s("mod_ready"), n)
                for g in range(4):
                    ins = mm(pmod[32 * g:32 * g + 32, :], cvec[:, k, :], raw[:, r % RAW_SLOTS, g * 512:(g + 1) * 512],
                             start=(k == 0), stop=(k == KD - 1))
                ins.then_inc(mod_used, 1)

            def mod_T(n):
                pe.wait_ge(s("modc_ready"), n + 1)
                for b in range(4):
                    ins = T_(pmod[:, b * P:(b + 1) * P], modc[:, b * P:(b + 1) * P])
                ins.then_inc(s("modT_done"), 1)

            def norm(n, t):
                for f in range(KD):
                    pe.wait_ge(s("sq_ready"), KD * n + f + 1)
                    mm(p5[:, 0:t], cst("ones"), n_sq[:, f % 2, 0:t], start=(f == 0), stop=(f == KD - 1))\
                        .then_inc(s("ss_mm"), 1)

            norm(0, T)
            for m in range(KD):
                mod_unit(m)
            mod_T(0)

            def product(outs, hi, lo, rhs, kts, first=True, last=True, ready=None):
                for m, o in enumerate(outs):
                    cols = slice(m * P, (m + 1) * P)
                    for j in range(kts):
                        if ready is not None and m == 0:
                            ready(j)
                        xh, xl = rhs(j)
                        mm(o, hi[:, j, cols], xh, start=(first and j == 0), stop=False)
                        mm(o, hi[:, j, cols], xl, start=False, stop=False)
                        ins = mm(o, lo[:, j, cols], xh, start=False, stop=(last and j == kts - 1))
                return ins

            def token_product(o, hi, lo, tt, cols):
                for j in range(KD):
                    xh, xl = (h[:, j, tt * P:(tt + 1) * P] for h in (Hhi, Hlo))
                    mm(o, xh, hi[:, j, cols], start=(j == 0), stop=False)
                    mm(o, xl, hi[:, j, cols], start=False, stop=False)
                    ins = mm(o, xh, lo[:, j, cols], start=False, stop=(j == KD - 1))
                return ins

            def stream_in(n):
                return lambda j: pe.wait_ge(s("h_lo"), KD * n + j + 1)

            H = lambda t: (lambda j: (Hhi[:, j, 0:t], Hlo[:, j, 0:t]))

            def auxA(m):
                n = (4, 6, 7, 8, 9)[m]
                pe.wait_ge(read_act, A_READS[n][1])
                if m == 0:
                    mm(p5[:, :], cst("ones"), sqA[:, 0, 0, :], start=True, stop=True)
                    mm(p7[:, :], cst("ones"), sqA[:, 0, 1, :], start=True, stop=True)
                else:
                    if m == 1:
                        pe.wait_ge(s("krt_ready"), 2)
                    for i in range(2):
                        h = 2 * (m - 1) + i
                        mm(p7[0:16, :], cst("headA", 15 - h, 31 - h), sqA[:, m % 2, i, :], start=(h == 0),
                           stop=(h == A_HEADS - 1))
                    pe.wait_ge(s("rope_done"), m)
                for i in range(2):
                    ins = mm(p6[:, i * LAT:(i + 1) * LAT], cst("rotA"), QK[:, 2 * m + i, 0:LAT], start=True, stop=True)
                ins.then_inc(s("aux_done"), 1)

            for n, (kind, _, _) in enumerate(blocksA):
                lo = 2 * (n % 2)
                if n >= 2:
                    who, count = A_READS[n - 2]
                    pe.wait_ge(read_act if who == "act" else read_dve, count)
                pe.wait_ge(lo_split, n + 1)
                w_h, w_l = split_block(n, KD)
                if kind == "v":
                    for t in range(TT):
                        ins = token_product(acc[:, lo + t // 2, (t % 2) * BC:(t % 2 + 1) * BC], w_h, w_l, t, slice(0, BC))
                else:
                    ins = product([acc[:, lo + m, :] for m in range(2)], w_h, w_l, H(T), KD,
                                  ready=stream_in(0) if n == 0 else None)
                ins.then_inc(block_done, 1)
                if 1 <= n <= 8:
                    mod_unit(KD + n - 1)
                if n == 5:
                    auxA(0)
                if 7 <= n <= 9:
                    auxA(n - 6)
            auxA(4)
            pe.wait_ge(s("qrow_ready"), 1)
            pe.wait_ge(s("rope_done"), 5)
            for t in range(TT):
                ins = T_(p6[:, 16 * t:16 * t + 16], qrow[0:16, t * P:(t + 1) * P], 16)
            ins.then_inc(s("qrow_T"), 1)
            mod_T(1)
            pe.wait_ge(s("qsc_root"), 1)
            pe.wait_ge(s("k_scaled"), 2)

            def attention(layer, nk_of, scores, value, pr, prT, out_of):
                n0 = 32 * layer

                def S_(u):
                    if u >= 3:
                        pe.wait_ge(s("exp_done"), n0 + u - 2)
                    scores(u).then_inc(s("s_done"), 1)

                def turn(u):
                    pe.wait_ge(s("p_norm"), n0 + u + 1)
                    if u >= 2:
                        pe.wait_ge(s("pT_copied"), n0 + u - 1)
                    c0, nkt = nk_of(u)
                    for j in range(nkt):
                        ins = T_(acc[:, 2 + u % 2, j * P:(j + 1) * P], pr[:, u % 3, (c0 + j) * P:(c0 + j + 1) * P])
                    ins.then_inc(s("pT_done"), 1)

                def pv(u):
                    pe.wait_ge(s("pT_copied"), n0 + u + 1)
                    tile = u // 4
                    if u % 4 == 0 and tile >= 2:
                        pe.wait_ge(s("o_lo"), 8 * layer + tile - 1)
                    c0, nkt = nk_of(u)
                    for j in range(nkt):
                        ins = mm(out_of(u), value(u, c0 + j), prT[:, u % 2, j * P:(j + 1) * P], start=(j == 0),
                                 stop=(j == nkt - 1))
                    ins.then_inc(s("pv_done"), 1)

                S_(0)
                S_(1)
                for u in range(32):
                    if u + 2 < 32:
                        S_(u + 2)
                    turn(u)
                    if u:
                        pv(u - 1)
                    if layer == 0:
                        if u % 8 < 4:
                            for i in range(2):
                                mod_unit(KD * (2 + u // 8) + 2 * (u % 8) + i)
                        if u % 8 == 5:
                            mod_T(2 + u // 8)
                pv(31)

            def scoresA(u):
                h, t = u // 4, u % 4
                cols = slice(0, T) if t < LT else slice(LAT, T)
                return mm(sbank[u % 3][:, cols], QK[:, A_KV + h, t * P:(t + 1) * P], QK[:, h // 4, cols], start=True,
                          stop=True)

            attention(0, lambda u: (0, 4) if u % 4 < 2 else (2, 2), scoresA,
                      lambda u, j: V[:, j, (u // 16) * P:(u // 16 + 1) * P], prob, probT,
                      lambda u: po[(u // 4) % 2][:, (u % 4) * P:(u % 4 + 1) * P])

            pe.wait_ge(s("conv_dve"), B_CONV * (BT - 1))
            pe.wait_ge(s("conv_pool"), 1)
            for i in range(BT):
                ins = mm(p7[:, :], cst("ones"), Y[:, i, :], start=(i == 0), stop=(i == BT - 1))
            ins.then_inc(s("mu_mm"), 1)
            pe.wait_ge(s("mod_ready"), 6)
            for i in range(BT):
                pe.wait_ge(s("yq_ready"), i + 1)
                mm(pmod[:, :], cst("ones"), yq[:, i % 2, :], start=(i == 0), stop=(i == BT - 1)).then_inc(s("var_mm"), 1)

            def out_projection(w, kt, hi, lo, t, reads0, waits):
                for n in range(8):
                    pair = n // 2
                    for sem_, count in waits.get(n, ()):
                        pe.wait_ge(sem_, count)
                    if n % 2 == 0 and pair >= 2:
                        pe.wait_ge(read_dve, reads0 + pair - 1)
                    pe.wait_ge(lo_split, w + n + 1)
                    w_h, w_l = split_block(w + n, kt)
                    product([acc[:, 2 * (pair % 2) + m, 0:t] for m in range(2)], w_h, w_l,
                            lambda j: (hi[:, kt * (n % 2) + j, 0:t], lo[:, kt * (n % 2) + j, 0:t]), kt,
                            first=(n % 2 == 0), last=(n % 2 == 1)).then_inc(block_done, 1)

            out_projection(A_OUT, 6, hid_hi, hid_lo, T, after_A_in["dve"],
                           {0: ((s("exp_done"), 32), (s("pT_copied"), 32), (s("o_lo"), 8)),
                            1: ((s("mixA_lo"), 4),)})
            norm(1, T)

            def ffn(l, t):
                w = FF[l][1]
                hid = sum(HALF) // 2 * l
                first = [True]
                for half, nt in enumerate(HALF):
                    R, R2 = FFN_READS[l][2 * half], FFN_READS[l][2 * half + 1]
                    pe.wait_ge(read_act, R["act"])
                    pe.wait_ge(read_dve, R["dve"])
                    pe.wait_ge(s("h_lo"), KD * (2 * l + 2))

                    def up_or_gate(w, q, it, pair, per):
                        side = q % 2
                        pe.wait_ge(read_dve if side else read_act, at(R["dve" if side else "act"] + pair, it, per))
                        pe.wait_ge(lo_split, at(w + q + 1, it, 4))
                        w_h, w_l = split_block(w + q, KD)
                        product([acc[:, 2 * side + m, 0:t] for m in range(2)], w_h, w_l, H(t), KD).then_inc(block_done, 1)

                    n_in = nt // 4
                    with pe.Fori(0, n_in) as it:
                        for q in range(4):
                            up_or_gate(w, q, it, q // 2, 2)
                    w += 4 * n_in
                    for q in range(nt % 4):
                        up_or_gate(w, q, None, nt // 2 - 1, 0)
                    w += nt % 4
                    hid += nt // 2
                    pe.wait_ge(read_act, R2["act"])
                    pe.wait_ge(s("hid_lo_done"), hid)
                    kt = nt // 2
                    with pe.Fori(0, 2) as it:
                        for q in range(4):
                            if q % 2 == 0:
                                pe.wait_ge(read_dve, at(R2["dve"] + q // 2 - 1, it, 2))
                            pe.wait_ge(lo_split, at(w + q + 1, it, 4))
                            w_h, w_l = split_block(w + q, kt)
                            product([acc[:, q // 2 * 2 + m, 0:t] for m in range(2)], w_h, w_l,
                                    lambda j: (hid_hi[:, kt * (q % 2) + j, 0:t], hid_lo[:, kt * (q % 2) + j, 0:t]),
                                    kt, first=(q % 2 == 0), last=(q % 2 == 1)).then_inc(block_done, 1)
                    w += 8

            ffn(0, T)

            norm(2, T)

            def auxC(m):
                if m == 0:
                    pe.wait_ge(read_act, C_READS[7][1])
                    mm(p5[:, :], cst("pair"), sqK, start=True, stop=True)
                    mm(p6[:, 0:LAT], cst("rotC"), Kc[:, 0:LAT], start=True, stop=True).then_inc(s("aux_done"), 1)
                    return
                pe.wait_ge(read_act, C_READS[7 + m][1])
                for i in range(2):
                    tile = 2 * (m - 1) + i
                    mm(p7[0:16, 0:LAT], cst("headC", 15 - 2 * tile, 31 - 2 * tile), sqQ[(m - 1) % 2][:, i, :],
                       start=(tile == 0), stop=(tile == KD - 1))
                pe.wait_ge(s("rope_done"), 5 + m)
                for i in range(2):
                    ins = mm(p6[:, i * LAT:(i + 1) * LAT], cst("rotC"), Q[:, 2 * (m - 1) + i, :], start=True, stop=True)
                ins.then_inc(s("aux_done"), 1)

            w = C_IN
            pe.wait_ge(read_dve, FFN_READS[0][3]["dve"] + 4)
            for n, (kind, _, _) in enumerate(blocksC):
                lo = 2 * (n % 2)
                if n >= 2:
                    who, count = C_READS[n - 2]
                    pe.wait_ge(read_act if who == "act" else read_dve, count)
                pe.wait_ge(lo_split, w + n + 1)
                w_h, w_l = split_block(w + n, KD, 32 if kind == "dt" else BC)
                if kind == "dt":
                    for t in range(TT):
                        ins = token_product(acc[:, lo, 32 * t:32 * t + 32], w_h, w_l, t, slice(0, 32))
                elif kind == "kv":
                    product([acc[:, lo, :]], w_h, w_l, H(T), KD)
                    for t in range(TT):
                        ins = token_product(acc[:, lo + 1, P * t:P * t + P], w_h, w_l, t, slice(P, 2 * P))
                elif kind == "z":
                    for t in range(LT):
                        ins = token_product(acc[:, lo + t, 0:BC], w_h, w_l, t, slice(0, BC))
                else:
                    t = T if kind == "x" and n < 5 else LAT
                    ins = product([acc[:, lo + m, 0:t] for m in range(2)], w_h, w_l, H(t), KD,
                                  ready=stream_in(2) if n == 0 else None)
                ins.then_inc(block_done, 1)
                if 8 <= n <= 12:
                    auxC(n - 8)
            pe.wait_ge(s("qrow_ready"), 2)
            pe.wait_ge(s("rope_done"), 10)
            for t in range(LT):
                ins = T_(p6[:, 16 * t:16 * t + 16], qrowC[:, t * P:(t + 1) * P], 16)
            ins.then_inc(s("qrow_T"), 1)

            pe.wait_ge(read_act, after_C_in["act"])
            pe.wait_ge(read_dve, after_C_in["dve"])
            pe.wait_ge(s("da_ready"), 1)
            da_of = lambda t, d: dts[:, 7, 32 * t + 16 * d:32 * t + 16 * d + 16]
            for k, parts in enumerate(CUM):
                for i, (tri, t, d) in enumerate(parts):
                    ins = mm(p7[:, 16 * k:16 * k + 16], cst(tri), da_of(t, d), start=(i == 0), stop=(i == len(parts) - 1))
            ins.then_inc(s("cum_mm"), 1)
            for k in range(8):
                pe.wait_ge(s("xc_ready"), 4 * (k % 2) + 4)
                if k >= 4:
                    pe.wait_ge(s("xs_act") if k % 2 else s("xs_dve"), (k - 4) // 2 + 1)
                for b in range(4):
                    f = 4 * (k % 2) + b
                    ins = T_(acc[:, k % 4, b * P:(b + 1) * P], XC[:, f, (k // 2) * P:(k // 2 + 1) * P])
                ins.then_inc(s("xsT_done"), 1)
            pe.wait_ge(s("qsc_root"), 2)
            pe.wait_ge(s("xc_ready"), XBC_T)
            for k in range(2):
                for b in range(4):
                    t, g = 2 * k + b // 2, b % 2
                    ins = T_(po[k][:, b * P:(b + 1) * P], XC[:, 8 + g, t * P:(t + 1) * P])
                ins.then_inc(s("bT_done"), 1)
            for n in range(4):
                c, g = n // 2, n % 2
                ins = mm(pmod[:, n * P:(n + 1) * P], XC[:, 8 + g, c * P:(c + 1) * P], Cc[:, g, c * P:(c + 1) * P],
                         start=True, stop=True)
            ins.then_inc(s("cb_mm"), 1)
            pe.wait_ge(s("btok_ready"), 2)
            pe.wait_ge(s("xs_act"), 4)
            pe.wait_ge(s("xs_dve"), 4)
            pe.wait_ge(s("cb_ready"), 2)
            pe.wait_ge(s("ex_ready"), 1)
            for n, (t, k, first, last) in enumerate(((2, 0, 1, 0), (3, 0, 0, 1), (0, 1, 1, 1), (2, 2, 1, 0), (3, 2, 0, 1),
                                                     (1, 3, 1, 1))):
                pe.wait_ge(s("xw_ready"), n + 1)
                for g in range(2):
                    ins = mm(stbank[2 * k + g], Btok[:, t, g * P:(g + 1) * P], XW[:, n % 2, g * 512:(g + 1) * 512],
                             start=bool(first), stop=bool(last))
                ins.then_inc(s("xw_used"), 1)
            pe.wait_ge(s("state_act"), 4)
            pe.wait_ge(s("state_dve"), 4)
            pe.wait_ge(s("xdt_ready"), 4)

            def decays(k):
                if k >= 2:
                    pe.wait_ge(s("seg_ready"), k - 1)
                pe.wait_ge(s("rx_ready"), k + 1)
                mm(po[k % 2][:, :], cst("ones"), rx[:, k % 2, :], start=True, stop=True).then_inc(s("R_mm"), 1)

            decays(0)
            decays(1)
            for k in range(16):
                if k < 12:
                    c, st, ex = INTER[k // 2]
                    g = k % 2
                    if k >= 2:
                        pe.wait_ge(s("inter_read"), k - 1)
                    mm((pmod, p7)[k % 2][:, :], Cc[:, g, c * P:(c + 1) * P], state[:, 2 * st + g, :], start=True, stop=True)\
                        .then_inc(s("inter_mm"), 1)
                c, g, d, hg = SEG[k]
                pe.wait_ge(s("m_ready"), k + 1)
                for h in range(4):
                    hh = 4 * hg + h
                    ins = mm(acc[:, 2 * c + g, hh * S_HD:(hh + 1) * S_HD], seg[:, k % 4, h * P:(h + 1) * P],
                             XDT[:, c, d, (8 * g + hh) * S_HD:(8 * g + hh + 1) * S_HD],
                             start=(d == 0 and hg == 0 and h == 0), stop=(d == 1), skip_group_check=True)
                ins.then_inc(s("intra_mm"), 1)
                if k + 2 < 16:
                    decays(k + 2)
            pe.wait_ge(s("yn_C"), 2)
            for k in range(4):
                for i in range(2):
                    for c in range(LT):
                        f = 2 * k + i
                        ins = T_(acc[:, k, (2 * i + c) * P:(2 * i + c + 1) * P], Ys[:, c, f * P:(f + 1) * P])
                ins.then_inc(s("yT_done"), 1)

            pe.wait_ge(s("mixC_lo_done"), 8)
            pe.wait_ge(s("k2_ready"), 1)
            pe.wait_ge(s("seg_ready"), 16)

            def scoresC(u):
                tile, t, e = u // 4, (u // 2) % 2, u % 2
                rows_ = slice(64 * e, 64 * e + 64)
                mm(sbank[u % 3], Q[rows_, tile, t * P:(t + 1) * P], K2[rows_, tile // 4, :], start=True, stop=False,
                   skip_group_check=True)
                o = 1 - t
                return mm(sbank[u % 3][:, o * P:(o + 1) * P], ident, cst("mask", t * P, (t + 1) * P), start=False,
                          stop=True, skip_group_check=True)

            attention(1, lambda u: (0, 4), scoresC, lambda u, j: Vc[:, j, (u // 16) * C_HD:(u // 16 + 1) * C_HD], probC,
                      probTC, lambda u: po[(u // 4) % 2][64 * (u % 2):64 * (u % 2) + 64,
                                                       ((u // 2) % 2) * P:((u // 2) % 2 + 1) * P])
            out_projection(C_OUT, 8, mixC_hi, mixC_lo, LAT, after_C_in["dve"],
                           {0: ((s("exp_done"), 64), (s("pT_copied"), 64), (s("o_lo"), 16))})
            norm(3, LAT)
            ffn(1, LAT)
            pe.wait_ge(read_dve, FFN_READS[1][3]["dve"] + 4)
            for k in range(4):
                for b in range(4):
                    ins = T_(acc[:, k, b * P:(b + 1) * P], X[:, 4 * (k % 2) + b, (k // 2) * P:(k // 2 + 1) * P])
                ins.then_inc(s("oT_done"), 1)


SEG = [(c, g, d, hg) for c in range(2) for g in range(2) for d in range(2) for hg in range(2)]
INTER = [(0, 0, 4), (0, 2, 9), (0, 3, 6), (1, 0, 8), (1, 1, 5), (1, 2, 7)]
CUM = [
    (("after", 2, 0), ("ones", 3, 0)), (("after", 3, 0),),
    (("before", 2, 1),), (("before", 3, 1), ("ones", 2, 1)),
    (("upto", 0, 0),), (("upto", 1, 0),),
    (("from", 0, 1),), (("from", 1, 1),),
    (("upto", 1, 0), ("ones", 0, 0)),
    (("from", 0, 1), ("ones", 1, 1)),
    (("after", 0, 0),), (("before", 1, 1),),
]
SMALLS = 18

INPUTS = ["x", "c", "ctx", "c_ctx", "mod_w", "mod_b", "norm1_g", "norm2_g", "ffn_w_in", "ffn_w_out", "ev_w_in",
          "ev_w_out", "ev_q_g", "ev_k_g", "ev_dw_w", "ev_dw_b", "ev_cn_g", "ev_cn_b", "od_w_in", "od_w_out",
          "od_q_g", "od_k_g", "od_sink", "od_conv_w", "od_conv_b", "od_dt_bias", "od_A_log", "od_D", "od_gnorm_g"]


def kernel(**inputs):
    import concourse.bacc as bacc
    from concourse.bass_utils import run_bass_kernel_spmd

    nc = bacc.Bacc("TRN2", target_bir_lowering=False, num_devices=1)
    arrays, aps = {}, {}
    for name in INPUTS + ["const"]:
        arr = constants() if name == "const" else np.ascontiguousarray(inputs[name])
        arrays[f"in_{name}"] = arr
        aps[name] = nc.dram_tensor(f"in_{name}", arr.shape, mybir.dt.from_np(arr.dtype), kind="ExternalInput").ap()
    out = nc.dram_tensor("out", (1, LAT, D), F32, kind="ExternalOutput").ap()
    build_trunk(nc, aps, out)
    r = run_bass_kernel_spmd(nc, [arrays], core_ids=[0])
    return r.results[0]["out"]
```

```python
import math
from contextlib import ExitStack

import numpy as np

import concourse.bass as bass
from concourse import mybir

F32 = mybir.dt.float32
F32R = mybir.dt.float32r
ALU = mybir.AluOpType
ACT = mybir.ActivationFunctionType
AX = mybir.AxisListType

P = 128
D = 1024
KD = D // P
LAT = 256
CTX = 256
T = LAT + CTX
TT = T // P
LT = LAT // P
DEPTH = 2
EPS = 1e-6
GRID_W = 64
THETA = 10000.0

A_HEADS, A_KV, A_HD = 8, 2, 128
B_WIDTH, B_CONV = 512, 31
BT = B_WIDTH // P
C_HEADS, C_HD, C_WINDOW = 16, 64, 128
S_HEADS, S_HD, S_STATE, S_GROUPS, S_CONV = 16, 64, 128, 2, 5
S_INNER = S_HEADS * S_HD
XBC_T = (S_INNER + 2 * S_GROUPS * S_STATE) // P
HG = S_HEADS // S_GROUPS
FFN = 2816
HALF = (12, 10)
BC = 256
RAW_SLOTS = 4
MOD_COLS = 2048
NEG = -1e30

CONST_COLS = {}


def _const_layout():
    at = 0
    for name, n in (("ident", P), ("ones", P), ("rotA", P), ("rotC", P), ("upto", P), ("from", P),
                    ("before", P), ("after", P), ("pair", P), ("headA", 32), ("headC", 32),
                    ("mask", 2 * P), ("cosA", LAT), ("sinA", LAT), ("cosC", LAT), ("sinC", LAT)):
        CONST_COLS[name] = (at, n)
        at += n
    return at


CONST_N = _const_layout()


def _rope(head_dim):
    rows = LAT // GRID_W
    row = np.repeat(np.arange(rows), GRID_W).astype(np.float32)
    col = np.tile(np.arange(GRID_W), rows).astype(np.float32)
    quarter = head_dim // 4
    inv = (np.float32(THETA) ** (-np.arange(quarter, dtype=np.float32) / np.float32(quarter))).astype(np.float32)
    ar, ac = row[:, None] * inv, col[:, None] * inv
    ang = np.concatenate([ar, ar, ac, ac], axis=-1)
    reps = P // head_dim
    return (np.tile(np.cos(ang).T.astype(np.float32), (reps, 1)),
            np.tile(np.sin(ang).T.astype(np.float32), (reps, 1)))


def _rot(head_dim):
    q = head_dim // 4
    m = np.zeros((P, P), np.float32)
    for o in range(P):
        if (o // q) % 2 == 0:
            m[o + q, o] = -1.0
        else:
            m[o - q, o] = 1.0
    return m


def constants():
    c = np.zeros((P, CONST_N), np.float32)
    k, i = np.arange(P)[:, None], np.arange(P)[None, :]

    def put(name, a):
        at, n = CONST_COLS[name]
        c[:, at:at + n] = a

    put("ident", np.eye(P))
    put("ones", 1.0)
    put("rotA", _rot(A_HD))
    put("rotC", _rot(C_HD))
    put("upto", k <= i)
    put("from", k >= i)
    put("before", k < i)
    put("after", k > i)
    put("pair", (k // C_HD) == (i // C_HD))
    j = np.arange(32)[None, :]
    put("headA", np.broadcast_to(j == 15, (P, 32)))
    put("headC", ((j == 15) & (k < C_HD)) | ((j == 16) & (k >= C_HD)))
    put("mask", np.concatenate([np.where(i <= k, 0.0, NEG), np.where(i >= k, 0.0, NEG)], axis=1))
    for name, hd in (("A", A_HD), ("C", C_HD)):
        cos, sin = _rope(hd)
        put("cos" + name, cos)
        put("sin" + name, sin)
    return c


MODB, N1G, N2G = 0, 96, 112
DWB, CNG, CNB, CVB, GNG, CVEC, AQG, AKG, CQG, CKG, CVW = 128, 132, 136, 140, 152, 160, 176, 177, 178, 179, 180
DWW = 240
VEC_N = 364
SH1, SC1, G1, SH2, SC2, G2 = 0, 8, 16, 24, 32, 40


class Chain:

    def __init__(self, eng, sem):
        self.eng, self.sem, self.n = eng, sem, 0

    def mark(self, ins):
        ins.then_inc(self.sem, 1)
        self.n += 1
        return self.n

    def need(self, count):
        self.eng.wait_ge(self.sem, count)

    def __call__(self, ins):
        self.need(self.mark(ins))


def at(base, it=None, per=0):
    return base if it is None or per == 0 else it * per + base


def build_trunk(nc, a, out):
    with ExitStack() as ctx:
        def sem(name):
            return ctx.enter_context(nc.semaphore(name))

        def psum(name, shape):
            return ctx.enter_context(nc.psum_tensor(name, shape, F32))

        base = (nc.sbuf_base + 31) // 32 * 32
        room = nc.sbuf_usable_end - base - 32
        ctx.enter_context(nc.sbuf_tensor("arena", [P, room // 4], F32))
        place = [base]

        def region(size):
            start = place[0]
            place[0] += (size + 31) // 32 * 32
            assert place[0] <= base + room, (place[0], base + room)
            return start

        def view(name, shape, offset, dtype=F32):
            return nc.alloc_sbuf_tensor_at(name, [P] + list(shape), dtype, offset=offset)

        r_x, r_h, r_big = region(KD * T * 4), region(2 * KD * T * 4), region(2 * 12 * T * 4)
        r_raw, r_split = region(RAW_SLOTS * 8192), region(4 * 8192)
        r_const, r_misc = region(CONST_N * 4), region(29632)
        X = view("X", [KD, T], r_x)
        Hhi = view("Hhi", [KD, T], r_h, F32R)
        Hlo = view("Hlo", [KD, T], r_h + KD * T * 4, F32R)
        hid_hi = view("hid_hi", [12, T], r_big, F32R)
        hid_lo = view("hid_lo", [12, T], r_big + 12 * T * 4, F32R)
        mixC_hi = view("mixC_hi", [16, LAT], r_big, F32R)
        mixC_lo = view("mixC_lo", [16, LAT], r_big + 16 * LAT * 4, F32R)
        raw = view("raw", [RAW_SLOTS, 2048], r_raw)
        w_hi = view("w_hi", [2, 2048], r_split, F32R)
        w_lo = view("w_lo", [2, 2048], r_split + 16384, F32R)
        const = view("const", [CONST_N], r_const)
        modc = view("modc", [512], region(2048))
        vec = view("vec", [VEC_N], region(VEC_N * 4))
        cvec = view("cvec", [KD, 32], region(1024))
        mod = view("mod", [DEPTH, 48, 2], region(768))
        gain = view("gain", [4, KD, 2], region(256))
        rows = view("rows", [96], region(384))
        qsc = view("qsc", [TT, 16], region(256))
        sm = view("sm", [3, 8], region(96))
        ysum = view("ysum", [4], region(32))
        epsc = view("epsc", [1], region(32))
        DTB, ALOG, DSK, SINK = rows[:, 0:32], rows[:, 32:64], rows[:, 64:80], rows[:, 80:96]
        assert VEC_N == DWW + B_CONV * BT

        xin = view("xin", [TT, D], r_h)
        vrow = view("vrow", [3, P], r_big)
        x_rms = view("x_rms", [KD, T], r_h + KD * T * 4)
        n_h = view("n_h", [4, T], r_misc)
        n_sq = view("n_sq", [2, T], r_misc + 8192)
        n_rt = view("n_rt", [T], r_misc + 12288)
        n_rs = view("n_rs", [T], r_misc + 14336)
        n_t = view("n_t", [2, T], r_misc + 16384)
        QK = view("QK", [A_KV + A_HEADS, T], r_misc)
        U = view("U", [BT, 2, LAT + B_CONV - 1], r_misc + 20480)
        sgate = view("sgate", [BT, T], r_big)
        sqA = view("sqA", [2, 2, T], r_big + 8192)
        ptap = view("ptap", [T], r_big + 20480)
        ropeT = view("ropeT", [2, LAT], r_big + 32768 - 2048)
        V = view("V", [TT, A_KV * A_HD], r_big + 8 * T * 4)
        Y = view("Y", [BT, T], r_big + 20 * T * 4)
        prob = view("prob", [3, T], r_h)
        probT = view("probT", [2, T], r_h + 6144)
        yc = view("yc", [BT, T], r_h + 10240)
        yq = view("yq", [2, T], r_h + 18432)
        l_rt = view("l_rt", [T], r_h + 22528)
        yz = view("yz", [2, T], r_h + 24576)
        qrow = view("qrow", [T], r_h + 28672)
        krt = view("krt", [2, T], r_big + 24576)
        Q = view("Q", [KD, LAT], r_misc)
        Kc = view("Kc", [T], r_misc + 8192)
        K2 = view("K2", [2, T], r_misc + 10240)
        Vc = view("Vc", [TT, 2 * C_HD], r_misc + 14336)
        Z = view("Z", [KD, LAT], r_misc + 16384)
        ptapC = view("ptapC", [2, LAT], r_misc + 16384)
        vT = view("vT", [T], r_misc + 18432)
        dtT = view("dtT", [T], r_misc + 20480)
        dts = view("dts", [8, TT * 32], r_misc + 24576)
        dt_, da = dts[:, 6, :], dts[:, 7, :]
        XB = view("XB", [XBC_T, 2, LAT + S_CONV - 1], r_big)
        r_xc = r_big + 24960
        XC = view("XC", [10, T], r_xc)
        Cc = view("Cc", [S_GROUPS, LAT], r_xc + 10 * T * 4)
        HF = view("HF", [2, KD, T], r_h)
        XS = [HF[:, t // 2, 4 * (t % 2):4 * (t % 2) + 4, LAT:T] for t in range(TT)]
        XDT = [[HF[:, c, 4 * d:4 * d + 4, 0:LAT] for d in range(2)] for c in range(LT)]
        state = view("state", [4, 2, 512], r_big)
        Btok = view("Btok", [TT, S_GROUPS * S_STATE], r_big + 12288)
        XW = view("XW", [2, S_INNER], r_big + 16384)
        Cd = view("Cd", [4, 512], r_big + 16384)
        Dcol = view("Dcol", [KD], region(32))
        ysq = view("ysq", [2, LAT], r_misc + 24576 + 512)
        yrs = view("yrs", [LAT], r_h + 26624)
        yN = view("yN", [2, LAT], r_h + 27648)
        EX = view("EX", [12, 16], region(768))
        PL = view("PL", [4, 16], region(256))
        DW = view("DW", [6, 16], region(384))
        CB = X[:, :, LAT:LAT + P]
        sqQ = [X[:, 2 * i:2 * i + 2, LAT:T] for i in range(2)]
        sqK = X[:, 4:6, LAT:T]
        kroot = X[:, 6:8, LAT:T]
        qrowC = X[0:16, 4, LAT:T]
        ropeC = modc[:, :].rearrange("p (s t) -> p s t", s=2)
        probC = view("probC", [3, T], r_h + 16384)
        probTC = view("probTC", [2, T], r_h + 22528)
        f_gate = view("f_gate", [2, T], r_misc)
        f_h = view("f_h", [2, T], r_misc + 4096)
        otile = view("otile", [LT, D], r_h)

        def cst(name, lo=0, hi=None, p0=0, p1=P):
            s, n = CONST_COLS[name]
            return const[p0:p1, s + lo:s + (n if hi is None else hi)]

        acc = psum("acc", [P, 4, 512])
        pmod = psum("pmod", [P, 512])
        p5 = psum("p5", [P, 512])
        p6 = psum("p6", [P, 512])
        p7 = psum("p7", [P, 512])
        sbank = [acc[:, 0, :], acc[:, 1, :], p7[:, :]]
        po = [p5, p6]
        stbank = [acc[:, 0, :], acc[:, 1, :], acc[:, 2, :], acc[:, 3, :], p5[:, :], p6[:, :], pmod[:, :], p7[:, :]]

        S = {}

        def s(name):
            if name not in S:
                S[name] = sem(name)
            return S[name]

        raw_loaded = [s(f"raw_loaded{i}") for i in range(RAW_SLOTS)]
        hi_split, lo_split, block_done = s("hi_split"), s("lo_split"), s("block_done")
        mod_used, read_act, read_dve = s("mod_used"), s("read_act"), s("read_dve")

        def tiles(w):
            return w.rearrange("(k p) n -> p k n", p=P)

        ev_in, ev_out = tiles(a["ev_w_in"][0]), tiles(a["ev_w_out"][0])
        od_in, od_out = tiles(a["od_w_in"][0]), tiles(a["od_w_out"][0])
        ffn_in = [tiles(a["ffn_w_in"][l]) for l in range(DEPTH)]
        ffn_out = [tiles(a["ffn_w_out"][l]) for l in range(DEPTH)]
        GLU_A, GLU_G = A_HEADS * A_HD + 2 * A_KV * A_HD, A_HEADS * A_HD + 2 * A_KV * A_HD + B_WIDTH
        blocksA = ([("g", ev_in, GLU_G + BC * i) for i in range(2)] + [("a", ev_in, GLU_A + BC * i) for i in range(2)]
                   + [("k", ev_in, A_HEADS * A_HD), ("v", ev_in, A_HEADS * A_HD + A_KV * A_HD)]
                   + [("q", ev_in, BC * i) for i in range(4)])
        C_Q = C_HEADS * C_HD
        C_X = C_Q + 4 * C_HD
        C_DT = C_X + XBC_T * P
        blocksC = ([("x", od_in, C_X), ("dt", od_in, C_DT)] + [("x", od_in, C_X + BC * i) for i in range(1, 6)]
                   + [("kv", od_in, C_Q)]
                   + [("q", od_in, BC * i) for i in range(4)] + [("z", od_in, C_DT + 32 + BC * i) for i in range(4)])
        stream = [("mod", 0, 0, k) for k in range(KD)]
        for n, (_, src, col) in enumerate(blocksA):
            stream.append(("w", src, 0, KD, col, BC))
            if 1 <= n <= 8:
                stream.append(("mod", 0, 1, n - 1))
        ev_out_blocks = [("w", ev_out, 6 * (n % 2), 6, BC * (n // 2), BC) for n in range(8)]
        stream.append(ev_out_blocks[0])
        for l, j in ((0, 2), (1, 0), (1, 1), (1, 2)):
            stream += [("mod", l, j, k) for k in range(KD)]
        stream += ev_out_blocks[1:]
        FF = []
        NW = lambda: sum(i[0] == "w" for i in stream)

        def add_ffn(l):
            FF.append((len(stream), NW()))
            for half, nt in enumerate(HALF):
                t0 = sum(HALF[:half])
                for p_ in range(nt // 2):
                    for side in range(2):
                        stream.append(("w", ffn_in[l], 0, KD, side * FFN + P * t0 + BC * p_, BC))
                for m in range(4):
                    for part in range(2):
                        stream.append(("w", ffn_out[l], t0 + part * nt // 2, nt // 2, BC * m, BC))

        add_ffn(0)
        C_IN = NW()
        stream += [("w", src, 0, KD, col, 32 if kind == "dt" else BC) for kind, src, col in blocksC]
        C_OUT = NW()
        stream += [("w", od_out, 8 * (n % 2), 8, BC * (n // 2), BC) for n in range(8)]
        add_ffn(1)
        A_OUT = len(blocksA)
        idle = (C_OUT + 1) % 2 * 8192
        rx = view("rx", [4, 512], r_split + idle)
        seg = view("seg", [4, 512], r_split + 16384 + idle)
        w_raw = [r for r, i in enumerate(stream) if i[0] == "w"]
        m_raw = [r for r, i in enumerate(stream) if i[0] == "mod"]
        w_index = {r: n for n, r in enumerate(w_raw)}
        m_index = {r: n for n, r in enumerate(m_raw)}

        def raw_block(r, kt, cols=BC):
            return raw[:, r % RAW_SLOTS, 0:kt * cols].rearrange("p (k n) -> p k n", k=kt)

        def split_block(w, kt, cols=BC):
            return [x[:, w % 2, 0:kt * cols].rearrange("p (k n) -> p k n", k=kt) for x in (w_hi, w_lo)]

        block = ctx.enter_context(nc.Block())

        fold = lambda x: x.rearrange("l (f p) -> (l f) p", p=P)
        VECTORS = [
            (1, CVEC - 128, 8, fold(a["c"])), (1, CVEC - 120, 8, a["c_ctx"].rearrange("(f p) -> f p", p=P)),
            (1, DWB - 128, 4, fold(a["ev_dw_b"])), (1, CNG - 128, 4, fold(a["ev_cn_g"])),
            (1, CNB - 128, 4, fold(a["ev_cn_b"])), (1, CVB - 128, 12, fold(a["od_conv_b"])),
            (1, GNG - 128, 8, fold(a["od_gnorm_g"])), (1, AQG - 128, 1, a["ev_q_g"]), (1, AKG - 128, 1, a["ev_k_g"]),
            (1, CVW - 128, 60, a["od_conv_w"][0].rearrange("t (f p) -> (t f) p", p=P)),
            (0, MODB, 96, fold(a["mod_b"])), (0, N1G, 16, fold(a["norm1_g"])), (0, N2G, 16, fold(a["norm2_g"])),
            (2, 0, 124, a["ev_dw_w"][0].rearrange("t (f p) -> (t f) p", p=P)),
        ]

        def small_rows(eng, part):
            for slot, r0, n, src in VECTORS[part::2]:
                eng.dma_start(vrow[r0:r0 + n, slot, :], src).then_inc(s("small_loaded"), 16)
            r0, name = ((CQG, "od_q_g"), (CKG, "od_k_g"))[part]
            for half in range(2):
                eng.dma_start(vrow[r0 - 128:r0 - 127, 1, half * C_HD:(half + 1) * C_HD], a[name])\
                    .then_inc(s("small_loaded"), 16)

        @block.sync
        def _(sp):
            small_rows(sp, 0)
            for t in range(TT):
                src = (a["x"] if t < LT else a["ctx"])[0]
                if t % LT == 0:
                    sp.dma_start(xin[:, t:t + LT, :], src.rearrange("(t p) d -> p t d", p=P)).then_inc(s("x_loaded"), 16)

            def free(r):
                if r < RAW_SLOTS:
                    return
                last = r - RAW_SLOTS
                if last in m_index:
                    sp.wait_ge(mod_used, m_index[last] + 1)
                else:
                    sp.wait_ge(lo_split, w_index[last] + 1)

            def load(r):
                item = stream[r]
                free(r)
                if item[0] == "mod":
                    _, l, j, k = item
                    sp.dma_start(raw[:, r % RAW_SLOTS, :],
                                 a["mod_w"][l, k * P:(k + 1) * P, j * MOD_COLS:(j + 1) * MOD_COLS])\
                        .then_inc(raw_loaded[r % RAW_SLOTS], 16)
                else:
                    _, src, k0, kt, col, cols = item
                    sp.dma_start(raw_block(r, kt, cols), src[:, k0:k0 + kt, col:col + cols])\
                        .then_inc(raw_loaded[r % RAW_SLOTS], 16)

            def load_loop(r, w, times, where):
                with sp.Fori(0, times) as it:
                    for q in range(4):
                        sp.wait_ge(lo_split, at(w + q - RAW_SLOTS + 1, it, 4))
                        src, kt = where(q, it)
                        sp.dma_start(raw_block(r + q, kt), src).then_inc(raw_loaded[(r + q) % RAW_SLOTS], 16)

            def load_ffn(l):
                r, w = FF[l]
                for half, nt in enumerate(HALF):
                    t0 = sum(HALF[:half])
                    n_in = nt // 4
                    load_loop(r, w, n_in, lambda q, it: (
                        ffn_in[l][:, :, bass.ds(it * (2 * BC) + ((q % 2) * FFN + P * t0 + BC * (q // 2)), BC)], KD))
                    r, w = r + 4 * n_in, w + 4 * n_in
                    for _ in range(nt % 4):
                        load(r)
                        r, w = r + 1, w + 1
                    load_loop(r, w, 2, lambda q, it: (
                        ffn_out[l][:, t0 + (q % 2) * nt // 2:t0 + (q % 2 + 1) * nt // 2,
                                   bass.ds(it * (2 * BC) + BC * (q // 2), BC)], nt // 2))
                    r, w = r + 8, w + 8
                return r

            for r in range(FF[0][0]):
                if r == RAW_SLOTS:
                    for lo, n, src in ((0, 32, a["od_dt_bias"]), (32, 32, a["od_A_log"])):
                        sp.dma_start(rows[:, lo:lo + n], src.rearrange("l d h -> l (d h)").partition_broadcast(P)[:, 0, :])\
                            .then_inc(s("rows_loaded"), 16)
                    for lo, n, src in ((64, 16, a["od_D"]), (80, 16, a["od_sink"])):
                        sp.dma_start(rows[:, lo:lo + n], src.partition_broadcast(P)[:, 0, :])\
                            .then_inc(s("rows_loaded"), 16)
                load(r)
            r = load_ffn(0)
            while r < FF[1][0]:
                load(r)
                r += 1
            load_ffn(1)
            for c in range(LT):
                sp.wait_ge(s("out_act"), c + 1)
                sp.wait_ge(s("out_dve"), c + 1)
                sp.dma_start(out[0, c * P:(c + 1) * P, :], otile[:, c, :]).then_inc(s("out_stored"), 16)
            sp.wait_ge(s("out_stored"), 16 * LT)

        def splitters(eng, kind):
            def split(w, it=None, first_only=False):
                r = w_raw[w]
                kt, cols = (8, BC) if it is not None else (stream[r][3], stream[r][5])
                n = kt * cols
                if kind == "hi":
                    eng.wait_ge(raw_loaded[r % RAW_SLOTS], at(16 * (r // RAW_SLOTS + 1), it, 16))
                    if w >= 2:
                        eng.wait_ge(block_done, at(w - 1, it, 4))
                    nc.scalar.activation(w_hi[:, w % 2, 0:n], raw[:, r % RAW_SLOTS, 0:n], ACT.Copy).then_inc(hi_split, 1)
                else:
                    eng.wait_ge(hi_split, at(w + 1, it, 4))
                    nc.vector.tensor_tensor(w_lo[:, w % 2, 0:n], raw[:, r % RAW_SLOTS, 0:n],
                                            w_hi[:, w % 2, 0:n].bitcast(F32), ALU.subtract).then_inc(lo_split, 1)
            return split

        def conv_C(i):
            if i < 10:
                return (XC[:, i, :].rearrange("p (s t) -> p s t", s=2), lambda tap: XB[:, i, :, tap:tap + LAT])
            return Cc[:, i - 10, :], lambda tap: XB[:, i, 0, tap:tap + LAT]

        XS_BANK = (p5, pmod, p5, pmod, p7, p5, pmod, p7)
        RB = (p5, p6, p7)

        def xs_half(k):
            return XS[XS_TILES[k // 2]][:, 2 * (k % 2):2 * (k % 2) + 2, :]

        def decayed_C(eng, k):
            b, c, _ = SEG[k]
            cv = Cd[:, k % 4, :].rearrange("p (h i) -> p h i", h=4)
            return eng.tensor_tensor(cv, cv, Cc[:, b // 2, c * P:(c + 1) * P].unsqueeze(1).to_broadcast([P, 4, P]), ALU.mult)

        def x_block(j):
            return j + (j > 0)

        def cvw(tap, i):
            return vec[:, CVW + XBC_T * tap + i:CVW + XBC_T * tap + i + 1]


        reads = {"act": 0, "dve": 0}
        A_READS, C_READS = [], []
        for kind, _, _ in blocksA:
            who = {"g": "act", "a": "dve", "k": "act", "v": "dve", "q": "act"}[kind]
            reads[who] += 1
            A_READS.append((who, reads[who]))
        after_A_in = dict(reads)
        reads["dve"] += 4
        FFN_READS = []

        def ffn_reads():
            res = []
            for nt in HALF:
                res.append(dict(reads))
                reads["act"] += nt // 2
                reads["dve"] += nt // 2
                res.append(dict(reads))
                reads["dve"] += 4
            FFN_READS.append(res)

        ffn_reads()
        for kind, _, _ in blocksC:
            who = {"x": "act", "dt": "act", "kv": "act", "q": "act", "z": "act"}[kind]
            reads[who] += 1
            C_READS.append((who, reads[who]))
        after_C_in = dict(reads)
        reads["dve"] += 4
        ffn_reads()

        @block.gpsimd
        def _(pool):
            step = Chain(pool, s("pool_step"))
            nc.gpsimd.memset(U[:, :, :, :], 0.0).then_inc(s("pads_A"), 1)

            def norm_lo(n, t):
                for f in range(KD):
                    if n == 0 and f % 2:
                        pool.wait_ge(s("h_lo_dve"), f // 2 + 1)
                        nc.gpsimd.memset(ptap[:, f:f + 1], 0.0).then_inc(s("h_lo"), 1)
                        continue
                    pool.wait_ge(s("h_hi"), KD * n + f + 1)
                    nc.gpsimd.tensor_tensor(Hlo[:, f, 0:t], n_h[:, f % 4, 0:t], Hhi[:, f, 0:t].bitcast(F32),
                                            ALU.subtract).then_inc(s("h_lo"), 1)

            norm_lo(0, T)
            pool.wait_ge(read_dve, 2)
            pool.wait_ge(s("vec_ready"), 1)
            i = BT - 1
            y = Y[:, i, :].rearrange("p (s t) -> p s t", s=2)
            z = ptap[:, :].rearrange("p (s t) -> p s t", s=2)
            step(nc.gpsimd.tensor_scalar(y, U[:, i, :, 0:LAT], vec[:, DWW + i:DWW + i + 1],
                                         vec[:, DWB + i:DWB + i + 1], ALU.mult, ALU.add))
            for tap in range(1, B_CONV):
                col = DWW + tap * BT + i
                step(nc.gpsimd.tensor_scalar(z, U[:, i, :, tap:tap + LAT], vec[:, col:col + 1], 0.0, ALU.mult, ALU.add))
                step(nc.gpsimd.tensor_tensor(y, y, z, ALU.add))
            nc.gpsimd.memset(ptap[:, 0:1], 0.0).then_inc(s("conv_pool"), 1)
            norm_lo(1, T)
            norm_lo(2, T)
            pool.wait_ge(s("h_lo"), 3 * KD)
            nc.gpsimd.memset(XB[:, :, :, 0:2], 0.0).then_inc(s("pads_C"), 1)
            nc.gpsimd.memset(XB[:, :, :, 2 + LAT:4 + LAT], 0.0).then_inc(s("pads_C"), 1)
            pool.wait_ge(s("pads_C"), 2)
            for i in range(8, XBC_T):
                pool.wait_ge(read_act, C_READS[x_block(i // 2)][1])
                o, src = conv_C(i)
                z = ptapC[:, 0:2, :] if i < 10 else ptapC[:, 0, :]
                step(nc.gpsimd.tensor_scalar(o, src(0), cvw(0, i), vec[:, CVB + i:CVB + i + 1], ALU.mult, ALU.add))
                for tap in range(1, S_CONV):
                    step(nc.gpsimd.tensor_scalar(z, src(tap), cvw(tap, i), 0.0, ALU.mult, ALU.add))
                    ins = nc.gpsimd.tensor_tensor(o, o, z, ALU.add)
                    if tap < S_CONV - 1:
                        step(ins)
                ins.then_inc(s("conv_C_pool"), 1)
                pool.wait_ge(s("conv_C_pool"), i - 7)
            pool.wait_ge(block_done, C_OUT)
            pool.wait_ge(s("da_ready"), 1)
            for k, (b, c, d) in enumerate(SEG):
                if k >= 4:
                    pool.wait_ge(s("R_mm"), k - 3)
                at_ = 32 * c + 16 * d + 4 * b
                nc.gpsimd.tensor_tensor(rx[:, k % 4, :].rearrange("p (h i) -> p h i", h=4),
                                        cst(("upto", "from")[d]).unsqueeze(1).to_broadcast([P, 4, P]),
                                        dts[:, 7, at_:at_ + 4].unsqueeze(2).to_broadcast([P, 4, P]), ALU.mult)\
                    .then_inc(s("rx_ready"), 1)
                if k >= 4 and k % 2:
                    pool.wait_ge(s("cexp_ready"), k - 3)
                    decayed_C(nc.gpsimd, k - 4).then_inc(s("cd_pool"), 1)
            pool.wait_ge(s("cexp_ready"), 14)
            decayed_C(nc.gpsimd, 13).then_inc(s("cd_pool"), 1)
            norm_lo(3, LAT)

        @block.scalar
        def _(act):
            step = Chain(act, s("act_step"))
            split = splitters(act, "hi")
            A = nc.scalar.activation

            act.dma_start(const[:, :], a["const"]).then_inc(s("const_loaded"), 16)
            small_rows(act, 1)

            act.wait_ge(s("vec_ready"), 1)
            act.wait_ge(s("cvec_zero"), 1)
            A(cvec[:, :, 0:2], vec[:, CVEC:CVEC + 16].rearrange("p (v k) -> p k v", v=2), ACT.Silu)\
                .then_inc(s("cvec_ready"), 1)

            def square(n, f, t, updates=0):
                if n:
                    act.wait_ge(read_dve, updates + f // 2 + 1)
                if f >= 2:
                    act.wait_ge(s("ss_mm"), KD * n + f - 1)
                A(n_sq[:, f % 2, 0:t], X[:, f, 0:t], ACT.Square).then_inc(s("sq_ready"), 1)

            for f in range(1, KD, 2):
                act.wait_ge(s("xT_done"), f + 1)
                A(X[:, f, :], acc[:, f % 4, :], ACT.Copy).then_inc(s("xT_act"), 1)
                act.wait_ge(s("xT_dve"), f // 2 + 1)
                square(0, f - 1, T)
                act.wait_ge(s("xT_act"), f // 2 + 1)
                square(0, f, T)

            def root(n, t):
                act.wait_ge(s("ss_mm"), KD * (n + 1))
                A(n_rt[:, 0:t], p5[:, 0:t], ACT.Sqrt, scale=1.0 / D, bias=epsc[:, 0:1]).then_inc(s("rt_ready"), 1)

            def norm(n, t, block):
                root(n, t)
                split(block)
                for f in range(KD):
                    act.wait_ge(s("h_ready"), KD * n + f + 1)
                    A(Hhi[:, f, 0:t], n_h[:, f % 4, 0:t], ACT.Copy).then_inc(s("h_hi"), 1)

            root(0, T)
            split(0)
            for f in range(KD):
                act.wait_ge(s("h_ready"), f + 1)
                A(Hhi[:, f, :], n_h[:, f % 4, :], ACT.Copy).then_inc(s("h_hi"), 1)

            nk = 0
            for n, (kind, _, _) in enumerate(blocksA):
                split(n + 1)
                lo = 2 * (n % 2)
                if kind in ("g", "k", "q"):
                    act.wait_ge(block_done, n + 1)
                if kind == "g":
                    A(sgate[:, 2 * n:2 * n + 2, :], acc[:, lo:lo + 2, :], ACT.Sigmoid).then_inc(read_act, 1)
                if kind in ("k", "q"):
                    if nk >= 2:
                        act.wait_ge(s("aux_done"), nk - 1)
                    if nk == 0:
                        act.wait_ge(s("h_lo"), KD)
                    step(A(sqA[:, nk % 2, :, :], acc[:, lo:lo + 2, :], ACT.Square))
                    g0 = AKG if kind == "k" else AQG
                    A(QK[:, 2 * nk:2 * nk + 2, :], acc[:, lo:lo + 2, :], ACT.Copy,
                      scale=vec[:, g0:g0 + 1]).then_inc(read_act, 1)
                    nk += 1
                if nk == 2 and kind == "q":
                    act.wait_ge(s("aux_done"), 1)
                    for h in range(A_KV):
                        A(krt[:, h, :], (p5, p7)[h][:, :], ACT.Sqrt, scale=1.0 / A_HD, bias=epsc[:, 0:1])\
                            .then_inc(s("krt_ready"), 1)
            act.wait_ge(s("qrow_T"), 1)
            A(qsc[:, :, :], p6[:, 0:64].rearrange("p (t h) -> p t h", t=TT), ACT.Sqrt, scale=1.0 / A_HD,
              bias=epsc[:, 0:1]).then_inc(s("qsc_root"), 1)

            def attention(layer, units, O_hi, tile_units, pr, prT, nk_of, qcol, sink=None, between=None):
                n0 = layer * 32

                def out_hi(tile):
                    act.wait_ge(s("pv_done"), n0 + tile_units * (tile + 1))
                    w = tile_units * P if layer == 0 else LAT
                    A(O_hi[:, tile, 0:w], po[tile % 2][:, 0:w], ACT.Copy).then_inc(s("o_hi"), 1)

                def exp(u):
                    n = n0 + u
                    act.wait_ge(s("nb_ready"), n + 1)
                    if u >= 3:
                        act.wait_ge(s("pT_done"), n - 2)
                    c0, nkt = nk_of(u)
                    A(pr[:, u % 3, c0 * P:T], sbank[u % 3][:, c0 * P:T], ACT.Exp, scale=qcol(u),
                      bias=sm[:, u % 3, 1:2], accum_out=sm[:, u % 3, 2:3]).then_inc(s("exp_done"), 1)
                    if sink is not None:
                        A(sm[:, u % 3, 3:4], sink(u), ACT.Exp, bias=sm[:, u % 3, 1:2]).then_inc(s("sink_done"), 1)

                exp(0)
                for u in range(units):
                    if u + 1 < units:
                        exp(u + 1)
                    copy_T(u, n0 + u, nk_of, prT)
                    if u % tile_units == 1 and u > tile_units:
                        out_hi(u // tile_units - 1)
                    if between is not None:
                        between(u)
                out_hi(units // tile_units - 1)

            def copy_T(u, n, nk_of, prT):
                act.wait_ge(s("pT_done"), n + 1)
                if u >= 2:
                    act.wait_ge(s("pv_done"), n - 1)
                w = nk_of(u)[1] * P
                A(prT[:, u % 2, 0:w], acc[:, 2 + u % 2, 0:w], ACT.Copy).then_inc(s("pT_copied"), 1)

            attention(0, 32, hid_hi, 4, prob, probT, lambda u: (0, 4) if u % 4 < 2 else (2, 2),
                      lambda u: qsc[:, u % 4, u // 4:u // 4 + 1])

            for i in range(BT):
                act.wait_ge(s("yc_ready"), i + 1)
                if i >= 2:
                    act.wait_ge(s("var_mm"), i - 1)
                A(yq[:, i % 2, :], yc[:, i, :], ACT.Square).then_inc(s("yq_ready"), 1)
            act.wait_ge(s("var_mm"), BT)
            A(l_rt[:, :], pmod[:, :], ACT.Sqrt, scale=1.0 / B_WIDTH, bias=epsc[:, 0:1]).then_inc(s("lrt_ready"), 1)
            for i in range(BT):
                act.wait_ge(s("yn_ready"), i + 1)
                if i >= 2:
                    act.wait_ge(s("mixA_lo"), i - 1)
                step(A(yz[:, i % 2, :], yc[:, i, :], ACT.Silu, scale=vec[:, CNG + i:CNG + i + 1],
                       bias=vec[:, CNB + i:CNB + i + 1]))
                A(hid_hi[:, 8 + i, :], yz[:, i % 2, :], ACT.Copy).then_inc(s("mixA_hi"), 1)

            def out_projection(w, n, t, updates, first=0):
                for q in range(8):
                    if q >= first:
                        split(w + q + 1)
                    if q in (3, 5, 7):
                        square(n, q - 3, t, updates)
                        square(n, q - 2, t, updates)
                square(n, 6, t, updates)
                square(n, 7, t, updates)

            out_projection(A_OUT, 1, T, after_A_in["dve"])
            norm(1, T, FF[0][1] + 1)

            def ffn(l, t):
                w = FF[l][1]
                for half, nt in enumerate(HALF):
                    def gate(w, q, it, pair, per):
                        act.wait_ge(block_done, at(w + q + 1, it, 4))
                        act.wait_ge(read_dve, at(FFN_READS[l][2 * half]["dve"] + pair, it, per))
                        A(f_gate[:, :, 0:t], acc[:, 0:2, 0:t], ACT.Silu).then_inc(read_act, 1)

                    def up(w, q, it, pair, per, hcol):
                        split(w + q + 1, it)
                        split(w + q + 2, it)
                        act.wait_ge(read_dve, at(FFN_READS[l][2 * half]["dve"] + pair + 1, it, per))
                        A(hcol, f_h[:, :, 0:t], ACT.Copy).then_inc(s("hid_hi_done"), 1)

                    n_in = nt // 4
                    with act.Fori(0, n_in) as it:
                        for p_ in range(2):
                            gate(w, 2 * p_, it, p_, 2)
                            up(w, 2 * p_ + 1, it, p_, 2, hid_hi[:, bass.ds(it * 4 + 2 * p_, 2), 0:t])
                    w += 4 * n_in
                    if nt % 4:
                        p_ = nt // 2 - 1
                        gate(w, 0, None, p_, 0)
                        up(w, 1, None, p_, 0, hid_hi[:, 2 * p_:2 * p_ + 2, 0:t])
                        w += 2
                    if half == 0:
                        with act.Fori(0, 2) as it:
                            for q in range(4):
                                split(w + q + 2, it)
                    elif l == 0:
                        out_projection(w, 2, t, FFN_READS[0][3]["dve"], 1)
                    else:
                        for q in range(1, 7):
                            split(w + q + 1)
                    w += 8

            ffn(0, T)

            norm(2, T, C_IN + 1)
            w = C_IN
            nq = 0

            def silu_xc(tiles_):
                for i in tiles_:
                    act.wait_ge(s("conv_C_dve") if i < 8 else s("conv_C_pool"), i + 1 if i < 8 else i - 7)
                    o = XC[:, i, :] if i < 10 else Cc[:, i - 10, :]
                    A(o, o, ACT.Silu).then_inc(s("xc_ready"), 1)

            def xs_copy(k):
                act.wait_ge(s("xsT_done"), k + 1)
                A(xs_half(k), XS_BANK[k][:, :].rearrange("p (b n) -> p b n", b=2), ACT.Copy).then_inc(s("xs_act"), 1)

            for n, (kind, _, _) in enumerate(blocksC):
                if n:
                    split(w + n + 1)
                lo = 2 * (n % 2)
                if n == 4:
                    act.wait_ge(s("dt_ready"), 1)
                    step(A(dts[:, 1, :], dts[:, 0, :], ACT.Abs))
                    step(A(dts[:, 1, :], dts[:, 1, :], ACT.Exp, scale=-1.0))
                    act.wait_ge(s("rows_loaded"), 64)
                    A(dts[:, 2, 0:32], ALOG, ACT.Exp).then_inc(s("spexp_ready"), 1)
                if n == 12:
                    silu_xc(range(8))
                    act.wait_ge(s("conv_C_pool"), 4)
                if n == 13:
                    silu_xc(range(8, XBC_T))
                    xs_copy(1)
                if n == 14:
                    xs_copy(3)
                if n == 15:
                    xs_copy(5)
                    xs_copy(7)
                act.wait_ge(block_done, w + n + 1)
                if kind == "x":
                    j = n - (n > 0)
                    if n == 0:
                        act.wait_ge(s("pads_C"), 2)
                    if j < 5:
                        for i in range(2):
                            ins = A(XB[:, 2 * j + i, :, 2:2 + LAT], acc[:, lo + i, :].rearrange("p (s t) -> p s t", s=2),
                                    ACT.Copy)
                            if i:
                                ins.then_inc(read_act, 1)
                            else:
                                step(ins)
                    else:
                        A(XB[:, 10:12, 0, 2:2 + LAT], acc[:, lo:lo + 2, 0:LAT], ACT.Copy).then_inc(read_act, 1)
                elif kind == "dt":
                    A(dtT[0:32, :], acc[0:32, lo, :], ACT.Copy).then_inc(read_act, 1)
                elif kind == "kv":
                    step(A(sqK, acc[:, lo, :].rearrange("p (s t) -> p s t", s=2), ACT.Square))
                    step(A(Kc[:, :], acc[:, lo, :], ACT.Copy, scale=vec[:, CKG:CKG + 1]))
                    A(vT[:, :], acc[:, lo + 1, :], ACT.Copy).then_inc(read_act, 1)
                elif kind == "q":
                    if nq >= 2:
                        act.wait_ge(s("aux_done"), 5 + nq)
                    step(A(sqQ[nq % 2], acc[:, lo:lo + 2, 0:LAT], ACT.Square))
                    A(Q[:, 2 * nq:2 * nq + 2, :], acc[:, lo:lo + 2, 0:LAT], ACT.Copy, scale=vec[:, CQG:CQG + 1])\
                        .then_inc(read_act, 1)
                    if nq == 0:
                        act.wait_ge(s("aux_done"), 6)
                        A(kroot, p5[:, :].rearrange("p (s t) -> p s t", s=2), ACT.Sqrt, scale=1.0 / C_HD, bias=epsc[:, 0:1])\
                            .then_inc(s("krt_ready"), 1)
                        act.wait_ge(s("vT_done"), 1)
                        A(Vc[:, :, :], pmod[:, :].rearrange("p (t n) -> p t n", t=TT), ACT.Copy).then_inc(s("v_ready"), 1)
                    if nq == 2:
                        act.wait_ge(s("cum_mm"), 1)
                        step(A(PL[:, :, :], pmod[:, 64:128].rearrange("p (n h) -> p n h", n=4), ACT.Copy))
                        A(EX[:, :, :], pmod[:, 0:192].rearrange("p (n h) -> p n h", n=12), ACT.Exp)\
                            .then_inc(s("ex_ready"), 1)
                    nq += 1
                elif kind == "z":
                    f = 2 * (n - 12)
                    A(Z[:, f:f + 2, :], acc[:, lo:lo + 2, 0:LAT], ACT.Silu).then_inc(read_act, 1)
            for k in range(4):
                act.wait_ge(s("xw_used"), (2, 2, 5, 5)[k])
                A(state[:, k // 2 * 2, k % 2, :], stbank[k // 2 * 4 + k % 2], ACT.Copy).then_inc(s("state_act"), 1)
            act.wait_ge(s("xw_used"), 6)

            def square_y(b):
                for f in (2 * b, 2 * b + 1):
                    act.wait_ge(s("yg_ready"), f + 1)
                    if f >= 2:
                        act.wait_ge(s("ssy_mm"), f - 1)
                    A(ysq[:, f % 2, :], XC[:, f, 0:LAT], ACT.Square).then_inc(s("ysq_ready"), 1)

            for k in range(16):
                act.wait_ge(s("seg_ready"), k + 1)
                A(seg[:, k % 4, :], seg[:, k % 4, :], ACT.Exp).then_inc(s("decay_ready"), 1)
                if k >= 4:
                    act.wait_ge(s("inter_mm"), k - 3)
                A(Cd[:, k % 4, :], RB[k % 3][:, :], ACT.Exp).then_inc(s("cexp_ready"), 1)
                if k % 4 == 1 and k > 4:
                    square_y(k // 4 - 1)
            square_y(3)
            act.wait_ge(s("qsc_copied"), 1)
            A(qsc[:, 0:LT, :], qsc[:, 0:LT, :], ACT.Sqrt, scale=1.0 / C_HD, bias=epsc[:, 0:1]).then_inc(s("qsc_root"), 1)
            act.wait_ge(s("ssy_mm"), KD)
            A(yrs[:, :], pmod[:, 0:LAT], ACT.Sqrt, scale=1.0 / S_INNER, bias=epsc[:, 0:1]).then_inc(s("yrt_ready"), 1)

            def gated_hi(u):
                if 2 <= u < 2 + KD:
                    act.wait_ge(s("yn_C"), u - 1)
                    A(mixC_hi[:, 8 + u - 2, :], yN[:, u % 2, :], ACT.Copy).then_inc(s("mixC_hi_done"), 1)

            attention(1, 32, mixC_hi, 4, probC, probTC, lambda u: (0, 4),
                      lambda u: qsc[:, (u // 2) % 2, 2 * (u // 4) + u % 2:2 * (u // 4) + u % 2 + 1],
                      lambda u: SINK[:, 2 * (u // 4) + u % 2:2 * (u // 4) + u % 2 + 1], gated_hi)
            out_projection(C_OUT, 3, LAT, after_C_in["dve"])
            norm(3, LAT, FF[1][1] + 1)
            ffn(1, LAT)
            for k in range(1, 4, 2):
                act.wait_ge(s("oT_done"), k + 1)
                A(otile[:, k // 2, 512:1024], acc[:, k % 4, :], ACT.Copy).then_inc(s("out_act"), 1)

        @block.vector
        def _(dve):
            step = Chain(dve, s("dve_step"))
            split = splitters(dve, "lo")
            V_ = nc.vector

            V_.memset(epsc[:, :], EPS).then_inc(s("cvec_zero"), 1)
            V_.memset(cvec[:, :, :], 0.0).then_inc(s("cvec_zero"), 1)
            dve.wait_ge(s("vec_T"), 1)
            V_.tensor_copy(vec[:, :], p7[:, 0:VEC_N]).then_inc(s("vec_ready"), 1)
            for f in range(0, KD, 2):
                dve.wait_ge(s("xT_done"), f + 1)
                V_.tensor_copy(X[:, f, :], acc[:, f % 4, :]).then_inc(s("xT_dve"), 1)

            GROUPS = [(l, j) for l in range(DEPTH) for j in range(3)]

            def mod_copy(n):
                dve.wait_ge(mod_used, KD * (n + 1))
                V_.tensor_copy(modc[:, :], pmod[:, :]).then_inc(s("modc_ready"), 1)

            def mod_final(n):
                l, j = GROUPS[n]
                dve.wait_ge(s("modT_done"), n + 1)
                for v in range(2):
                    src = pmod[:, :].rearrange("p (b g c) -> p g b c", b=4, g=4)[:, :, :, v]
                    b0 = MODB + 48 * l + 16 * j
                    step(V_.tensor_tensor(mod[:, l, 16 * j:16 * j + 16, v].rearrange("p (g b) -> p g b", g=4), src,
                                          vec[:, b0:b0 + 16].rearrange("p (g b) -> p g b", g=4), ALU.add))
                norm_of = {0: (2 * l, SC1, N1G), 2: (2 * l + 1, SC2, N2G)}.get(j)
                if norm_of:
                    k, sc, g0 = norm_of
                    for v in range(2):
                        step(V_.scalar_tensor_tensor(out=gain[:, k, :, v], in0=mod[:, l, sc:sc + KD, v], scalar=1.0,
                                                     in1=vec[:, g0 + KD * l:g0 + KD * (l + 1)], op0=ALU.add,
                                                     op1=ALU.mult))
                V_.memset(ysum[:, 0:1], 0.0).then_inc(s("mod_ready"), 1)

            def scaled(n, f, t, o):
                return V_.tensor_tensor(o, X[:, f, 0:t], n_rs[:, 0:t], ALU.mult)

            def modulated(n, f, t, src):
                l, sh = n // 2, (SH1, SH2)[n % 2]
                if f >= 4:
                    dve.wait_ge(s("h_lo"), KD * n + f - 3)
                for v in range(t // LAT):
                    ins = V_.tensor_scalar(n_h[:, f % 4, v * LAT:(v + 1) * LAT], src[:, v * LAT:(v + 1) * LAT],
                                           gain[:, n, f, v:v + 1], mod[:, l, sh + f, v:v + 1], ALU.mult, ALU.add)
                ins.then_inc(s("h_ready"), 1)

            def norm(n, t):
                dve.wait_ge(s("rt_ready"), n + 1)
                step(V_.reciprocal(n_rs[:, 0:t], n_rt[:, 0:t]))
                done = [step.mark(scaled(n, 0, t, n_t[:, 0, 0:t]))]
                for f in range(KD):
                    if f + 1 < KD:
                        if f >= 1:
                            dve.wait_ge(s("h_ready"), KD * n + f)
                        done.append(step.mark(scaled(n, f + 1, t, n_t[:, (f + 1) % 2, 0:t])))
                    step.need(done[f])
                    modulated(n, f, t, n_t[:, f % 2, 0:t])

            dve.wait_ge(s("rt_ready"), 1)
            step(V_.reciprocal(n_rs[:, :], n_rt[:, :]))
            for f in range(KD):
                ins = scaled(0, f, T, x_rms[:, f, :])
            x_scaled = step.mark(ins)
            mod_copy(0)
            mod_final(0)
            step.need(x_scaled)
            modulated(0, 0, T, x_rms[:, 0, :])
            modulated(0, 1, T, x_rms[:, 1, :])
            split(0)
            for f in range(2, KD + 2, 2):
                if f < KD:
                    modulated(0, f, T, x_rms[:, f, :])
                    modulated(0, f + 1, T, x_rms[:, f + 1, :])
                dve.wait_ge(s("h_hi"), f)
                V_.tensor_tensor(Hlo[:, f - 1, :], n_h[:, (f - 1) % 4, :], Hhi[:, f - 1, :].bitcast(F32),
                                 ALU.subtract).then_inc(s("h_lo_dve"), 1)

            def rope(out2, rot, tmp, cos, sin, n):
                step(V_.tensor_tensor(tmp, rot, sin, ALU.mult))
                step(V_.tensor_tensor(out2, out2, cos, ALU.mult))
                V_.tensor_tensor(out2, out2, tmp, ALU.add).then_inc(s("rope_done"), 1)

            def both(x):
                return x.unsqueeze(1).to_broadcast([P, 2, LAT])

            taps = [(tap, i) for tap in range(B_CONV) for i in range(BT - 1)]

            def conv_taps(count):
                for _ in range(min(count, len(taps))):
                    tap, i = taps.pop(0)
                    y = Y[:, i, :].rearrange("p (s t) -> p s t", s=2)
                    col = vec[:, DWW + tap * BT + i:DWW + tap * BT + i + 1]
                    if tap == 0:
                        ins = V_.tensor_scalar(y, U[:, i, :, 0:LAT], col, vec[:, DWB + i:DWB + i + 1], ALU.mult,
                                               ALU.add)
                    else:
                        dve.wait_ge(s("conv_dve"), (BT - 1) * (tap - 1) + i + 1)
                        ins = V_.scalar_tensor_tensor(out=y, in0=U[:, i, :, tap:tap + LAT], scalar=col, in1=y,
                                                      op0=ALU.mult, op1=ALU.add)
                    ins.then_inc(s("conv_dve"), 1)

            dve.wait_ge(s("pads_A"), 1)
            nk = 0
            for n, (kind, _, _) in enumerate(blocksA):
                split(n + 1)
                lo = 2 * (n % 2)
                if kind == "a":
                    i0 = 2 * (n - 2)
                    dve.wait_ge(block_done, n + 1)
                    dve.wait_ge(read_act, A_READS[n - 2][1])
                    for i in range(2):
                        ins = V_.tensor_tensor(U[:, i0 + i, :, B_CONV // 2:B_CONV // 2 + LAT],
                                               acc[:, lo + i, :].rearrange("p (s t) -> p s t", s=2),
                                               sgate[:, i0 + i, :].rearrange("p (s t) -> p s t", s=2), ALU.mult)
                    ins.then_inc(read_dve, 1)
                if kind == "v":
                    dve.wait_ge(block_done, n + 1)
                    V_.tensor_copy(V[:, :, :].rearrange("p (b t) n -> p b (t n)", b=2), acc[:, lo:lo + 2, :])\
                        .then_inc(read_dve, 1)
                if n == 4:
                    dve.wait_ge(read_dve, 2)
                if n >= 4:
                    conv_taps(8)
                if n >= 5 and n != 6:
                    dve.wait_ge(s("aux_done"), nk + 1)
                    rope(QK[:, 2 * nk:2 * nk + 2, 0:LAT], p6[:, :].rearrange("p (s t) -> p s t", s=2), ropeT[:, :, :],
                         both(cst("cosA")), both(cst("sinA")), nk)
                    nk += 1
                if n == 7:
                    for h in range(A_KV):
                        dve.wait_ge(s("krt_ready"), h + 1)
                        step(V_.reciprocal(krt[:, h, :], krt[:, h, :]))
                        V_.tensor_tensor(QK[:, h, :], QK[:, h, :], krt[:, h, :], ALU.mult).then_inc(s("k_scaled"), 1)
                        dve.wait_ge(s("k_scaled"), h + 1)
            mod_copy(1)
            dve.wait_ge(s("aux_done"), 5)
            rope(QK[:, 8:10, 0:LAT], p6[:, :].rearrange("p (s t) -> p s t", s=2), ropeT[:, :, :], both(cst("cosA")),
                 both(cst("sinA")), 4)
            V_.tensor_copy(qrow[0:16, :], p7[0:16, :]).then_inc(s("qrow_ready"), 1)
            dve.wait_ge(s("qsc_root"), 1)
            step(V_.reciprocal(qsc[:, :, :], qsc[:, :, :]))
            V_.tensor_scalar(qsc[:, :, :], qsc[:, :, :], A_HD ** -0.5, None, ALU.mult).then_inc(s("qsc_ready"), 1)
            dve.wait_ge(s("qsc_ready"), 1)
            mod_final(1)

            def attention(layer, O_hi, O_lo, pr, nk_of, qcol, sink=None, between=None):
                n0 = 32 * layer

                def exp_bias(u, n):
                    dve.wait_ge(s("s_done"), n0 + u + 1)
                    yield step.mark(V_.reduce_max(sm[:, u % 3, 0:1], sbank[u % 3][:, n * P:T], AX.X))
                    if sink is not None:
                        yield step.mark(V_.tensor_scalar(sm[:, u % 3, 5:6], sm[:, u % 3, 0:1], qcol(u), sink(u), ALU.mult,
                                                         ALU.max))
                        V_.tensor_scalar(sm[:, u % 3, 1:2], sm[:, u % 3, 5:6], -1.0, None, ALU.mult)\
                            .then_inc(s("nb_ready"), 1)
                    else:
                        V_.tensor_scalar(sm[:, u % 3, 1:2], sm[:, u % 3, 0:1], qcol(u), -1.0, ALU.mult, ALU.mult)\
                            .then_inc(s("nb_ready"), 1)

                def normalise(u, n):
                    dve.wait_ge(s("exp_done"), n0 + u + 1)
                    total = sm[:, u % 3, 2:3]
                    if sink is not None:
                        dve.wait_ge(s("sink_done"), u + 1)
                        yield step.mark(V_.tensor_tensor(sm[:, u % 3, 6:7], total, sm[:, u % 3, 3:4], ALU.add))
                        total = sm[:, u % 3, 6:7]
                    yield step.mark(V_.reciprocal(sm[:, u % 3, 4:5], total))
                    V_.tensor_scalar(pr[:, u % 3, n * P:T], pr[:, u % 3, n * P:T], sm[:, u % 3, 4:5], None, ALU.mult)\
                        .then_inc(s("p_norm"), 1)

                def by_turns(*chains):
                    ready = [(chain, None) for chain in chains]
                    while ready:
                        chain, count = ready.pop(0)
                        if count is not None:
                            step.need(count)
                        count = next(chain, None)
                        if count is not None:
                            ready.append((chain, count))

                def out_lo(tile):
                    dve.wait_ge(s("o_hi"), 8 * layer + tile + 1)
                    w = T if layer == 0 else LAT
                    V_.tensor_tensor(O_lo[:, tile, 0:w], po[tile % 2][:, 0:w], O_hi[:, tile, 0:w].bitcast(F32),
                                     ALU.subtract).then_inc(s("o_lo"), 1)

                c0 = lambda u: nk_of(u)[0]
                by_turns(exp_bias(0, c0(0)))
                by_turns(exp_bias(1, c0(1)))
                by_turns(normalise(0, c0(0)))
                for u in range(32):
                    if u + 2 < 32:
                        by_turns(exp_bias(u + 2, c0(u + 2)), normalise(u + 1, c0(u + 1)))
                    elif u + 1 < 32:
                        by_turns(normalise(u + 1, c0(u + 1)))
                    if layer == 0:
                        conv_taps(2)
                    if layer == 0 and u % 8 == 4:
                        mod_copy(2 + u // 8)
                    if layer == 0 and u % 8 == 6:
                        mod_final(2 + u // 8)
                    if u % 4 == 1 and u > 4:
                        out_lo(u // 4 - 1)
                    if between is not None:
                        between(u)
                out_lo(7)

            attention(0, hid_hi, hid_lo, prob, lambda u: (0, 4) if u % 4 < 2 else (2, 2),
                      lambda u: qsc[:, u % 4, u // 4:u // 4 + 1])

            dve.wait_ge(s("mu_mm"), 1)
            for i in range(BT):
                V_.scalar_tensor_tensor(out=yc[:, i, :], in0=p7[:, :], scalar=-1.0 / B_WIDTH, in1=Y[:, i, :],
                                        op0=ALU.mult, op1=ALU.add).then_inc(s("yc_ready"), 1)
            dve.wait_ge(s("lrt_ready"), 1)
            step(V_.reciprocal(l_rt[:, :], l_rt[:, :]))
            for i in range(BT):
                V_.tensor_tensor(yc[:, i, :], yc[:, i, :], l_rt[:, :], ALU.mult).then_inc(s("yn_ready"), 1)
            for i in range(BT):
                dve.wait_ge(s("mixA_hi"), i + 1)
                V_.tensor_tensor(hid_lo[:, 8 + i, :], yz[:, i % 2, :], hid_hi[:, 8 + i, :].bitcast(F32),
                                 ALU.subtract).then_inc(s("mixA_lo"), 1)

            def update(l, g0, pair, m, t, it=None):
                for i in range(2):
                    for v in range(t // LAT):
                        cols = slice(v * LAT, (v + 1) * LAT)
                        if it is None:
                            xs, gt = X[:, m + i, cols], mod[:, l, g0 + m + i, v:v + 1]
                        else:
                            xs = X[:, bass.ds(it * 4 + (m + i), 1), cols].rearrange("p a t -> p (a t)")
                            gt = mod[:, l, bass.ds(it * 4 + (g0 + m + i), 1), v:v + 1].rearrange("p a v -> p (a v)")
                        ins = V_.scalar_tensor_tensor(out=xs, in0=acc[:, 2 * pair + i, cols], scalar=gt, in1=xs,
                                                      op0=ALU.mult, op1=ALU.add)
                ins.then_inc(read_dve, 1)

            def out_projection(w, l, t):
                for n in range(8):
                    split(w + n + 1)
                    if n % 2:
                        dve.wait_ge(block_done, w + n + 1)
                        update(l, G1, (n // 2) % 2, 2 * (n // 2), t)

            out_projection(A_OUT, 0, T)
            norm(1, T)
            split(FF[0][1] + 1)

            def ffn(l, t):
                w = FF[l][1]
                hid = sum(HALF) // 2 * l
                for half, nt in enumerate(HALF):
                    R = FFN_READS[l][2 * half]

                    def up(w, q, it, pair, per, hi, lo):
                        split(w + q + 1, it)
                        dve.wait_ge(block_done, at(w + q + 1, it, 4))
                        dve.wait_ge(read_act, at(R["act"] + pair + 1, it, per))
                        V_.tensor_tensor(f_h[:, :, 0:t], acc[:, 2:4, 0:t], f_gate[:, :, 0:t], ALU.mult)\
                            .then_inc(read_dve, 1)
                        split(w + q + 2, it)
                        dve.wait_ge(s("hid_hi_done"), at(hid + pair + 1, it, per))
                        V_.tensor_tensor(lo, f_h[:, :, 0:t], hi.bitcast(F32), ALU.subtract).then_inc(s("hid_lo_done"), 1)
                        dve.wait_ge(s("hid_lo_done"), at(hid + pair + 1, it, per))

                    n_in = nt // 4
                    with dve.Fori(0, n_in) as it:
                        for p_ in range(2):
                            cols = bass.ds(it * 4 + 2 * p_, 2)
                            up(w, 2 * p_ + 1, it, p_, 2, hid_hi[:, cols, 0:t], hid_lo[:, cols, 0:t])
                    w += 4 * n_in
                    if nt % 4:
                        p_ = nt // 2 - 1
                        up(w, 1, None, p_, 0, hid_hi[:, 2 * p_:2 * p_ + 2, 0:t], hid_lo[:, 2 * p_:2 * p_ + 2, 0:t])
                        w += 2
                    hid += nt // 2
                    if half == 0:
                        with dve.Fori(0, 2) as it:
                            for q in range(4):
                                split(w + q + 2, it)
                                if q % 2:
                                    dve.wait_ge(block_done, at(w + q + 1, it, 4))
                                    update(l, G2, q // 2, 2 * (q // 2), t, it)
                    else:
                        for q in range(8):
                            if q and (l == 0 or q < 7):
                                split(w + q + 1)
                            if q % 2:
                                dve.wait_ge(block_done, w + q + 1)
                                update(l, G2, (q // 2) % 2, 2 * (q // 2), t)
                    w += 8

            ffn(0, T)

            def softplus():
                dve.wait_ge(s("spexp_ready"), 1)
                DTR, e, z2, q, tmp = dts[:, 0, :], dts[:, 1, :], dts[:, 4, :], dts[:, 5, :], dts[:, 3, :]
                step(V_.tensor_scalar(tmp, e, 2.0, None, ALU.add))
                step(V_.reciprocal(tmp, tmp))
                step(V_.tensor_tensor(e, e, tmp, ALU.mult))
                step(V_.tensor_tensor(z2, e, e, ALU.mult))
                step(V_.tensor_scalar(q, z2, 1.0 / 15, None, ALU.mult))
                for odd in (13, 11, 9, 7, 5, 3):
                    step(V_.scalar_tensor_tensor(out=q, in0=q, scalar=1.0 / odd, in1=z2, op0=ALU.add, op1=ALU.mult))
                step(V_.scalar_tensor_tensor(out=q, in0=q, scalar=1.0, in1=e, op0=ALU.add, op1=ALU.mult))
                step(V_.tensor_scalar(tmp, DTR, 0.0, None, ALU.max))
                step(V_.scalar_tensor_tensor(out=dt_, in0=q, scalar=2.0, in1=tmp, op0=ALU.mult, op1=ALU.add))
                by_tile = lambda x: x.rearrange("p (t h) -> p t h", t=TT)
                V_.scalar_tensor_tensor(out=by_tile(da), in0=by_tile(dt_), scalar=-1.0,
                                        in1=dts[:, 2, 0:32].unsqueeze(1).to_broadcast([P, TT, 32]), op0=ALU.mult,
                                        op1=ALU.mult).then_inc(s("da_ready"), 1)

            dt_of = lambda t, d: dts[:, 6, 32 * t + 16 * d:32 * t + 16 * d + 16]
            by_head = lambda x: x.rearrange("p b (h n) -> p b h n", n=S_HD)
            head_cols = lambda x: x.rearrange("p (b h) -> p b h", b=4).unsqueeze(3).to_broadcast([P, 4, 4, S_HD])
            SRC = ((2, 0, 0), (3, 0, 1), (0, 0, 10), (2, 1, 2), (3, 1, 3), (1, 1, 11))

            def xs_copy(k):
                dve.wait_ge(s("xsT_done"), k + 1)
                V_.tensor_copy(xs_half(k), XS_BANK[k][:, :].rearrange("p (b n) -> p b n", b=2)).then_inc(s("xs_dve"), 1)

            def btok_copy(k):
                dve.wait_ge(s("bT_done"), k + 1)
                t = XS_TILES[2 * k]
                V_.tensor_copy(Btok[:, t:t + 2, :], (p6, p5)[k][:, :].rearrange("p (t n) -> p t n", t=2))\
                    .then_inc(s("btok_ready"), 1)

            def xw(n):
                t = SRC[n][0]
                if n < 2:
                    dve.wait_ge(s("xs_act"), n + 1)
                    dve.wait_ge(s("xs_dve"), n + 1)
                else:
                    dve.wait_ge(s("xs_act"), 4)
                    dve.wait_ge(s("xs_dve"), 4)
                    dve.wait_ge(s("xw_used"), n - 1)
                V_.tensor_tensor(XW[:, n % 2, :].rearrange("p (b h n) -> p b h n", b=4, h=4), by_head(XS[t]),
                                 head_cols(DW[:, n, :]), ALU.mult).then_inc(s("xw_ready"), 1)

            norm(2, T)
            w = C_IN
            for n, (kind, _, _) in enumerate(blocksC):
                split(w + n + 1)
                if n == 13:
                    dve.wait_ge(s("aux_done"), 10)
                    V_.tensor_copy(qrowC, p7[0:16, 0:LAT]).then_inc(s("qrow_ready"), 1)
                    for e in range(2):
                        V_.tensor_copy(Dcol[64 * e:64 * e + 64, :],
                                       DSK[64 * e:64 * e + 64, :].rearrange("p (f e) -> p e f", e=2)[:, e, :])
                    dve.wait_ge(s("ex_ready"), 1)
                    for i, (t, d, k) in enumerate(SRC):
                        ins = V_.tensor_tensor(DW[:, i, :], dt_of(t, d), EX[:, k, :], ALU.mult)
                    step(ins)
                    xs_copy(0)
                if n == 14:
                    dve.wait_ge(s("qrow_T"), 2)
                    V_.tensor_copy(qsc[:, 0:LT, :], p6[:, 0:32].rearrange("p (t h) -> p t h", t=LT))\
                        .then_inc(s("qsc_copied"), 1)
                    xs_copy(2)
                    xs_copy(4)
                    xw(0)
                if n == 15:
                    xs_copy(6)
                    btok_copy(0)
                    xw(1)
                if n == 3:
                    dve.wait_ge(s("dtT_done"), 1)
                    dve.wait_ge(s("rows_loaded"), 64)
                    V_.tensor_tensor(dts[:, 0, :].rearrange("p (t h) -> p t h", t=TT),
                                     p7[:, 0:TT * 32].rearrange("p (t h) -> p t h", t=TT),
                                     DTB.unsqueeze(1).to_broadcast([P, TT, 32]), ALU.add).then_inc(s("dt_ready"), 1)
                if n == 6:
                    softplus()
                if n == 8:
                    dve.wait_ge(s("aux_done"), 6)
                    rope(Kc[:, 0:LAT], p6[:, 0:LAT], modc[:, 0:LAT], cst("cosC"), cst("sinC"), 5)
                    dve.wait_ge(s("krt_ready"), 3)
                    step(V_.reciprocal(kroot, kroot))
                    kv = Kc[:, :].rearrange("p (s t) -> p s t", s=2)
                    dve.wait_ge(s("rope_done"), 6)
                    step(V_.tensor_tensor(kv, kv, kroot, ALU.mult))
                    for g in range(2):
                        for e in range(2):
                            ins = V_.tensor_copy(K2[64 * e:64 * e + 64, g, :], Kc[64 * g:64 * g + 64, :])
                    ins.then_inc(s("k2_ready"), 1)
                if n in (1, 3, 4, 5):
                    j = (1, 3, 4, 5).index(n)
                    dve.wait_ge(read_act, C_READS[x_block(j)][1])
                    dve.wait_ge(s("pads_C"), 2)
                    for tap in range(S_CONV):
                        for i in (2 * j, 2 * j + 1):
                            o, src = conv_C(i)
                            if tap == 0:
                                ins = V_.tensor_scalar(o, src(0), cvw(0, i), vec[:, CVB + i:CVB + i + 1], ALU.mult,
                                                       ALU.add)
                            else:
                                ins = V_.scalar_tensor_tensor(out=o, in0=src(tap), scalar=cvw(tap, i), in1=o,
                                                              op0=ALU.mult, op1=ALU.add)
                            if tap == S_CONV - 1:
                                ins.then_inc(s("conv_C_dve"), 1)
                            else:
                                step(ins)
                if 9 <= n <= 12:
                    nq = n - 9
                    dve.wait_ge(s("aux_done"), 7 + nq)
                    rope(Q[:, 2 * nq:2 * nq + 2, :], p6[:, :].rearrange("p (s t) -> p s t", s=2), ropeC, both(cst("cosC")),
                         both(cst("sinC")), 6 + nq)
            dve.wait_ge(s("bT_done"), 2)
            btok_copy(1)
            dve.wait_ge(s("cb_mm"), 1)
            pcb = pmod[:, :].rearrange("p (n i) -> p n i", n=4)
            for d, tri in ((0, "upto"), (1, "from")):
                V_.tensor_tensor(CB[:, 4 * d:4 * d + 4, :], pcb, cst(tri).unsqueeze(1).to_broadcast([P, 4, P]),
                                 ALU.mult).then_inc(s("cb_ready"), 1)

            def xdt(c, d):
                V_.tensor_tensor(by_head(XDT[c][d]), by_head(XS[c]), head_cols(dt_of(c, d)), ALU.mult)\
                    .then_inc(s("xdt_ready"), 1)

            def join(k, used):
                dve.wait_ge(s("state_act"), 2 * k)
                dve.wait_ge(s("xw_used"), used)
                to, frm = state[:, 2 * k - 1, :, :], state[:, 2 * k - 2, :, :]
                step(V_.tensor_tensor(to.rearrange("p g (h n) -> p (g h) n", n=S_HD),
                                      frm.rearrange("p g (h n) -> p (g h) n", n=S_HD),
                                      EX[:, 7 + k, :].unsqueeze(2).to_broadcast([P, S_HEADS, S_HD]), ALU.mult))
                for g in range(2):
                    ins = V_.tensor_tensor(state[:, 2 * k - 1, g, :], state[:, 2 * k - 1, g, :],
                                           stbank[4 * k - 2 + g], ALU.add)
                ins.then_inc(s("state_dve"), 1)

            xw(2)
            xdt(0, 0)
            xw(3)
            xdt(1, 0)
            xw(4)
            join(1, 3)
            xw(5)
            xdt(1, 1)
            xdt(0, 1)
            join(2, 6)

            def segments(k):
                b, c, d = SEG[k]
                dve.wait_ge(s("R_mm"), k + 1)
                if k >= 4:
                    dve.wait_ge(s("intra_mm"), k - 3)
                for h in range(4):
                    col = PL[:, 2 * d + c, 4 * b + h:4 * b + h + 1]
                    ins = V_.tensor_scalar(seg[:, k % 4, h * P:(h + 1) * P], RB[k % 3][:, h * P:(h + 1) * P], col, 0.0,
                                           ALU.subtract, ALU.min)
                ins.then_inc(s("seg_ready"), 1)

            def gate_y(b):
                dve.wait_ge(s("intra_mm"), 4 * b + 4)
                dve.wait_ge(s("inter_mm"), 4 * b + 4)
                for i in range(2):
                    f = 2 * b + i
                    y = XC[:, f, 0:LAT]
                    step(V_.scalar_tensor_tensor(out=y, in0=y, scalar=Dcol[:, f:f + 1],
                                                 in1=acc[:, b, i * LAT:(i + 1) * LAT], op0=ALU.mult, op1=ALU.add))
                    V_.tensor_tensor(y, y, Z[:, f, :], ALU.mult).then_inc(s("yg_ready"), 1)

            segments(0)
            segments(1)
            for k in range(16):
                b, c, d = SEG[k]
                heads4 = lambda x: x.rearrange("p (h i) -> p h i", h=4)
                dve.wait_ge(s("decay_ready"), k + 1)
                sv = heads4(seg[:, k % 4, :])
                V_.tensor_tensor(sv, sv, CB[:, 4 * d + 2 * c + b // 2, :].unsqueeze(1).to_broadcast([P, 4, P]), ALU.mult)\
                    .then_inc(s("m_ready"), 1)
                if k % 2 == 0 or k == 15:
                    dve.wait_ge(s("cexp_ready"), k + 1)
                    decayed_C(V_, k).then_inc(s("cd_dve"), 1)
                if k + 2 < 16:
                    segments(k + 2)
                if k % 4 == 0 and k:
                    gate_y(k // 4 - 1)
            gate_y(3)
            dve.wait_ge(s("qsc_root"), 2)
            step(V_.reciprocal(qsc[:, 0:LT, :], qsc[:, 0:LT, :]))
            step(V_.tensor_scalar(qsc[:, 0:LT, :], qsc[:, 0:LT, :], C_HD ** -0.5, None, ALU.mult))

            def gated_norm(u):
                if u == 1:
                    dve.wait_ge(s("yrt_ready"), 1)
                    step(V_.reciprocal(yrs[:, :], yrs[:, :]))
                if 3 <= u < 3 + KD:
                    f = u - 3
                    dve.wait_ge(s("mixC_hi_done"), f + 1)
                    step(V_.tensor_tensor(mixC_lo[:, 8 + f, :], yN[:, f % 2, :], mixC_hi[:, 8 + f, :].bitcast(F32),
                                          ALU.subtract))
                if 1 <= u < 1 + KD:
                    f = u - 1
                    V_.scalar_tensor_tensor(out=yN[:, f % 2, :], in0=XC[:, f, 0:LAT], scalar=vec[:, GNG + f:GNG + f + 1],
                                            in1=yrs[:, :], op0=ALU.mult, op1=ALU.mult).then_inc(s("yn_C"), 1)
                    dve.wait_ge(s("yn_C"), u)

            attention(1, mixC_hi, mixC_lo, probC, lambda u: (0, 4),
                      lambda u: qsc[:, (u // 2) % 2, 2 * (u // 4) + u % 2:2 * (u // 4) + u % 2 + 1],
                      lambda u: SINK[:, 2 * (u // 4) + u % 2:2 * (u // 4) + u % 2 + 1], gated_norm)
            out_projection(C_OUT, 1, LAT)
            norm(3, LAT)
            split(FF[1][1] + 1)
            ffn(1, LAT)
            for c in range(LT):
                dve.wait_ge(s("oT_done"), 2 * c + 1)
                V_.tensor_copy(otile[:, c, 0:512], acc[:, 2 * c, :]).then_inc(s("out_dve"), 1)

        @block.tensor
        def _(pe):
            mm = nc.tensor.matmul
            ident = cst("ident")

            def T_(o, x, n=P):
                return nc.tensor.transpose(o, x, cst("ident", 0, n, 0, n))

            pe.wait_ge(s("const_loaded"), 16)
            pe.wait_ge(s("small_loaded"), 16 * SMALLS)
            T_(p7[:, 0:128], vrow[:, 0, :])
            T_(p7[:, 128:240], vrow[0:112, 1, :], 112)
            T_(p7[:, 240:364], vrow[0:124, 2, :], 124).then_inc(s("vec_T"), 1)
            pe.wait_ge(s("x_loaded"), 32)
            for f in range(KD):
                if f >= 4:
                    pe.wait_ge(s("xT_act") if f % 2 else s("xT_dve"), (f - 4) // 2 + 1)
                for t in range(TT):
                    ins = T_(acc[:, f % 4, t * P:(t + 1) * P], xin[:, t, f * P:(f + 1) * P])
                ins.then_inc(s("xT_done"), 1)

            def mod_unit(m):
                n, k = m // KD, m % KD
                r = m_raw[m]
                pe.wait_ge(raw_loaded[r % RAW_SLOTS], 16 * (r // RAW_SLOTS + 1))
                if m == 0:
                    pe.wait_ge(s("cvec_ready"), 1)
                if k == 0 and n:
                    pe.wait_ge(s("mod_ready"), n)
                for g in range(4):
                    ins = mm(pmod[32 * g:32 * g + 32, :], cvec[:, k, :], raw[:, r % RAW_SLOTS, g * 512:(g + 1) * 512],
                             start=(k == 0), stop=(k == KD - 1))
                ins.then_inc(mod_used, 1)

            def mod_T(n):
                pe.wait_ge(s("modc_ready"), n + 1)
                for b in range(4):
                    ins = T_(pmod[:, b * P:(b + 1) * P], modc[:, b * P:(b + 1) * P])
                ins.then_inc(s("modT_done"), 1)

            def sum_square(n, f, t):
                pe.wait_ge(s("sq_ready"), KD * n + f + 1)
                mm(p5[:, 0:t], cst("ones"), n_sq[:, f % 2, 0:t], start=(f == 0), stop=(f == KD - 1))\
                    .then_inc(s("ss_mm"), 1)

            for f in range(KD):
                sum_square(0, f, T)
            for m in range(KD):
                mod_unit(m)
            mod_T(0)

            def product(outs, hi, lo, rhs, kts, first=True, last=True, ready=None):
                order = [(m, j) for m in range(len(outs)) for j in range(kts)]
                if ready is not None:
                    order.sort(key=lambda mj: mj[1])
                for m, j in order:
                    if ready is not None and m == 0:
                        ready(j)
                    cols = slice(m * P, (m + 1) * P)
                    xh, xl = rhs(j)
                    mm(outs[m], hi[:, j, cols], xh, start=(first and j == 0), stop=False)
                    mm(outs[m], hi[:, j, cols], xl, start=False, stop=False)
                    ins = mm(outs[m], lo[:, j, cols], xh, start=False, stop=(last and j == kts - 1))
                return ins

            def token_product(o, hi, lo, tt, cols):
                for j in range(KD):
                    xh, xl = (h[:, j, tt * P:(tt + 1) * P] for h in (Hhi, Hlo))
                    mm(o, xh, hi[:, j, cols], start=(j == 0), stop=False)
                    mm(o, xl, hi[:, j, cols], start=False, stop=False)
                    ins = mm(o, xh, lo[:, j, cols], start=False, stop=(j == KD - 1))
                return ins

            def stream_in(n):
                return lambda j: pe.wait_ge(s("h_lo"), KD * n + j + 1)

            H = lambda t: (lambda j: (Hhi[:, j, 0:t], Hlo[:, j, 0:t]))

            def auxA(m):
                n = (4, 6, 7, 8, 9)[m]
                pe.wait_ge(read_act, A_READS[n][1])
                if m == 0:
                    mm(p5[:, :], cst("ones"), sqA[:, 0, 0, :], start=True, stop=True)
                    mm(p7[:, :], cst("ones"), sqA[:, 0, 1, :], start=True, stop=True)
                else:
                    if m == 1:
                        pe.wait_ge(s("krt_ready"), 2)
                    for i in range(2):
                        h = 2 * (m - 1) + i
                        mm(p7[0:16, :], cst("headA", 15 - h, 31 - h), sqA[:, m % 2, i, :], start=(h == 0),
                           stop=(h == A_HEADS - 1))
                    pe.wait_ge(s("rope_done"), m)
                for i in range(2):
                    ins = mm(p6[:, i * LAT:(i + 1) * LAT], cst("rotA"), QK[:, 2 * m + i, 0:LAT], start=True, stop=True)
                ins.then_inc(s("aux_done"), 1)

            for n, (kind, _, _) in enumerate(blocksA):
                lo = 2 * (n % 2)
                if n >= 2:
                    who, count = A_READS[n - 2]
                    pe.wait_ge(read_act if who == "act" else read_dve, count)
                pe.wait_ge(lo_split, n + 1)
                w_h, w_l = split_block(n, KD)
                if kind == "v":
                    for t in range(TT):
                        ins = token_product(acc[:, lo + t // 2, (t % 2) * BC:(t % 2 + 1) * BC], w_h, w_l, t, slice(0, BC))
                else:
                    ins = product([acc[:, lo + m, :] for m in range(2)], w_h, w_l, H(T), KD,
                                  ready=stream_in(0) if n == 0 else None)
                ins.then_inc(block_done, 1)
                if 1 <= n <= 8:
                    mod_unit(KD + n - 1)
                if n == 5:
                    auxA(0)
                if 7 <= n <= 9:
                    auxA(n - 6)
            auxA(4)
            pe.wait_ge(s("qrow_ready"), 1)
            pe.wait_ge(s("rope_done"), 5)
            for t in range(TT):
                ins = T_(p6[:, 16 * t:16 * t + 16], qrow[0:16, t * P:(t + 1) * P], 16)
            ins.then_inc(s("qrow_T"), 1)
            mod_T(1)
            pe.wait_ge(s("qsc_root"), 1)
            pe.wait_ge(s("k_scaled"), 2)

            def attention(layer, nk_of, scores, value, pr, prT, out_of):
                n0 = 32 * layer

                def S_(u):
                    if u >= 3:
                        pe.wait_ge(s("exp_done"), n0 + u - 2)
                    scores(u).then_inc(s("s_done"), 1)

                def turn(u):
                    pe.wait_ge(s("p_norm"), n0 + u + 1)
                    if u >= 2:
                        pe.wait_ge(s("pT_copied"), n0 + u - 1)
                    c0, nkt = nk_of(u)
                    for j in range(nkt):
                        ins = T_(acc[:, 2 + u % 2, j * P:(j + 1) * P], pr[:, u % 3, (c0 + j) * P:(c0 + j + 1) * P])
                    ins.then_inc(s("pT_done"), 1)

                def pv(u):
                    pe.wait_ge(s("pT_copied"), n0 + u + 1)
                    tile = u // 4
                    if u % 4 == 0 and tile >= 2:
                        pe.wait_ge(s("o_lo"), 8 * layer + tile - 1)
                    c0, nkt = nk_of(u)
                    for j in range(nkt):
                        ins = mm(out_of(u), value(u, c0 + j), prT[:, u % 2, j * P:(j + 1) * P], start=(j == 0),
                                 stop=(j == nkt - 1))
                    ins.then_inc(s("pv_done"), 1)

                S_(0)
                S_(1)
                for u in range(32):
                    if u + 2 < 32:
                        S_(u + 2)
                    turn(u)
                    if u:
                        pv(u - 1)
                    if layer == 0:
                        if u % 8 < 4:
                            for i in range(2):
                                mod_unit(KD * (2 + u // 8) + 2 * (u % 8) + i)
                        if u % 8 == 5:
                            mod_T(2 + u // 8)
                pv(31)

            def scoresA(u):
                h, t = u // 4, u % 4
                cols = slice(0, T) if t < LT else slice(LAT, T)
                return mm(sbank[u % 3][:, cols], QK[:, A_KV + h, t * P:(t + 1) * P], QK[:, h // 4, cols], start=True,
                          stop=True)

            attention(0, lambda u: (0, 4) if u % 4 < 2 else (2, 2), scoresA,
                      lambda u, j: V[:, j, (u // 16) * P:(u // 16 + 1) * P], prob, probT,
                      lambda u: po[(u // 4) % 2][:, (u % 4) * P:(u % 4 + 1) * P])

            pe.wait_ge(s("conv_dve"), B_CONV * (BT - 1))
            pe.wait_ge(s("conv_pool"), 1)
            for i in range(BT):
                ins = mm(p7[:, :], cst("ones"), Y[:, i, :], start=(i == 0), stop=(i == BT - 1))
            ins.then_inc(s("mu_mm"), 1)
            pe.wait_ge(s("mod_ready"), 6)
            for i in range(BT):
                pe.wait_ge(s("yq_ready"), i + 1)
                mm(pmod[:, :], cst("ones"), yq[:, i % 2, :], start=(i == 0), stop=(i == BT - 1)).then_inc(s("var_mm"), 1)

            def square_sums(n, q, t):
                if q in (3, 5, 7):
                    for f in range(q - 3, KD if q == 7 else q - 1):
                        sum_square(n, f, t)

            def out_projection(w, kt, hi, lo, t, reads0, waits, norm):
                for n in range(8):
                    pair = n // 2
                    for sem_, count in waits.get(n, ()):
                        pe.wait_ge(sem_, count)
                    if n % 2 == 0 and pair >= 2:
                        pe.wait_ge(read_dve, reads0 + pair - 1)
                    pe.wait_ge(lo_split, w + n + 1)
                    w_h, w_l = split_block(w + n, kt)
                    product([acc[:, 2 * (pair % 2) + m, 0:t] for m in range(2)], w_h, w_l,
                            lambda j: (hi[:, kt * (n % 2) + j, 0:t], lo[:, kt * (n % 2) + j, 0:t]), kt,
                            first=(n % 2 == 0), last=(n % 2 == 1)).then_inc(block_done, 1)
                    square_sums(norm, n, t)

            out_projection(A_OUT, 6, hid_hi, hid_lo, T, after_A_in["dve"],
                           {0: ((s("exp_done"), 32), (s("pT_copied"), 32), (s("o_lo"), 8)),
                            1: ((s("mixA_lo"), 4),)}, 1)

            def ffn(l, t):
                w = FF[l][1]
                hid = sum(HALF) // 2 * l
                first = [True]
                for half, nt in enumerate(HALF):
                    R, R2 = FFN_READS[l][2 * half], FFN_READS[l][2 * half + 1]
                    pe.wait_ge(read_act, R["act"])
                    pe.wait_ge(read_dve, R["dve"] - 1)

                    def up_or_gate(w, q, it, pair, per):
                        side = q % 2
                        pe.wait_ge(read_dve if side else read_act, at(R["dve" if side else "act"] + pair, it, per))
                        pe.wait_ge(lo_split, at(w + q + 1, it, 4))
                        w_h, w_l = split_block(w + q, KD)
                        product([acc[:, 2 * side + m, 0:t] for m in range(2)], w_h, w_l, H(t), KD,
                                ready=stream_in(2 * l + 1) if half == 0 and q == 0 else None).then_inc(block_done, 1)

                    n_in = nt // 4
                    with pe.Fori(0, n_in) as it:
                        for q in range(4):
                            up_or_gate(w, q, it, q // 2, 2)
                    w += 4 * n_in
                    for q in range(nt % 4):
                        up_or_gate(w, q, None, nt // 2 - 1, 0)
                    w += nt % 4
                    hid += nt // 2
                    pe.wait_ge(read_act, R2["act"])
                    kt = nt // 2

                    def out_block(w, q, it, per, pair_use):
                        if q == 0:
                            pe.wait_ge(s("hid_lo_done"), hid - nt // 2 + (kt + 1) // 2)
                        if q == 1:
                            pe.wait_ge(s("hid_lo_done"), hid)
                        if q % 2 == 0:
                            pe.wait_ge(read_dve, at(R2["dve"] + pair_use - 1, it, per))
                        pe.wait_ge(lo_split, at(w + q + 1, it, 2 * per))
                        w_h, w_l = split_block(w + q, kt)
                        product([acc[:, q // 2 % 2 * 2 + m, 0:t] for m in range(2)], w_h, w_l,
                                lambda j: (hid_hi[:, kt * (q % 2) + j, 0:t], hid_lo[:, kt * (q % 2) + j, 0:t]),
                                kt, first=(q % 2 == 0), last=(q % 2 == 1)).then_inc(block_done, 1)

                    if half == 0:
                        with pe.Fori(0, 2) as it:
                            for q in range(4):
                                out_block(w, q, it, 2, q // 2)
                    else:
                        for q in range(8):
                            out_block(w, q, None, 0, q // 2)
                            if l == 0:
                                square_sums(2, q, t)
                    w += 8

            ffn(0, T)

            def auxC(m):
                if m == 0:
                    pe.wait_ge(read_act, C_READS[7][1])
                    mm(p5[:, :], cst("pair"), sqK, start=True, stop=True)
                    mm(p6[:, 0:LAT], cst("rotC"), Kc[:, 0:LAT], start=True, stop=True).then_inc(s("aux_done"), 1)
                    return
                pe.wait_ge(read_act, C_READS[7 + m][1])
                for i in range(2):
                    tile = 2 * (m - 1) + i
                    mm(p7[0:16, 0:LAT], cst("headC", 15 - 2 * tile, 31 - 2 * tile), sqQ[(m - 1) % 2][:, i, :],
                       start=(tile == 0), stop=(tile == KD - 1))
                pe.wait_ge(s("rope_done"), 5 + m)
                for i in range(2):
                    ins = mm(p6[:, i * LAT:(i + 1) * LAT], cst("rotC"), Q[:, 2 * (m - 1) + i, :], start=True, stop=True)
                ins.then_inc(s("aux_done"), 1)

            def xs_turn(k):
                t = XS_TILES[k // 2]
                pe.wait_ge(s("xc_ready"), 4 * (k % 2) + 4)
                for b in range(4):
                    f = 4 * (k % 2) + b
                    ins = T_(XS_BANK[k][:, b * P:(b + 1) * P], XC[:, f, t * P:(t + 1) * P])
                ins.then_inc(s("xsT_done"), 1)

            def b_turn(k):
                pe.wait_ge(s("xc_ready"), XBC_T)
                for b in range(4):
                    t, g = XS_TILES[2 * k] + b // 2, b % 2
                    ins = T_((p6, p5)[k][:, b * P:(b + 1) * P], XC[:, 8 + g, t * P:(t + 1) * P])
                ins.then_inc(s("bT_done"), 1)

            w = C_IN
            pe.wait_ge(read_dve, FFN_READS[0][3]["dve"] + 4)
            for n, (kind, _, _) in enumerate(blocksC):
                lo = 2 * (n % 2)
                if n >= 2:
                    who, count = C_READS[n - 2]
                    pe.wait_ge(read_act if who == "act" else read_dve, count)
                pe.wait_ge(lo_split, w + n + 1)
                w_h, w_l = split_block(w + n, KD, 32 if kind == "dt" else BC)
                if kind == "dt":
                    for k in range(KD):
                        xh, xl = H(T)(k)
                        for p_, (wt, xt) in enumerate(((w_h, xh), (w_h, xl), (w_l, xh))):
                            ins = mm(acc[0:32, lo, :], wt[:, k, :], xt, start=(k == 0 and p_ == 0),
                                     stop=(k == KD - 1 and p_ == 2))
                else:
                    t = T if kind == "kv" or kind == "x" and n < 6 else LAT
                    ins = product([acc[:, lo + m, 0:t] for m in range(2)], w_h, w_l, H(t), KD,
                                  ready=stream_in(2) if n == 0 else None)
                ins.then_inc(block_done, 1)
                if n == 2:
                    pe.wait_ge(read_act, C_READS[1][1])
                    for t in range(TT):
                        ins = T_(p7[:, 32 * t:32 * t + 32], dtT[0:32, t * P:(t + 1) * P], 32)
                    ins.then_inc(s("dtT_done"), 1)
                if 8 <= n <= 12:
                    if n == 9:
                        pe.wait_ge(s("dt_ready"), 1)
                    auxC(n - 8)
                if n == 8:
                    for t in range(TT):
                        ins = T_(pmod[:, t * P:(t + 1) * P], vT[:, t * P:(t + 1) * P])
                    ins.then_inc(s("vT_done"), 1)
                if n == 9:
                    pe.wait_ge(s("da_ready"), 1)
                    pe.wait_ge(s("v_ready"), 1)
                    da_of = lambda t, d: dts[:, 7, 32 * t + 16 * d:32 * t + 16 * d + 16]
                    for k, parts in enumerate(CUM):
                        for i, (tri, t, d) in enumerate(parts):
                            ins = mm(pmod[:, 16 * k:16 * k + 16], cst(tri), da_of(t, d), start=(i == 0),
                                     stop=(i == len(parts) - 1))
                    ins.then_inc(s("cum_mm"), 1)
                if n == 12:
                    pe.wait_ge(s("krt_ready"), 3)
                    pe.wait_ge(s("ex_ready"), 1)
                    xs_turn(0)
                    xs_turn(1)
                if n == 13:
                    pe.wait_ge(s("qrow_ready"), 2)
                    pe.wait_ge(s("rope_done"), 10)
                    for t in range(LT):
                        ins = T_(p6[:, 16 * t:16 * t + 16], qrowC[:, t * P:(t + 1) * P], 16)
                    ins.then_inc(s("qrow_T"), 1)
                    pe.wait_ge(s("xs_dve"), 1)
                    xs_turn(2)
                    pe.wait_ge(s("xs_act"), 1)
                    xs_turn(3)
                    xs_turn(4)
                if n == 14:
                    pe.wait_ge(s("xs_dve"), 2)
                    xs_turn(5)
                    pe.wait_ge(s("xs_act"), 2)
                    xs_turn(6)
                    pe.wait_ge(s("xs_dve"), 3)
                    xs_turn(7)
                    pe.wait_ge(s("qsc_copied"), 1)
                    b_turn(0)

            pe.wait_ge(s("xs_act"), 3)
            b_turn(1)
            pe.wait_ge(s("xs_dve"), 4)
            for n in range(4):
                c, g = n // 2, n % 2
                ins = mm(pmod[:, n * P:(n + 1) * P], XC[:, 8 + g, c * P:(c + 1) * P], Cc[:, g, c * P:(c + 1) * P],
                         start=True, stop=True)
            ins.then_inc(s("cb_mm"), 1)
            pe.wait_ge(read_act, after_C_in["act"])
            pe.wait_ge(read_dve, after_C_in["dve"])
            pe.wait_ge(s("btok_ready"), 2)
            for n, (t, k, first, last) in enumerate(((2, 0, 1, 0), (3, 0, 0, 1), (0, 1, 1, 1), (2, 2, 1, 0), (3, 2, 0, 1),
                                                     (1, 3, 1, 1))):
                pe.wait_ge(s("xw_ready"), n + 1)
                if n == 5:
                    pe.wait_ge(s("cb_ready"), 2)
                    pe.wait_ge(s("xs_act"), 4)
                for g in range(2):
                    ins = mm(stbank[2 * k + g], Btok[:, t, g * P:(g + 1) * P], XW[:, n % 2, g * 512:(g + 1) * 512],
                             start=bool(first), stop=bool(last))
                ins.then_inc(s("xw_used"), 1)

            def decays(k):
                if k >= 3:
                    pe.wait_ge(s("cexp_ready"), k - 2)
                pe.wait_ge(s("rx_ready"), k + 1)
                mm(RB[k % 3][:, :], cst("ones"), rx[:, k % 4, :], start=True, stop=True).then_inc(s("R_mm"), 1)

            def sum_y(b):
                for f in (2 * b, 2 * b + 1):
                    pe.wait_ge(s("ysq_ready"), f + 1)
                    mm(pmod[:, 0:LAT], cst("ones"), ysq[:, f % 2, :], start=(f == 0), stop=(f == KD - 1))\
                        .then_inc(s("ssy_mm"), 1)

            pe.wait_ge(s("state_act"), 4)
            decays(0)
            decays(1)
            pe.wait_ge(s("state_dve"), 2)
            decays(2)
            for k in range(16):
                b, c, d = SEG[k]
                if k < 4:
                    pe.wait_ge(s("xdt_ready"), k + 1)
                st = SEG_STATE[(c, d)]
                outs = [acc[64 * (h % 2):64 * (h % 2) + 64, b, h // 2 * LAT + c * P:h // 2 * LAT + (c + 1) * P]
                        for h in range(4)]
                pe.wait_ge(s("m_ready"), k + 1)
                for h in range(4):
                    ins = mm(outs[h], XDT[c][d][:, b, h * S_HD:(h + 1) * S_HD], seg[:, k % 4, h * P:(h + 1) * P],
                             start=(k % 4 == 0 and h < 2), stop=False, skip_group_check=True)
                ins.then_inc(s("intra_mm"), 1)
                if k % 2 and k < 15:
                    pe.wait_ge(s("cd_pool"), k // 2 + 1)
                else:
                    pe.wait_ge(s("cd_dve"), (k + 1) // 2 + 1)
                for h in range(4):
                    hh = 4 * (b % 2) + h
                    ins = mm(outs[h], state[:, st, b // 2, hh * S_HD:(hh + 1) * S_HD], Cd[:, k % 4, h * P:(h + 1) * P],
                             start=False, stop=(k % 4 == 3), skip_group_check=True)
                ins.then_inc(s("inter_mm"), 1)
                if k + 3 < 16:
                    decays(k + 3)
                if k % 4 == 2 and k > 4:
                    sum_y(k // 4 - 1)
            sum_y(3)

            pe.wait_ge(s("k2_ready"), 1)
            pe.wait_ge(s("yg_ready"), KD)
            pe.wait_ge(s("cexp_ready"), 16)

            def scoresC(u):
                tile, t, e = u // 4, (u // 2) % 2, u % 2
                rows_ = slice(64 * e, 64 * e + 64)
                mm(sbank[u % 3], Q[rows_, tile, t * P:(t + 1) * P], K2[rows_, tile // 4, :], start=True, stop=False,
                   skip_group_check=True)
                o = 1 - t
                return mm(sbank[u % 3][:, o * P:(o + 1) * P], ident, cst("mask", t * P, (t + 1) * P), start=False,
                          stop=True, skip_group_check=True)

            attention(1, lambda u: (0, 4), scoresC, lambda u, j: Vc[:, j, (u // 16) * C_HD:(u // 16 + 1) * C_HD], probC,
                      probTC, lambda u: po[(u // 4) % 2][64 * (u % 2):64 * (u % 2) + 64,
                                                       ((u // 2) % 2) * P:((u // 2) % 2 + 1) * P])
            out_projection(C_OUT, 8, mixC_hi, mixC_lo, LAT, after_C_in["dve"],
                           {0: ((s("exp_done"), 64), (s("pT_copied"), 64), (s("o_lo"), 16))}, 3)
            ffn(1, LAT)
            pe.wait_ge(read_dve, FFN_READS[1][3]["dve"] + 4)
            for k in range(4):
                for b in range(4):
                    ins = T_(acc[:, k, b * P:(b + 1) * P], X[:, 4 * (k % 2) + b, (k // 2) * P:(k // 2 + 1) * P])
                ins.then_inc(s("oT_done"), 1)


SEG = [(b, c, d) for b in range(4) for c, d in ((0, 0), (1, 0), (1, 1), (0, 1))]
SEG_STATE = {(0, 0): 0, (1, 0): 1, (1, 1): 2, (0, 1): 3}
XS_TILES = (2, 3, 0, 1)
CUM = [
    (("after", 2, 0), ("ones", 3, 0)), (("after", 3, 0),),
    (("before", 2, 1),), (("before", 3, 1), ("ones", 2, 1)),
    (("upto", 0, 0),), (("upto", 1, 0),),
    (("from", 0, 1),), (("from", 1, 1),),
    (("ones", 0, 0),), (("ones", 1, 1),),
    (("after", 0, 0),), (("before", 1, 1),),
]
SMALLS = 18

INPUTS = ["x", "c", "ctx", "c_ctx", "mod_w", "mod_b", "norm1_g", "norm2_g", "ffn_w_in", "ffn_w_out", "ev_w_in",
          "ev_w_out", "ev_q_g", "ev_k_g", "ev_dw_w", "ev_dw_b", "ev_cn_g", "ev_cn_b", "od_w_in", "od_w_out",
          "od_q_g", "od_k_g", "od_sink", "od_conv_w", "od_conv_b", "od_dt_bias", "od_A_log", "od_D", "od_gnorm_g"]


def kernel(**inputs):
    import concourse.bacc as bacc
    from concourse.bass_utils import run_bass_kernel_spmd

    nc = bacc.Bacc("TRN2", target_bir_lowering=False, num_devices=1)
    arrays, aps = {}, {}
    for name in INPUTS + ["const"]:
        arr = constants() if name == "const" else np.ascontiguousarray(inputs[name])
        arrays[f"in_{name}"] = arr
        aps[name] = nc.dram_tensor(f"in_{name}", arr.shape, mybir.dt.from_np(arr.dtype), kind="ExternalInput").ap()
    out = nc.dram_tensor("out", (1, LAT, D), F32, kind="ExternalOutput").ap()
    build_trunk(nc, aps, out)
    r = run_bass_kernel_spmd(nc, [arrays], core_ids=[0])
    return r.results[0]["out"]
```

```python
import math
from contextlib import ExitStack

import numpy as np

import concourse.bass as bass
from concourse import mybir

F32 = mybir.dt.float32
F32R = mybir.dt.float32r
ALU = mybir.AluOpType
ACT = mybir.ActivationFunctionType
AX = mybir.AxisListType

P = 128
D = 1024
KD = D // P
LAT = 256
CTX = 256
T = LAT + CTX
TT = T // P
LT = LAT // P
DEPTH = 2
EPS = 1e-6
GRID_W = 64
THETA = 10000.0

A_HEADS, A_KV, A_HD = 8, 2, 128
B_WIDTH, B_CONV = 512, 31
BT = B_WIDTH // P
C_HEADS, C_HD, C_WINDOW = 16, 64, 128
S_HEADS, S_HD, S_STATE, S_GROUPS, S_CONV = 16, 64, 128, 2, 5
S_INNER = S_HEADS * S_HD
XBC_T = (S_INNER + 2 * S_GROUPS * S_STATE) // P
FFN = 2816
HALF = (12, 10)
BC = 256
RAW_SLOTS = 4
MOD_COLS = 2048
NEG = -1e30

CONST_COLS = {}


def _const_layout():
    at = 0
    for name, n in (("ident", P), ("ones", P), ("spread", TT * P), ("rotA", P), ("rotC", P), ("upto", P), ("from", P),
                    ("before", P), ("after", P), ("pair", P), ("headA", 32), ("headC", 32),
                    ("mask", 2 * P), ("cosA", LAT), ("sinA", LAT), ("cosC", LAT), ("sinC", LAT)):
        CONST_COLS[name] = (at, n)
        at += n
    return at


CONST_N = _const_layout()


def _rope(head_dim):
    rows = LAT // GRID_W
    row = np.repeat(np.arange(rows), GRID_W).astype(np.float32)
    col = np.tile(np.arange(GRID_W), rows).astype(np.float32)
    quarter = head_dim // 4
    inv = (np.float32(THETA) ** (-np.arange(quarter, dtype=np.float32) / np.float32(quarter))).astype(np.float32)
    ar, ac = row[:, None] * inv, col[:, None] * inv
    ang = np.concatenate([ar, ar, ac, ac], axis=-1)
    reps = P // head_dim
    return (np.tile(np.cos(ang).T.astype(np.float32), (reps, 1)),
            np.tile(np.sin(ang).T.astype(np.float32), (reps, 1)))


def _rot(head_dim):
    q = head_dim // 4
    m = np.zeros((P, P), np.float32)
    for o in range(P):
        if (o // q) % 2 == 0:
            m[o + q, o] = -1.0
        else:
            m[o - q, o] = 1.0
    return m


def constants():
    c = np.zeros((P, CONST_N), np.float32)
    k, i = np.arange(P)[:, None], np.arange(P)[None, :]

    def put(name, a):
        at, n = CONST_COLS[name]
        c[:, at:at + n] = a

    put("ident", np.eye(P))
    put("ones", 1.0)
    put("spread", np.concatenate([np.broadcast_to(k == 32 * g, (P, P)) for g in range(TT)], axis=1))
    put("rotA", _rot(A_HD))
    put("rotC", _rot(C_HD))
    put("upto", k <= i)
    put("from", k >= i)
    put("before", k < i)
    put("after", k > i)
    put("pair", (k // C_HD) == (i // C_HD))
    j = np.arange(32)[None, :]
    put("headA", np.broadcast_to(j == 15, (P, 32)))
    put("headC", ((j == 15) & (k < C_HD)) | ((j == 16) & (k >= C_HD)))
    put("mask", np.concatenate([np.where(i <= k, 0.0, NEG), np.where(i >= k, 0.0, NEG)], axis=1))
    for name, hd in (("A", A_HD), ("C", C_HD)):
        cos, sin = _rope(hd)
        put("cos" + name, cos)
        put("sin" + name, sin)
    return c


MODB, N1G, N2G = 0, 96, 112
DWB, CNG, CNB, CVB, GNG, CVEC, AQG, AKG, CQG, CKG, CVW = 128, 132, 136, 140, 152, 160, 176, 177, 178, 179, 180
DWW = 240
VEC_N = 364
SH1, SC1, G1, SH2, SC2, G2 = 0, 8, 16, 24, 32, 40


class Chain:

    def __init__(self, eng, sem):
        self.eng, self.sem, self.n = eng, sem, 0

    def mark(self, ins):
        ins.then_inc(self.sem, 1)
        self.n += 1
        return self.n

    def need(self, count):
        self.eng.wait_ge(self.sem, count)

    def __call__(self, ins):
        self.need(self.mark(ins))


def at(base, it=None, per=0):
    return base if it is None or per == 0 else it * per + base


def build_trunk(nc, a, out):
    with ExitStack() as ctx:
        def sem(name):
            return ctx.enter_context(nc.semaphore(name))

        def psum(name, shape):
            return ctx.enter_context(nc.psum_tensor(name, shape, F32))

        base = (nc.sbuf_base + 31) // 32 * 32
        room = nc.sbuf_usable_end - base - 32
        ctx.enter_context(nc.sbuf_tensor("arena", [P, room // 4], F32))
        place = [base]

        def region(size):
            start = place[0]
            place[0] += (size + 31) // 32 * 32
            assert place[0] <= base + room, (place[0], base + room)
            return start

        def view(name, shape, offset, dtype=F32):
            return nc.alloc_sbuf_tensor_at(name, [P] + list(shape), dtype, offset=offset)

        r_x, r_h, r_big = region(KD * T * 4), region(2 * KD * T * 4), region(2 * 12 * T * 4)
        r_raw, r_split = region(RAW_SLOTS * 8192), region(4 * 8192)
        r_const, r_misc = region(CONST_N * 4), region(29632)
        X = view("X", [KD, T], r_x)
        Hhi = view("Hhi", [KD, T], r_h, F32R)
        Hlo = view("Hlo", [KD, T], r_h + KD * T * 4, F32R)
        hid_hi = view("hid_hi", [12, T], r_big, F32R)
        hid_lo = view("hid_lo", [12, T], r_big + 12 * T * 4, F32R)
        mixC_hi = view("mixC_hi", [16, LAT], r_big, F32R)
        mixC_lo = view("mixC_lo", [16, LAT], r_big + 16 * LAT * 4, F32R)
        raw = view("raw", [RAW_SLOTS, 2048], r_raw)
        w_hi = view("w_hi", [2, 2048], r_split, F32R)
        w_lo = view("w_lo", [2, 2048], r_split + 16384, F32R)
        const = view("const", [CONST_N], r_const)
        modc = view("modc", [512], region(2048))
        vec = view("vec", [VEC_N], region(VEC_N * 4))
        cvec = view("cvec", [KD, 32], region(1024))
        mod = view("mod", [DEPTH, 48, 2], region(768))
        gain = view("gain", [4, KD, 2], region(256))
        rows = view("rows", [96], region(384))
        qsc = view("qsc", [TT, 16], region(256))
        sm = view("sm", [3, 8], region(96))
        ysum = view("ysum", [4], region(32))
        epsc = view("epsc", [1], region(32))
        DTB, ALOG, DSK, SINK = rows[:, 0:32], rows[:, 32:64], rows[:, 64:80], rows[:, 80:96]
        assert VEC_N == DWW + B_CONV * BT

        xin = view("xin", [TT, D], r_h)
        vrow = view("vrow", [3, P], r_big)
        x_rms = view("x_rms", [KD, T], r_h + KD * T * 4)
        n_h = view("n_h", [4, T], r_misc)
        n_sq = view("n_sq", [2, T], r_misc + 8192)
        n_rt = view("n_rt", [P], r_misc + 12288)
        n_rs = view("n_rs", [P], r_misc + 14336)
        n_t = view("n_t", [2, T], r_misc + 16384)
        QK = view("QK", [A_KV + A_HEADS, T], r_misc)
        U = view("U", [BT, 2, LAT + B_CONV - 1], r_misc + 20480)
        sgate = view("sgate", [BT, T], r_big)
        sqA = view("sqA", [2, 2, T], r_big + 8192)
        ptap = view("ptap", [T], r_big + 20480)
        Ypart = view("Ypart", [T], r_big + 22528)
        ropeT = view("ropeT", [2, LAT], r_big + 32768 - 2048)
        V = view("V", [TT, A_KV * A_HD], r_big + 8 * T * 4)
        Y = view("Y", [BT, T], r_big + 20 * T * 4)
        prob = view("prob", [3, T], r_h)
        probT = view("probT", [2, T], r_h + 6144)
        yc = view("yc", [BT, T], r_h + 10240)
        yq = view("yq", [2, T], r_h + 18432)
        l_rt = view("l_rt", [T], r_h + 22528)
        yz = view("yz", [2, T], r_h + 24576)
        qrow = view("qrow", [T], r_h + 28672)
        krt = view("krt", [2, T], r_big + 24576)
        Q = view("Q", [KD, LAT], r_misc)
        Kc = view("Kc", [T], r_misc + 8192)
        K2 = view("K2", [2, T], r_misc + 10240)
        Vc = view("Vc", [TT, 2 * C_HD], r_misc + 14336)
        Z = view("Z", [KD, LAT], r_misc + 16384)
        ptapC = view("ptapC", [2, LAT], r_misc + 16384)
        vT = view("vT", [T], r_misc + 18432)
        dtT = view("dtT", [T], r_misc + 20480)
        dts = view("dts", [8, TT * 32], r_misc + 24576)
        dt_, da = dts[:, 6, :], dts[:, 7, :]
        XB = view("XB", [XBC_T, 2, LAT + S_CONV - 1], r_big)
        r_xc = r_big + 24960
        XC = view("XC", [10, T], r_xc)
        Cc = view("Cc", [S_GROUPS, LAT], r_xc + 10 * T * 4)
        HF = view("HF", [2, KD, T], r_h)
        XS = [HF[:, t // 2, 4 * (t % 2):4 * (t % 2) + 4, LAT:T] for t in range(TT)]
        XDT = [[HF[:, c, 4 * d:4 * d + 4, 0:LAT] for d in range(2)] for c in range(LT)]
        state = view("state", [4, 2, 512], r_big)
        Btok = view("Btok", [TT, S_GROUPS * S_STATE], r_big + 12288)
        XW = view("XW", [2, S_INNER], r_big + 16384)
        Cd = view("Cd", [4, 512], r_big + 16384)
        Dcol = view("Dcol", [KD], region(32))
        ysq = view("ysq", [2, LAT], r_misc + 24576 + 512)
        yrs = view("yrs", [LAT], r_h + 26624)
        yN = view("yN", [2, LAT], r_h + 27648)
        EX = view("EX", [12, 16], r_xc + 22528)
        PL = view("PL", [4, 16], r_xc + 22528 + 768)
        DW = view("DW", [6, 16], r_xc + 22528 + 1024)
        CB = X[:, :, LAT:LAT + P]
        sqQ = [X[:, 2 * i:2 * i + 2, LAT:T] for i in range(2)]
        sqK = X[:, 4:6, LAT:T]
        kroot = X[:, 6:8, LAT:T]
        qrowC = X[0:16, 4, LAT:T]
        ropeC = modc[:, :].rearrange("p (s t) -> p s t", s=2)
        probC = view("probC", [3, T], r_h + 16384)
        probTC = view("probTC", [2, T], r_h + 22528)
        f_gate = view("f_gate", [2, T], r_misc)
        f_h = view("f_h", [2, T], r_misc + 4096)
        otile = view("otile", [LT, D], r_h)

        def cst(name, lo=0, hi=None, p0=0, p1=P):
            s, n = CONST_COLS[name]
            return const[p0:p1, s + lo:s + (n if hi is None else hi)]

        acc = psum("acc", [P, 4, 512])
        pmod = psum("pmod", [P, 512])
        p5 = psum("p5", [P, 512])
        p6 = psum("p6", [P, 512])
        p7 = psum("p7", [P, 512])
        sbank = [acc[:, 0, :], acc[:, 1, :], p7[:, :]]
        po = [p5, p6]
        stbank = [acc[:, 0, :], acc[:, 1, :], acc[:, 2, :], acc[:, 3, :], p5[:, :], p6[:, :], pmod[:, :], p7[:, :]]

        S = {}

        def s(name):
            if name not in S:
                S[name] = sem(name)
            return S[name]

        raw_loaded = [s(f"raw_loaded{i}") for i in range(RAW_SLOTS)]
        hi_split, lo_split, block_done = s("hi_split"), s("lo_split"), s("block_done")
        mod_used, read_act, read_dve = s("mod_used"), s("read_act"), s("read_dve")

        def tiles(w):
            return w.rearrange("(k p) n -> p k n", p=P)

        ev_in, ev_out = tiles(a["ev_w_in"][0]), tiles(a["ev_w_out"][0])
        od_in, od_out = tiles(a["od_w_in"][0]), tiles(a["od_w_out"][0])
        ffn_in = [tiles(a["ffn_w_in"][l]) for l in range(DEPTH)]
        ffn_out = [tiles(a["ffn_w_out"][l]) for l in range(DEPTH)]
        GLU_A, GLU_G = A_HEADS * A_HD + 2 * A_KV * A_HD, A_HEADS * A_HD + 2 * A_KV * A_HD + B_WIDTH
        blocksA = ([("g", ev_in, GLU_G + BC * i) for i in range(2)] + [("a", ev_in, GLU_A + BC * i) for i in range(2)]
                   + [("k", ev_in, A_HEADS * A_HD), ("v", ev_in, A_HEADS * A_HD + A_KV * A_HD)]
                   + [("q", ev_in, BC * i) for i in range(4)])
        C_Q = C_HEADS * C_HD
        C_X = C_Q + 4 * C_HD
        C_DT = C_X + XBC_T * P
        blocksC = ([("x", od_in, C_X), ("dt", od_in, C_DT)] + [("x", od_in, C_X + BC * i) for i in range(1, 6)]
                   + [("kv", od_in, C_Q)]
                   + [("q", od_in, BC * i) for i in range(4)] + [("z", od_in, C_DT + 32 + BC * i) for i in range(4)])
        stream = [("mod", 0, 0, k) for k in range(KD)]
        for n, (_, src, col) in enumerate(blocksA):
            stream.append(("w", src, 0, KD, col, BC))
            if 1 <= n <= 8:
                stream.append(("mod", 0, 1, n - 1))
        ev_out_blocks = [("w", ev_out, 6 * part, 6, BC * pair, BC) for pair, part in OUT_ORDER[0]]
        stream.append(ev_out_blocks[0])
        for l, j in ((0, 2), (1, 0)):
            stream += [("mod", l, j, k) for k in range(KD)]
        stream += ev_out_blocks[1:]
        FF = []
        NW = lambda: sum(i[0] == "w" for i in stream)

        def add_ffn(l):
            FF.append((len(stream), NW()))
            for half, nt in enumerate(HALF):
                t0 = sum(HALF[:half])
                for p_ in range(nt // 2):
                    for side in range(2):
                        stream.append(("w", ffn_in[l], 0, KD, side * FFN + P * t0 + BC * p_, BC))
                for m in range(4):
                    for part in range(2):
                        stream.append(("w", ffn_out[l], t0 + part * nt // 2, nt // 2, BC * m, BC))

        add_ffn(0)
        C_IN = NW()
        stream += [("w", src, 0, KD, col, 32 if kind == "dt" else BC) for kind, src, col in blocksC]
        C_OUT = NW()
        od_out_blocks = [("w", od_out, 8 * part, 8, BC * pair, BC) for pair, part in OUT_ORDER[1]]
        stream.append(od_out_blocks[0])
        for j in (1, 2):
            stream += [("mod", 1, j, k) for k in range(KD)]
        stream += od_out_blocks[1:]
        add_ffn(1)
        A_OUT = len(blocksA)
        idle = (C_OUT + 1) % 2 * 8192
        rx = view("rx", [4, 512], r_split + idle)
        seg = view("seg", [4, 512], r_split + 16384 + idle)
        w_raw = [r for r, i in enumerate(stream) if i[0] == "w"]
        m_raw = [r for r, i in enumerate(stream) if i[0] == "mod"]
        w_index = {r: n for n, r in enumerate(w_raw)}
        m_index = {r: n for n, r in enumerate(m_raw)}

        def raw_block(r, kt, cols=BC):
            return raw[:, r % RAW_SLOTS, 0:kt * cols].rearrange("p (k n) -> p k n", k=kt)

        def split_block(w, kt, cols=BC):
            return [x[:, w % 2, 0:kt * cols].rearrange("p (k n) -> p k n", k=kt) for x in (w_hi, w_lo)]

        block = ctx.enter_context(nc.Block())

        fold = lambda x: x.rearrange("l (f p) -> (l f) p", p=P)
        VECTORS = [
            (1, CVEC - 128, 8, fold(a["c"])), (1, CVEC - 120, 8, a["c_ctx"].rearrange("(f p) -> f p", p=P)),
            (1, DWB - 128, 4, fold(a["ev_dw_b"])), (1, CNG - 128, 4, fold(a["ev_cn_g"])),
            (1, CNB - 128, 4, fold(a["ev_cn_b"])), (1, CVB - 128, 12, fold(a["od_conv_b"])),
            (1, GNG - 128, 8, fold(a["od_gnorm_g"])), (1, AQG - 128, 1, a["ev_q_g"]), (1, AKG - 128, 1, a["ev_k_g"]),
            (1, CVW - 128, 60, a["od_conv_w"][0].rearrange("t (f p) -> (t f) p", p=P)),
            (0, MODB, 96, fold(a["mod_b"])), (0, N1G, 16, fold(a["norm1_g"])), (0, N2G, 16, fold(a["norm2_g"])),
            (2, 0, 124, a["ev_dw_w"][0].rearrange("t (f p) -> (t f) p", p=P)),
        ]

        def small_rows(eng, part):
            for slot, r0, n, src in VECTORS[part::2]:
                eng.dma_start(vrow[r0:r0 + n, slot, :], src).then_inc(s("small_loaded"), 16)
            r0, name = ((CQG, "od_q_g"), (CKG, "od_k_g"))[part]
            for half in range(2):
                eng.dma_start(vrow[r0 - 128:r0 - 127, 1, half * C_HD:(half + 1) * C_HD], a[name])\
                    .then_inc(s("small_loaded"), 16)

        @block.sync
        def _(sp):
            for t in range(0, TT, LT):
                src = (a["x"] if t < LT else a["ctx"])[0]
                sp.dma_start(xin[:, t:t + LT, :], src.rearrange("(t p) d -> p t d", p=P)).then_inc(s("x_loaded"), 16)
            small_rows(sp, 0)

            def free(r):
                if r < RAW_SLOTS:
                    return
                last = r - RAW_SLOTS
                if last in m_index:
                    sp.wait_ge(mod_used, m_index[last] + 1)
                else:
                    sp.wait_ge(lo_split, w_index[last] + 1)

            def load(r):
                item = stream[r]
                free(r)
                if item[0] == "mod":
                    _, l, j, k = item
                    sp.dma_start(raw[:, r % RAW_SLOTS, :],
                                 a["mod_w"][l, k * P:(k + 1) * P, j * MOD_COLS:(j + 1) * MOD_COLS])\
                        .then_inc(raw_loaded[r % RAW_SLOTS], 16)
                else:
                    _, src, k0, kt, col, cols = item
                    sp.dma_start(raw_block(r, kt, cols), src[:, k0:k0 + kt, col:col + cols])\
                        .then_inc(raw_loaded[r % RAW_SLOTS], 16)

            def load_loop(r, w, times, where):
                with sp.Fori(0, times) as it:
                    for q in range(4):
                        sp.wait_ge(lo_split, at(w + q - RAW_SLOTS + 1, it, 4))
                        src, kt = where(q, it)
                        sp.dma_start(raw_block(r + q, kt), src).then_inc(raw_loaded[(r + q) % RAW_SLOTS], 16)

            def load_ffn(l):
                r, w = FF[l]
                for half, nt in enumerate(HALF):
                    t0 = sum(HALF[:half])
                    n_in = nt // 4
                    load_loop(r, w, n_in, lambda q, it: (
                        ffn_in[l][:, :, bass.ds(it * (2 * BC) + ((q % 2) * FFN + P * t0 + BC * (q // 2)), BC)], KD))
                    r, w = r + 4 * n_in, w + 4 * n_in
                    for _ in range(nt % 4):
                        load(r)
                        r, w = r + 1, w + 1
                    load_loop(r, w, 2, lambda q, it: (
                        ffn_out[l][:, t0 + (q % 2) * nt // 2:t0 + (q % 2 + 1) * nt // 2,
                                   bass.ds(it * (2 * BC) + BC * (q // 2), BC)], nt // 2))
                    r, w = r + 8, w + 8
                return r

            for r in range(FF[0][0]):
                if r == KD + 2:
                    first = sum(CONST_COLS["spread"])
                    sp.dma_start(const[:, first:], a["const"][:, first:]).then_inc(s("tables_loaded"), 16)
                    for lo, n, src in ((0, 32, a["od_dt_bias"]), (32, 32, a["od_A_log"])):
                        sp.dma_start(rows[:, lo:lo + n], src.rearrange("l d h -> l (d h)").partition_broadcast(P)[:, 0, :])\
                            .then_inc(s("rows_loaded"), 16)
                    for lo, n, src in ((64, 16, a["od_D"]), (80, 16, a["od_sink"])):
                        sp.dma_start(rows[:, lo:lo + n], src.partition_broadcast(P)[:, 0, :])\
                            .then_inc(s("rows_loaded"), 16)
                load(r)
            r = load_ffn(0)
            while r < FF[1][0]:
                load(r)
                r += 1
            load_ffn(1)
            for half in range(2):
                for c in range(LT):
                    sp.wait_ge(*((s("out_first"), c + 1) if half == 0 else (s(f"out_ready{c}"), 1)))
                    cols = slice(512 * half, 512 * half + 512)
                    sp.dma_start(out[0, c * P:(c + 1) * P, cols], otile[:, c, cols]).then_inc(s("out_stored"), 16)
            sp.wait_ge(s("out_stored"), 16 * 2 * LT)

        def splitters(eng, kind):
            def split(w, it=None):
                r = w_raw[w]
                kt, cols = (8, BC) if it is not None else (stream[r][3], stream[r][5])
                n = kt * cols
                if kind == "hi":
                    eng.wait_ge(raw_loaded[r % RAW_SLOTS], at(16 * (r // RAW_SLOTS + 1), it, 16))
                    if w >= 2:
                        eng.wait_ge(block_done, at(w - 1, it, 4))
                    nc.scalar.activation(w_hi[:, w % 2, 0:n], raw[:, r % RAW_SLOTS, 0:n], ACT.Copy).then_inc(hi_split, 1)
                else:
                    eng.wait_ge(hi_split, at(w + 1, it, 4))
                    nc.vector.tensor_tensor(w_lo[:, w % 2, 0:n], raw[:, r % RAW_SLOTS, 0:n],
                                            w_hi[:, w % 2, 0:n].bitcast(F32), ALU.subtract).then_inc(lo_split, 1)
            return split

        def conv_C(i):
            if i < 10:
                return (XC[:, i, :].rearrange("p (s t) -> p s t", s=2), lambda tap: XB[:, i, :, tap:tap + LAT])
            return Cc[:, i - 10, :], lambda tap: XB[:, i, 0, tap:tap + LAT]

        XS_BANK = (p5, pmod, p5, pmod, p7, p5, pmod, p7)
        ROT_BANK = (p6, p5)
        OUT_BANK = ((p5, p6), (p7, pmod))
        RB = (p5, p6, p7)

        def xs_half(k):
            return XS[XS_TILES[k // 2]][:, 2 * (k % 2):2 * (k % 2) + 2, :]

        def decayed_C(eng, k):
            b, c, _ = SEG[k]
            cv = Cd[:, k % 4, :].rearrange("p (h i) -> p h i", h=4)
            return eng.tensor_tensor(cv, cv, Cc[:, b // 2, c * P:(c + 1) * P].unsqueeze(1).to_broadcast([P, 4, P]), ALU.mult)

        def x_block(j):
            return j + (j > 0)

        def cvw(tap, i):
            return vec[:, CVW + XBC_T * tap + i:CVW + XBC_T * tap + i + 1]


        reads = {"act": 0, "dve": 0}
        A_READS, C_READS = [], []
        for kind, _, _ in blocksA:
            who = {"g": "act", "a": "dve", "k": "act", "v": "dve", "q": "act"}[kind]
            reads[who] += 1
            A_READS.append((who, reads[who]))
        after_A_in = dict(reads)
        reads["dve"] += 4
        FFN_READS = []

        def ffn_reads():
            res = []
            for nt in HALF:
                res.append(dict(reads))
                reads["act"] += nt // 2
                reads["dve"] += nt // 2
                res.append(dict(reads))
                reads["dve"] += 4
            FFN_READS.append(res)

        ffn_reads()
        for kind, _, _ in blocksC:
            who = {"x": "act", "dt": "act", "kv": "act", "q": "act", "z": "act"}[kind]
            reads[who] += 1
            C_READS.append((who, reads[who]))
        after_C_in = dict(reads)
        reads["dve"] += 4
        ffn_reads()

        @block.gpsimd
        def _(pool):
            step = Chain(pool, s("pool_step"))
            nc.gpsimd.memset(U[:, :, :, :], 0.0).then_inc(s("pads_A"), 1)

            def norm_lo(n, t):
                for f in range(KD):
                    if n == 0 and f % 2:
                        pool.wait_ge(s("h_lo_dve"), f // 2 + 1)
                        nc.gpsimd.memset(ptap[:, f:f + 1], 0.0).then_inc(s("h_lo"), 1)
                        continue
                    pool.wait_ge(s("h_hi"), KD * n + f + 1)
                    nc.gpsimd.tensor_tensor(Hlo[:, f, 0:t], n_h[:, f % 4, 0:t], Hhi[:, f, 0:t].bitcast(F32),
                                            ALU.subtract).then_inc(s("h_lo"), 1)

            norm_lo(0, T)
            pool.wait_ge(read_dve, 2)
            pool.wait_ge(s("vec_ready"), 1)
            z = ptap[:, :].rearrange("p (s t) -> p s t", s=2)

            def conv_A(o, i, first, bias):
                y = o.rearrange("p (s t) -> p s t", s=2)
                for tap in range(first, B_CONV):
                    col = DWW + tap * BT + i
                    to = y if tap == first else z
                    step(nc.gpsimd.tensor_scalar(to, U[:, i, :, tap:tap + LAT], vec[:, col:col + 1],
                                                 bias if tap == first else 0.0, ALU.mult, ALU.add))
                    if tap > first:
                        step(nc.gpsimd.tensor_tensor(y, y, z, ALU.add))
                nc.gpsimd.memset(ptap[:, 0:1], 0.0).then_inc(s("conv_pool"), 1)

            conv_A(Y[:, BT - 1, :], BT - 1, 0, vec[:, DWB + BT - 1:DWB + BT])
            pool.wait_ge(s("conv_pool"), 1)
            conv_A(Ypart[:, :], BT - 2, POOL_TAPS, 0.0)
            norm_lo(1, T)
            norm_lo(2, T)
            pool.wait_ge(s("h_lo"), 3 * KD)
            nc.gpsimd.memset(XB[:, :, :, 0:2], 0.0).then_inc(s("pads_C"), 1)
            nc.gpsimd.memset(XB[:, :, :, 2 + LAT:4 + LAT], 0.0).then_inc(s("pads_C"), 1)
            pool.wait_ge(s("pads_C"), 2)
            for i in range(8, XBC_T):
                pool.wait_ge(read_act, C_READS[x_block(i // 2)][1])
                o, src = conv_C(i)
                z = ptapC[:, 0:2, :] if i < 10 else ptapC[:, 0, :]
                step(nc.gpsimd.tensor_scalar(o, src(0), cvw(0, i), vec[:, CVB + i:CVB + i + 1], ALU.mult, ALU.add))
                for tap in range(1, S_CONV):
                    step(nc.gpsimd.tensor_scalar(z, src(tap), cvw(tap, i), 0.0, ALU.mult, ALU.add))
                    ins = nc.gpsimd.tensor_tensor(o, o, z, ALU.add)
                    if tap < S_CONV - 1:
                        step(ins)
                ins.then_inc(s("conv_C_pool"), 1)
                pool.wait_ge(s("conv_C_pool"), i - 7)
            pool.wait_ge(block_done, C_OUT)
            pool.wait_ge(s("da_ready"), 1)
            for k, (b, c, d) in enumerate(SEG):
                if k >= 4:
                    pool.wait_ge(s("R_mm"), k - 3)
                at_ = 32 * c + 16 * d + 4 * b
                nc.gpsimd.tensor_tensor(rx[:, k % 4, :].rearrange("p (h i) -> p h i", h=4),
                                        cst(("upto", "from")[d]).unsqueeze(1).to_broadcast([P, 4, P]),
                                        dts[:, 7, at_:at_ + 4].unsqueeze(2).to_broadcast([P, 4, P]), ALU.mult)\
                    .then_inc(s("rx_ready"), 1)
                if k >= 4 and k % 2:
                    pool.wait_ge(s("cexp_ready"), k - 3)
                    decayed_C(nc.gpsimd, k - 4).then_inc(s("cd_pool"), 1)
            pool.wait_ge(s("cexp_ready"), 14)
            decayed_C(nc.gpsimd, 13).then_inc(s("cd_pool"), 1)
            norm_lo(3, LAT)

        @block.scalar
        def _(act):
            step = Chain(act, s("act_step"))
            split = splitters(act, "hi")
            A = nc.scalar.activation

            first = sum(CONST_COLS["spread"])
            act.dma_start(const[:, 0:first], a["const"][:, 0:first]).then_inc(s("const_loaded"), 16)
            small_rows(act, 1)

            act.wait_ge(s("vec_ready"), 1)
            act.wait_ge(s("cvec_zero"), 1)
            A(cvec[:, :, 0:2], vec[:, CVEC:CVEC + 16].rearrange("p (v k) -> p k v", v=2), ACT.Silu)\
                .then_inc(s("cvec_ready"), 1)

            def square(n, f, t, updates=0):
                if n:
                    act.wait_ge(read_dve, updates + f // 2 + 1)
                if f >= 2:
                    act.wait_ge(s("ss_mm"), KD * n + f - 1)
                A(n_sq[:, f % 2, 0:t], X[:, f, 0:t], ACT.Square).then_inc(s("sq_ready"), 1)

            for f in range(1, KD, 2):
                act.wait_ge(s("xT_done"), f + 1)
                A(X[:, f, :], acc[:, f % 4, :], ACT.Copy).then_inc(s("xT_act"), 1)
                act.wait_ge(s("xT_dve"), f // 2 + 1)
                square(0, f - 1, T)
                act.wait_ge(s("xT_act"), f // 2 + 1)
                square(0, f, T)

            def root(n, t):
                act.wait_ge(s("ss_mm"), KD * (n + 1))
                used = 32 * (t // P)
                A(n_rt[0:used, :], p5[0:used, 0:P], ACT.Sqrt, scale=1.0 / D, bias=epsc[0:used, 0:1])\
                    .then_inc(s("rt_ready"), 1)

            def norm(n, t, block):
                root(n, t)
                split(block)
                for f in range(KD):
                    act.wait_ge(s("h_ready"), KD * n + f + 1)
                    A(Hhi[:, f, 0:t], n_h[:, f % 4, 0:t], ACT.Copy).then_inc(s("h_hi"), 1)

            root(0, T)
            split(0)
            for f in range(KD):
                act.wait_ge(s("h_ready"), f + 1)
                A(Hhi[:, f, :], n_h[:, f % 4, :], ACT.Copy).then_inc(s("h_hi"), 1)

            nk = 0
            for n, (kind, _, _) in enumerate(blocksA):
                split(n + 1)
                lo = 2 * (n % 2)
                if kind in ("g", "k", "q"):
                    act.wait_ge(block_done, n + 1)
                if kind == "g":
                    A(sgate[:, 2 * n:2 * n + 2, :], acc[:, lo:lo + 2, :], ACT.Sigmoid).then_inc(read_act, 1)
                if kind in ("k", "q"):
                    if nk >= 2:
                        act.wait_ge(s("aux_done"), nk - 1)
                    if nk == 0:
                        act.wait_ge(s("h_lo"), KD)
                    step(A(sqA[:, nk % 2, :, :], acc[:, lo:lo + 2, :], ACT.Square))
                    g0 = AKG if kind == "k" else AQG
                    A(QK[:, 2 * nk:2 * nk + 2, :], acc[:, lo:lo + 2, :], ACT.Copy,
                      scale=vec[:, g0:g0 + 1]).then_inc(read_act, 1)
                    nk += 1
                if nk == 2 and kind == "q":
                    act.wait_ge(s("aux_done"), 1)
                    for h in range(A_KV):
                        A(krt[:, h, :], (p5, p7)[h][:, :], ACT.Sqrt, scale=1.0 / A_HD, bias=epsc[:, 0:1])\
                            .then_inc(s("krt_ready"), 1)
            act.wait_ge(s("qrow_T"), 1)
            A(qsc[:, :, :], p5[:, 0:64].rearrange("p (t h) -> p t h", t=TT), ACT.Sqrt, scale=1.0 / A_HD,
              bias=epsc[:, 0:1]).then_inc(s("qsc_root"), 1)

            def attention(layer, units, O_hi, tile_units, pr, prT, nk_of, qcol, at_end, sink=None, between=None):
                n0 = layer * 32

                def out_hi(tile):
                    act.wait_ge(s("pv_done"), n0 + tile_units * (tile + 1))
                    w = tile_units * P if layer == 0 else LAT
                    A(O_hi[:, tile, 0:w], po[tile % 2][:, 0:w], ACT.Copy).then_inc(s("o_hi"), 1)

                def exp(u):
                    n = n0 + u
                    act.wait_ge(s("nb_ready"), n + 1)
                    if u >= 3:
                        act.wait_ge(s("pT_done"), n - 2)
                    c0, nkt = nk_of(u)
                    A(pr[:, u % 3, c0 * P:T], sbank[u % 3][:, c0 * P:T], ACT.Exp, scale=qcol(u),
                      bias=sm[:, u % 3, 1:2], accum_out=sm[:, u % 3, 2:3]).then_inc(s("exp_done"), 1)
                    if sink is not None:
                        A(sm[:, u % 3, 3:4], sink(u), ACT.Exp, bias=sm[:, u % 3, 1:2]).then_inc(s("sink_done"), 1)

                exp(0)
                for u in range(units):
                    if u + 1 < units:
                        exp(u + 1)
                    copy_T(u, n0 + u, nk_of, prT)
                    if u % tile_units == 1 and u > tile_units:
                        out_hi(u // tile_units - 1)
                    if between is not None:
                        between(u)
                at_end()
                out_hi(units // tile_units - 1)

            def copy_T(u, n, nk_of, prT):
                act.wait_ge(s("pT_done"), n + 1)
                if u >= 2:
                    act.wait_ge(s("pv_done"), n - 1)
                w = nk_of(u)[1] * P
                A(prT[:, u % 2, 0:w], acc[:, 2 + u % 2, 0:w], ACT.Copy).then_inc(s("pT_copied"), 1)

            def conv_squares(u):
                for i in {22: (0, 1), 24: (2, 3)}.get(u, ()):
                    act.wait_ge(s("yc_ready"), i + 1)
                    if i >= 2:
                        act.wait_ge(s("var_mm"), i - 1)
                    A(yq[:, i % 2, :], yc[:, i, :], ACT.Square).then_inc(s("yq_ready"), 1)

            def conv_activation():
                split(A_OUT + 1)
                act.wait_ge(s("var_mm"), BT)
                A(l_rt[:, :], pmod[:, :], ACT.Sqrt, scale=1.0 / B_WIDTH, bias=epsc[:, 0:1]).then_inc(s("lrt_ready"), 1)
                for n, i in enumerate(CONV_ORDER):
                    act.wait_ge(s("yn_ready"), n + 1)
                    if n >= 2:
                        act.wait_ge(s("mixA_lo"), n - 1)
                        act.wait_ge(s("pv_done"), 32)
                    step(A(yz[:, i % 2, :], yc[:, i, :], ACT.Silu, scale=vec[:, CNG + i:CNG + i + 1],
                           bias=vec[:, CNB + i:CNB + i + 1]))
                    A(hid_hi[:, 8 + i, :], yz[:, i % 2, :], ACT.Copy).then_inc(s("mixA_hi"), 1)

            attention(0, 32, hid_hi, 4, prob, probT, lambda u: (0, 4) if u % 4 < 2 else (2, 2),
                      lambda u: qsc[:, u % 4, u // 4:u // 4 + 1], conv_activation, between=conv_squares)

            def out_projection(w, n, t, updates, first=0):
                for q in range(8):
                    if q >= first:
                        split(w + q + 1)
                    if q in (3, 5, 7):
                        square(n, q - 3, t, updates)
                        square(n, q - 2, t, updates)
                step(A(sm[:, 0, 7:8], epsc[:, 0:1], ACT.Sqrt))
                square(n, 6, t, updates)
                square(n, 7, t, updates)

            out_projection(A_OUT, 1, T, after_A_in["dve"], 1)
            norm(1, T, FF[0][1] + 1)

            def ffn(l, t):
                w = FF[l][1]
                for half, nt in enumerate(HALF):
                    def gate(w, q, it, pair, per):
                        split(w + q + 2, it)
                        act.wait_ge(block_done, at(w + q + 1, it, 4))
                        act.wait_ge(read_dve, at(FFN_READS[l][2 * half]["dve"] + pair, it, per))
                        A(f_gate[:, :, 0:t], acc[:, 0:2, 0:t], ACT.Silu).then_inc(read_act, 1)

                    def up(w, q, it, pair, per, hcol):
                        split(w + q + 2, it)
                        act.wait_ge(read_dve, at(FFN_READS[l][2 * half]["dve"] + pair + 1, it, per))
                        A(hcol, f_h[:, :, 0:t], ACT.Copy).then_inc(s("hid_hi_done"), 1)

                    n_in = nt // 4
                    with act.Fori(0, n_in) as it:
                        for p_ in range(2):
                            gate(w, 2 * p_, it, p_, 2)
                            up(w, 2 * p_ + 1, it, p_, 2, hid_hi[:, bass.ds(it * 4 + 2 * p_, 2), 0:t])
                    w += 4 * n_in
                    if nt % 4:
                        p_ = nt // 2 - 1
                        gate(w, 0, None, p_, 0)
                        up(w, 1, None, p_, 0, hid_hi[:, 2 * p_:2 * p_ + 2, 0:t])
                        w += 2
                    if half == 0:
                        with act.Fori(0, 2) as it:
                            for q in range(4):
                                split(w + q + 2, it)
                    elif l == 0:
                        out_projection(w, 2, t, FFN_READS[0][3]["dve"], 1)
                    else:
                        for q in range(1, 7):
                            split(w + q + 1)
                    w += 8

            ffn(0, T)

            norm(2, T, C_IN + 1)
            w = C_IN
            nq = 0

            def silu_xc(tiles_):
                for i in tiles_:
                    act.wait_ge(s("conv_C_dve") if i < 8 else s("conv_C_pool"), i + 1 if i < 8 else i - 7)
                    o = XC[:, i, :] if i < 10 else Cc[:, i - 10, :]
                    A(o, o, ACT.Silu).then_inc(s("xc_ready"), 1)

            def xs_copy(k):
                act.wait_ge(s("xsT_done"), k + 1)
                A(xs_half(k), XS_BANK[k][:, :].rearrange("p (b n) -> p b n", b=2), ACT.Copy).then_inc(s("xs_act"), 1)

            for n, (kind, _, _) in enumerate(blocksC):
                if n:
                    split(w + n + 1)
                lo = 2 * (n % 2)
                if n == 4:
                    act.wait_ge(s("dt_ready"), 1)
                    step(A(dts[:, 1, :], dts[:, 0, :], ACT.Abs))
                    step(A(dts[:, 1, :], dts[:, 1, :], ACT.Exp, scale=-1.0))
                    act.wait_ge(s("rows_loaded"), 64)
                    A(dts[:, 2, 0:32], ALOG, ACT.Exp).then_inc(s("spexp_ready"), 1)
                if n == 12:
                    silu_xc(range(8))
                    act.wait_ge(s("conv_C_pool"), 4)
                if n == 13:
                    silu_xc(range(8, XBC_T))
                    xs_copy(1)
                if n == 14:
                    xs_copy(3)
                if n == 15:
                    xs_copy(5)
                    xs_copy(7)
                act.wait_ge(block_done, w + n + 1)
                if kind == "x":
                    j = n - (n > 0)
                    if n == 0:
                        act.wait_ge(s("pads_C"), 2)
                    if j < 5:
                        for i in range(2):
                            ins = A(XB[:, 2 * j + i, :, 2:2 + LAT], acc[:, lo + i, :].rearrange("p (s t) -> p s t", s=2),
                                    ACT.Copy)
                            if i:
                                ins.then_inc(read_act, 1)
                            else:
                                step(ins)
                    else:
                        A(XB[:, 10:12, 0, 2:2 + LAT], acc[:, lo:lo + 2, 0:LAT], ACT.Copy).then_inc(read_act, 1)
                elif kind == "dt":
                    A(dtT[0:32, :], acc[0:32, lo, :], ACT.Copy).then_inc(read_act, 1)
                elif kind == "kv":
                    step(A(sqK, acc[:, lo, :].rearrange("p (s t) -> p s t", s=2), ACT.Square))
                    step(A(Kc[:, :], acc[:, lo, :], ACT.Copy, scale=vec[:, CKG:CKG + 1]))
                    A(vT[:, :], acc[:, lo + 1, :], ACT.Copy).then_inc(read_act, 1)
                elif kind == "q":
                    if nq >= 2:
                        act.wait_ge(s("aux_done"), 5 + nq)
                    step(A(sqQ[nq % 2], acc[:, lo:lo + 2, 0:LAT], ACT.Square))
                    A(Q[:, 2 * nq:2 * nq + 2, :], acc[:, lo:lo + 2, 0:LAT], ACT.Copy, scale=vec[:, CQG:CQG + 1])\
                        .then_inc(read_act, 1)
                    if nq == 0:
                        act.wait_ge(s("aux_done"), 6)
                        A(kroot, p5[:, :].rearrange("p (s t) -> p s t", s=2), ACT.Sqrt, scale=1.0 / C_HD, bias=epsc[:, 0:1])\
                            .then_inc(s("krt_ready"), 1)
                        act.wait_ge(s("vT_done"), 1)
                        A(Vc[:, :, :], pmod[:, :].rearrange("p (t n) -> p t n", t=TT), ACT.Copy).then_inc(s("v_ready"), 1)
                    if nq == 2:
                        act.wait_ge(s("cum_mm"), 1)
                        step(A(PL[:, :, :], pmod[:, 64:128].rearrange("p (n h) -> p n h", n=4), ACT.Copy))
                        A(EX[:, :, :], pmod[:, 0:192].rearrange("p (n h) -> p n h", n=12), ACT.Exp)\
                            .then_inc(s("ex_ready"), 1)
                    nq += 1
                elif kind == "z":
                    f = 2 * (n - 12)
                    A(Z[:, f:f + 2, :], acc[:, lo:lo + 2, 0:LAT], ACT.Silu).then_inc(read_act, 1)
            for k in range(4):
                act.wait_ge(s("xw_used"), (2, 2, 5, 5)[k])
                A(state[:, k // 2 * 2, k % 2, :], stbank[k // 2 * 4 + k % 2], ACT.Copy).then_inc(s("state_act"), 1)
            act.wait_ge(s("xw_used"), 6)

            def square_y(b):
                for f in (2 * b, 2 * b + 1):
                    act.wait_ge(s("yg_ready"), f + 1)
                    if f >= 2:
                        act.wait_ge(s("ssy_mm"), f - 1)
                    A(ysq[:, f % 2, :], XC[:, f, 0:LAT], ACT.Square).then_inc(s("ysq_ready"), 1)

            for k in range(16):
                act.wait_ge(s("seg_ready"), k + 1)
                A(seg[:, k % 4, :], seg[:, k % 4, :], ACT.Exp).then_inc(s("decay_ready"), 1)
                if k >= 4:
                    act.wait_ge(s("inter_mm"), k - 3)
                A(Cd[:, k % 4, :], RB[k % 3][:, :], ACT.Exp).then_inc(s("cexp_ready"), 1)
                if k % 4 == 1 and k > 4:
                    square_y(k // 4 - 1)
            square_y(3)
            act.wait_ge(s("qsc_copied"), 1)
            A(qsc[:, 0:LT, :], qsc[:, 0:LT, :], ACT.Sqrt, scale=1.0 / C_HD, bias=epsc[:, 0:1]).then_inc(s("qsc_root"), 1)
            act.wait_ge(s("ssy_mm"), KD)
            A(yrs[:, :], pmod[:, 0:LAT], ACT.Sqrt, scale=1.0 / S_INNER, bias=epsc[:, 0:1]).then_inc(s("yrt_ready"), 1)

            def gated_hi(u):
                if 2 <= u < 2 + KD:
                    act.wait_ge(s("yn_C"), u - 1)
                    A(mixC_hi[:, 8 + u - 2, :], yN[:, u % 2, :], ACT.Copy).then_inc(s("mixC_hi_done"), 1)

            attention(1, 32, mixC_hi, 4, probC, probTC, lambda u: (0, 4),
                      lambda u: qsc[:, (u // 2) % 2, 2 * (u // 4) + u % 2:2 * (u // 4) + u % 2 + 1],
                      lambda: split(C_OUT + 1), lambda u: SINK[:, 2 * (u // 4) + u % 2:2 * (u // 4) + u % 2 + 1],
                      gated_hi)
            out_projection(C_OUT, 3, LAT, after_C_in["dve"], 1)
            norm(3, LAT, FF[1][1] + 1)
            ffn(1, LAT)
            act.wait_ge(s("oT_done1"), 4 * LT)
            A(otile[:, 1, 512:1024], OUT_BANK[1][1][:, :], ACT.Copy).then_inc(s("out_ready1"), 1)

        @block.vector
        def _(dve):
            step = Chain(dve, s("dve_step"))
            split = splitters(dve, "lo")
            V_ = nc.vector

            V_.memset(epsc[:, :], EPS).then_inc(s("cvec_zero"), 1)
            V_.memset(cvec[:, :, :], 0.0).then_inc(s("cvec_zero"), 1)
            dve.wait_ge(s("vec_T"), 1)
            V_.tensor_copy(vec[:, :], p7[:, 0:VEC_N]).then_inc(s("vec_ready"), 1)
            for f in range(0, KD, 2):
                dve.wait_ge(s("xT_done"), f + 1)
                V_.tensor_copy(X[:, f, :], acc[:, f % 4, :]).then_inc(s("xT_dve"), 1)

            GROUPS = [(l, j) for l in range(DEPTH) for j in range(3)]

            def mod_copy(n):
                dve.wait_ge(mod_used, KD * (n + 1))
                V_.tensor_copy(modc[:, :], pmod[:, :]).then_inc(s("modc_ready"), 1)

            def mod_final(n):
                l, j = GROUPS[n]
                dve.wait_ge(s("modT_done"), n + 1)
                for v in range(2):
                    src = pmod[:, :].rearrange("p (b g c) -> p g b c", b=4, g=4)[:, :, :, v]
                    b0 = MODB + 48 * l + 16 * j
                    step(V_.tensor_tensor(mod[:, l, 16 * j:16 * j + 16, v].rearrange("p (g b) -> p g b", g=4), src,
                                          vec[:, b0:b0 + 16].rearrange("p (g b) -> p g b", g=4), ALU.add))
                norm_of = {0: (2 * l, SC1, N1G), 2: (2 * l + 1, SC2, N2G)}.get(j)
                if norm_of:
                    k, sc, g0 = norm_of
                    for v in range(2):
                        step(V_.scalar_tensor_tensor(out=gain[:, k, :, v], in0=mod[:, l, sc:sc + KD, v], scalar=1.0,
                                                     in1=vec[:, g0 + KD * l:g0 + KD * (l + 1)], op0=ALU.add,
                                                     op1=ALU.mult))
                V_.memset(ysum[:, 0:1], 0.0).then_inc(s("mod_ready"), 1)

            def scaled(f, t, o):
                return V_.tensor_tensor(o, X[:, f, 0:t], p6[:, 0:t], ALU.mult)

            def inverse_root(n, t):
                used = 32 * (t // P)
                dve.wait_ge(s("rt_ready"), n + 1)
                V_.reciprocal(n_rs[0:used, :], n_rt[0:used, :]).then_inc(s("rs_ready"), 1)
                dve.wait_ge(s("rs_spread"), n + 1)

            def modulated(n, f, t, src):
                l, sh = n // 2, (SH1, SH2)[n % 2]
                if f >= 4:
                    dve.wait_ge(s("h_lo"), KD * n + f - 3)
                for v in range(t // LAT):
                    ins = V_.tensor_scalar(n_h[:, f % 4, v * LAT:(v + 1) * LAT], src[:, v * LAT:(v + 1) * LAT],
                                           gain[:, n, f, v:v + 1], mod[:, l, sh + f, v:v + 1], ALU.mult, ALU.add)
                ins.then_inc(s("h_ready"), 1)

            def norm(n, t):
                inverse_root(n, t)
                done = [step.mark(scaled(0, t, n_t[:, 0, 0:t]))]
                for f in range(KD):
                    if f + 1 < KD and f:
                        dve.wait_ge(s("h_ready"), KD * n + f)
                        done.append(step.mark(scaled(f + 1, t, n_t[:, (f + 1) % 2, 0:t])))
                    step.need(done[f])
                    modulated(n, f, t, n_t[:, f % 2, 0:t])
                    if f == 0:
                        done.append(step.mark(scaled(1, t, n_t[:, 1, 0:t])))

            inverse_root(0, T)
            for f in range(KD):
                ins = scaled(f, T, x_rms[:, f, :])
            x_scaled = step.mark(ins)
            mod_copy(0)
            mod_final(0)
            step.need(x_scaled)
            modulated(0, 0, T, x_rms[:, 0, :])
            modulated(0, 1, T, x_rms[:, 1, :])
            split(0)
            for f in range(2, KD + 2, 2):
                if f < KD:
                    modulated(0, f, T, x_rms[:, f, :])
                    modulated(0, f + 1, T, x_rms[:, f + 1, :])
                dve.wait_ge(s("h_hi"), f)
                V_.tensor_tensor(Hlo[:, f - 1, :], n_h[:, (f - 1) % 4, :], Hhi[:, f - 1, :].bitcast(F32),
                                 ALU.subtract).then_inc(s("h_lo_dve"), 1)

            def rope(out2, rot, tmp, cos, sin):
                step(V_.tensor_tensor(tmp, rot, sin, ALU.mult))
                step(V_.tensor_tensor(out2, out2, cos, ALU.mult))
                V_.tensor_tensor(out2, out2, tmp, ALU.add).then_inc(s("rope_done"), 1)

            def both(x):
                return x.unsqueeze(1).to_broadcast([P, 2, LAT])

            taps = [(tap, i) for tap in range(B_CONV) for i in range(BT - 1) if i < BT - 2 or tap < POOL_TAPS]
            taps.append(("pool", BT - 2))
            tile_count, count = {}, [0]

            def conv_taps(n):
                for _ in range(min(n, len(taps))):
                    tap, i = taps.pop(0)
                    y = Y[:, i, :].rearrange("p (s t) -> p s t", s=2)
                    if i in tile_count:
                        dve.wait_ge(s("conv_dve"), tile_count[i])
                    if tap == "pool":
                        dve.wait_ge(s("conv_pool"), 2)
                        ins = V_.tensor_tensor(Y[:, i, :], Y[:, i, :], Ypart[:, :], ALU.add)
                    elif tap == 0:
                        ins = V_.tensor_scalar(y, U[:, i, :, 0:LAT], vec[:, DWW + i:DWW + i + 1],
                                               vec[:, DWB + i:DWB + i + 1], ALU.mult, ALU.add)
                    else:
                        col = vec[:, DWW + tap * BT + i:DWW + tap * BT + i + 1]
                        ins = V_.scalar_tensor_tensor(out=y, in0=U[:, i, :, tap:tap + LAT], scalar=col, in1=y,
                                                      op0=ALU.mult, op1=ALU.add)
                    ins.then_inc(s("conv_dve"), 1)
                    count[0] += 1
                    tile_count[i] = count[0]

            dve.wait_ge(s("pads_A"), 1)
            nk = 0
            for n, (kind, _, _) in enumerate(blocksA):
                split(n + 1)
                lo = 2 * (n % 2)
                if kind == "a":
                    i0 = 2 * (n - 2)
                    dve.wait_ge(block_done, n + 1)
                    dve.wait_ge(read_act, A_READS[n - 2][1])
                    for i in range(2):
                        ins = V_.tensor_tensor(U[:, i0 + i, :, B_CONV // 2:B_CONV // 2 + LAT],
                                               acc[:, lo + i, :].rearrange("p (s t) -> p s t", s=2),
                                               sgate[:, i0 + i, :].rearrange("p (s t) -> p s t", s=2), ALU.mult)
                    ins.then_inc(read_dve, 1)
                if kind == "v":
                    dve.wait_ge(block_done, n + 1)
                    V_.tensor_copy(V[:, :, :].rearrange("p (b t) n -> p b (t n)", b=2), acc[:, lo:lo + 2, :])\
                        .then_inc(read_dve, 1)
                if n == 4:
                    dve.wait_ge(read_dve, 2)
                if n >= 4:
                    conv_taps(8 if n < 9 else 3)
                if n == 5:
                    dve.wait_ge(s("tables_loaded"), 16)
                if n >= 5 and n != 6:
                    dve.wait_ge(s("aux_done"), nk + 1)
                    if nk:
                        dve.wait_ge(s("rope_done"), nk)
                    rope(QK[:, 2 * nk:2 * nk + 2, 0:LAT], ROT_BANK[nk % 2][:, :].rearrange("p (s t) -> p s t", s=2), ropeT[:, :, :],
                         both(cst("cosA")), both(cst("sinA")))
                    nk += 1
                if n == 7:
                    for h in range(A_KV):
                        dve.wait_ge(s("krt_ready"), h + 1)
                        step(V_.reciprocal(krt[:, h, :], krt[:, h, :]))
                        V_.tensor_tensor(QK[:, h, :], QK[:, h, :], krt[:, h, :], ALU.mult).then_inc(s("k_scaled"), 1)
                        dve.wait_ge(s("k_scaled"), h + 1)
            dve.wait_ge(s("aux_done"), 5)
            V_.tensor_copy(qrow[0:16, :], p7[0:16, :]).then_inc(s("qrow_ready"), 1)
            dve.wait_ge(s("rope_done"), 4)
            rope(QK[:, 8:10, 0:LAT], p6[:, :].rearrange("p (s t) -> p s t", s=2), ropeT[:, :, :], both(cst("cosA")),
                 both(cst("sinA")))
            mod_copy(1)
            dve.wait_ge(s("qsc_root"), 1)
            step(V_.reciprocal(qsc[:, :, :], qsc[:, :, :]))
            V_.tensor_scalar(qsc[:, :, :], qsc[:, :, :], A_HD ** -0.5, None, ALU.mult).then_inc(s("qsc_ready"), 1)
            dve.wait_ge(s("qsc_ready"), 1)
            mod_final(1)

            def attention(layer, O_hi, O_lo, pr, nk_of, qcol, at_end, sink=None, between=None):
                n0 = 32 * layer

                def softmax_step(v, u):
                    if v is not None:
                        dve.wait_ge(s("s_done"), n0 + v + 1)
                        top = step.mark(V_.reduce_max(sm[:, v % 3, 0:1], sbank[v % 3][:, nk_of(v)[0] * P:T], AX.X))
                    if u is not None:
                        dve.wait_ge(s("exp_done"), n0 + u + 1)
                        total = sm[:, u % 3, 2:3]
                        if sink is not None:
                            dve.wait_ge(s("sink_done"), u + 1)
                            total = sm[:, u % 3, 6:7]
                            summed = step.mark(V_.tensor_tensor(total, sm[:, u % 3, 2:3], sm[:, u % 3, 3:4], ALU.add))
                    if v is not None and sink is not None:
                        step.need(top)
                        top = step.mark(V_.tensor_scalar(sm[:, v % 3, 5:6], sm[:, v % 3, 0:1], qcol(v), sink(v), ALU.mult,
                                                         ALU.max))
                    if u is not None:
                        if sink is not None:
                            step.need(summed)
                        inverse = step.mark(V_.reciprocal(sm[:, u % 3, 4:5], total))
                    if v is not None:
                        step.need(top)
                        if sink is not None:
                            ins = V_.tensor_scalar(sm[:, v % 3, 1:2], sm[:, v % 3, 5:6], -1.0, None, ALU.mult)
                        else:
                            ins = V_.tensor_scalar(sm[:, v % 3, 1:2], sm[:, v % 3, 0:1], qcol(v), -1.0, ALU.mult, ALU.mult)
                        ins.then_inc(s("nb_ready"), 1)
                    if u is not None:
                        step.need(inverse)
                        p_ = pr[:, u % 3, nk_of(u)[0] * P:T]
                        V_.tensor_scalar(p_, p_, sm[:, u % 3, 4:5], None, ALU.mult).then_inc(s("p_norm"), 1)

                def out_lo(tile):
                    dve.wait_ge(s("o_hi"), 8 * layer + tile + 1)
                    w = T if layer == 0 else LAT
                    V_.tensor_tensor(O_lo[:, tile, 0:w], po[tile % 2][:, 0:w], O_hi[:, tile, 0:w].bitcast(F32),
                                     ALU.subtract).then_inc(s("o_lo"), 1)

                softmax_step(0, None)
                softmax_step(1, None)
                softmax_step(None, 0)
                for u in range(32):
                    softmax_step(u + 2 if u + 2 < 32 else None, u + 1 if u + 1 < 32 else None)
                    if u in MOD_TURN[layer]:
                        mod_copy(2 + 2 * layer + MOD_TURN[layer].index(u))
                    if u - 1 in MOD_TURN[layer]:
                        mod_final(2 + 2 * layer + MOD_TURN[layer].index(u - 1))
                    if layer == 0:
                        conv_taps(3 if u % 4 >= 2 else 2)
                    if u % 4 == 1 and u > 4:
                        out_lo(u // 4 - 1)
                    if between is not None:
                        between(u)
                at_end()
                out_lo(7)

            def conv_centre(u):
                for i in {21: (0, 1), 22: (2, 3)}.get(u, ()):
                    dve.wait_ge(s("mu_mm"), 1)
                    V_.scalar_tensor_tensor(out=yc[:, i, :], in0=pmod[:, :], scalar=-1.0 / B_WIDTH, in1=Y[:, i, :],
                                            op0=ALU.mult, op1=ALU.add).then_inc(s("yc_ready"), 1)

            def conv_norm():
                split(A_OUT + 1)
                dve.wait_ge(s("lrt_ready"), 1)
                step(V_.reciprocal(l_rt[:, :], l_rt[:, :]))
                for i in CONV_ORDER:
                    V_.tensor_tensor(yc[:, i, :], yc[:, i, :], l_rt[:, :], ALU.mult).then_inc(s("yn_ready"), 1)
                for n, i in enumerate(CONV_ORDER):
                    dve.wait_ge(s("mixA_hi"), n + 1)
                    V_.tensor_tensor(hid_lo[:, 8 + i, :], yz[:, i % 2, :], hid_hi[:, 8 + i, :].bitcast(F32),
                                     ALU.subtract).then_inc(s("mixA_lo"), 1)

            attention(0, hid_hi, hid_lo, prob, lambda u: (0, 4) if u % 4 < 2 else (2, 2),
                      lambda u: qsc[:, u % 4, u // 4:u // 4 + 1], conv_norm, between=conv_centre)

            def update(l, g0, pair, m, t, it=None):
                for i in range(2):
                    for v in range(t // LAT):
                        cols = slice(v * LAT, (v + 1) * LAT)
                        if it is None:
                            xs, gt = X[:, m + i, cols], mod[:, l, g0 + m + i, v:v + 1]
                        else:
                            xs = X[:, bass.ds(it * 4 + (m + i), 1), cols].rearrange("p a t -> p (a t)")
                            gt = mod[:, l, bass.ds(it * 4 + (g0 + m + i), 1), v:v + 1].rearrange("p a v -> p (a v)")
                        ins = V_.scalar_tensor_tensor(out=xs, in0=acc[:, 2 * pair + i, cols], scalar=gt, in1=xs,
                                                      op0=ALU.mult, op1=ALU.add)
                ins.then_inc(read_dve, 1)

            def out_projection(w, l, t, first=0):
                for n, (pair, _) in enumerate(OUT_ORDER[l]):
                    if n >= first:
                        split(w + n + 1)
                    if n in (2, 3, 5, 7):
                        dve.wait_ge(block_done, w + n + 1)
                        update(l, G1, pair % 2, 2 * pair, t)

            out_projection(A_OUT, 0, T, 1)
            norm(1, T)
            split(FF[0][1] + 1)

            def ffn(l, t):
                w = FF[l][1]
                hid = sum(HALF) // 2 * l
                for half, nt in enumerate(HALF):
                    R = FFN_READS[l][2 * half]

                    def up(w, q, it, pair, per, hi, lo):
                        split(w + q + 1, it)
                        dve.wait_ge(block_done, at(w + q + 1, it, 4))
                        dve.wait_ge(read_act, at(R["act"] + pair + 1, it, per))
                        V_.tensor_tensor(f_h[:, :, 0:t], acc[:, 2:4, 0:t], f_gate[:, :, 0:t], ALU.mult)\
                            .then_inc(read_dve, 1)
                        split(w + q + 2, it)
                        dve.wait_ge(s("hid_hi_done"), at(hid + pair + 1, it, per))
                        V_.tensor_tensor(lo, f_h[:, :, 0:t], hi.bitcast(F32), ALU.subtract).then_inc(s("hid_lo_done"), 1)
                        dve.wait_ge(s("hid_lo_done"), at(hid + pair + 1, it, per))

                    n_in = nt // 4
                    with dve.Fori(0, n_in) as it:
                        for p_ in range(2):
                            cols = bass.ds(it * 4 + 2 * p_, 2)
                            up(w, 2 * p_ + 1, it, p_, 2, hid_hi[:, cols, 0:t], hid_lo[:, cols, 0:t])
                    w += 4 * n_in
                    if nt % 4:
                        p_ = nt // 2 - 1
                        up(w, 1, None, p_, 0, hid_hi[:, 2 * p_:2 * p_ + 2, 0:t], hid_lo[:, 2 * p_:2 * p_ + 2, 0:t])
                        w += 2
                    hid += nt // 2
                    if half == 0:
                        with dve.Fori(0, 2) as it:
                            for q in range(4):
                                split(w + q + 2, it)
                                if q % 2:
                                    dve.wait_ge(block_done, at(w + q + 1, it, 4))
                                    update(l, G2, q // 2, 2 * (q // 2), t, it)
                    else:
                        for q in range(8):
                            if q and (l == 0 or q < 7):
                                split(w + q + 1)
                            if q % 2:
                                dve.wait_ge(block_done, w + q + 1)
                                update(l, G2, (q // 2) % 2, 2 * (q // 2), t)
                            if l == 1 and q == 6:
                                dve.wait_ge(s("oT_done0"), 4 * LT)
                                for c in range(LT):
                                    V_.tensor_copy(otile[:, c, 0:512], OUT_BANK[0][c][:, :])\
                                        .then_inc(s("out_first"), 1)
                    w += 8

            ffn(0, T)

            def softplus():
                dve.wait_ge(s("spexp_ready"), 1)
                DTR, e, z2, q, tmp = dts[:, 0, :], dts[:, 1, :], dts[:, 4, :], dts[:, 5, :], dts[:, 3, :]
                step(V_.tensor_scalar(tmp, e, 2.0, None, ALU.add))
                step(V_.reciprocal(tmp, tmp))
                step(V_.tensor_tensor(e, e, tmp, ALU.mult))
                step(V_.tensor_tensor(z2, e, e, ALU.mult))
                step(V_.tensor_scalar(q, z2, 1.0 / 15, None, ALU.mult))
                for odd in (13, 11, 9, 7, 5, 3):
                    step(V_.scalar_tensor_tensor(out=q, in0=q, scalar=1.0 / odd, in1=z2, op0=ALU.add, op1=ALU.mult))
                step(V_.scalar_tensor_tensor(out=q, in0=q, scalar=1.0, in1=e, op0=ALU.add, op1=ALU.mult))
                step(V_.tensor_scalar(tmp, DTR, 0.0, None, ALU.max))
                step(V_.scalar_tensor_tensor(out=dt_, in0=q, scalar=2.0, in1=tmp, op0=ALU.mult, op1=ALU.add))
                by_tile = lambda x: x.rearrange("p (t h) -> p t h", t=TT)
                V_.scalar_tensor_tensor(out=by_tile(da), in0=by_tile(dt_), scalar=-1.0,
                                        in1=dts[:, 2, 0:32].unsqueeze(1).to_broadcast([P, TT, 32]), op0=ALU.mult,
                                        op1=ALU.mult).then_inc(s("da_ready"), 1)

            dt_of = lambda t, d: dts[:, 6, 32 * t + 16 * d:32 * t + 16 * d + 16]
            by_head = lambda x: x.rearrange("p b (h n) -> p b h n", n=S_HD)
            head_cols = lambda x: x.rearrange("p (b h) -> p b h", b=4).unsqueeze(3).to_broadcast([P, 4, 4, S_HD])
            SRC = ((2, 0, 0), (3, 0, 1), (0, 0, 10), (2, 1, 2), (3, 1, 3), (1, 1, 11))

            def xs_copy(k):
                dve.wait_ge(s("xsT_done"), k + 1)
                V_.tensor_copy(xs_half(k), XS_BANK[k][:, :].rearrange("p (b n) -> p b n", b=2)).then_inc(s("xs_dve"), 1)

            def btok_copy(k):
                dve.wait_ge(s("bT_done"), k + 1)
                t = XS_TILES[2 * k]
                V_.tensor_copy(Btok[:, t:t + 2, :], (p6, p5)[k][:, :].rearrange("p (t n) -> p t n", t=2))\
                    .then_inc(s("btok_ready"), 1)

            def xw(n):
                t = SRC[n][0]
                if n < 2:
                    dve.wait_ge(s("xs_act"), n + 1)
                    dve.wait_ge(s("xs_dve"), n + 1)
                else:
                    dve.wait_ge(s("xs_act"), 4)
                    dve.wait_ge(s("xs_dve"), 4)
                    dve.wait_ge(s("xw_used"), n - 1)
                V_.tensor_tensor(XW[:, n % 2, :].rearrange("p (b h n) -> p b h n", b=4, h=4), by_head(XS[t]),
                                 head_cols(DW[:, n, :]), ALU.mult).then_inc(s("xw_ready"), 1)

            norm(2, T)
            w = C_IN
            for n, (kind, _, _) in enumerate(blocksC):
                split(w + n + 1)
                if n == 13:
                    dve.wait_ge(s("aux_done"), 10)
                    V_.tensor_copy(qrowC, p7[0:16, 0:LAT]).then_inc(s("qrow_ready"), 1)
                    for e in range(2):
                        V_.tensor_copy(Dcol[64 * e:64 * e + 64, :],
                                       DSK[64 * e:64 * e + 64, :].rearrange("p (f e) -> p e f", e=2)[:, e, :])
                    dve.wait_ge(s("ex_ready"), 1)
                    for i, (t, d, k) in enumerate(SRC):
                        ins = V_.tensor_tensor(DW[:, i, :], dt_of(t, d), EX[:, k, :], ALU.mult)
                    step(ins)
                    xs_copy(0)
                if n == 14:
                    dve.wait_ge(s("qrow_T"), 2)
                    V_.tensor_copy(qsc[:, 0:LT, :], p6[:, 0:32].rearrange("p (t h) -> p t h", t=LT))\
                        .then_inc(s("qsc_copied"), 1)
                    xs_copy(2)
                    xs_copy(4)
                    xw(0)
                if n == 15:
                    xs_copy(6)
                    btok_copy(0)
                    xw(1)
                if n == 3:
                    dve.wait_ge(s("dtT_done"), 1)
                    dve.wait_ge(s("rows_loaded"), 64)
                    V_.tensor_tensor(dts[:, 0, :].rearrange("p (t h) -> p t h", t=TT),
                                     p7[:, 0:TT * 32].rearrange("p (t h) -> p t h", t=TT),
                                     DTB.unsqueeze(1).to_broadcast([P, TT, 32]), ALU.add).then_inc(s("dt_ready"), 1)
                if n == 6:
                    softplus()
                if n == 8:
                    dve.wait_ge(s("aux_done"), 6)
                    rope(Kc[:, 0:LAT], p6[:, 0:LAT], modc[:, 0:LAT], cst("cosC"), cst("sinC"))
                    dve.wait_ge(s("krt_ready"), 3)
                    step(V_.reciprocal(kroot, kroot))
                    kv = Kc[:, :].rearrange("p (s t) -> p s t", s=2)
                    dve.wait_ge(s("rope_done"), 6)
                    step(V_.tensor_tensor(kv, kv, kroot, ALU.mult))
                    for g in range(2):
                        for e in range(2):
                            ins = V_.tensor_copy(K2[64 * e:64 * e + 64, g, :], Kc[64 * g:64 * g + 64, :])
                    ins.then_inc(s("k2_ready"), 1)
                if n in (1, 3, 4, 5):
                    j = (1, 3, 4, 5).index(n)
                    dve.wait_ge(read_act, C_READS[x_block(j)][1])
                    dve.wait_ge(s("pads_C"), 2)
                    for tap in range(S_CONV):
                        for i in (2 * j, 2 * j + 1):
                            o, src = conv_C(i)
                            if tap == 0:
                                ins = V_.tensor_scalar(o, src(0), cvw(0, i), vec[:, CVB + i:CVB + i + 1], ALU.mult,
                                                       ALU.add)
                            else:
                                ins = V_.scalar_tensor_tensor(out=o, in0=src(tap), scalar=cvw(tap, i), in1=o,
                                                              op0=ALU.mult, op1=ALU.add)
                            if tap == S_CONV - 1:
                                ins.then_inc(s("conv_C_dve"), 1)
                            else:
                                step(ins)
                if 9 <= n <= 12:
                    nq = n - 9
                    dve.wait_ge(s("aux_done"), 7 + nq)
                    rope(Q[:, 2 * nq:2 * nq + 2, :], p6[:, :].rearrange("p (s t) -> p s t", s=2), ropeC, both(cst("cosC")),
                         both(cst("sinC")))
            dve.wait_ge(s("bT_done"), 2)
            btok_copy(1)
            dve.wait_ge(s("cb_mm"), 1)
            pcb = pmod[:, :].rearrange("p (n i) -> p n i", n=4)
            for d, tri in ((0, "upto"), (1, "from")):
                V_.tensor_tensor(CB[:, 4 * d:4 * d + 4, :], pcb, cst(tri).unsqueeze(1).to_broadcast([P, 4, P]),
                                 ALU.mult).then_inc(s("cb_ready"), 1)

            def xdt(c, d):
                V_.tensor_tensor(by_head(XDT[c][d]), by_head(XS[c]), head_cols(dt_of(c, d)), ALU.mult)\
                    .then_inc(s("xdt_ready"), 1)

            def join(k, used):
                dve.wait_ge(s("state_act"), 2 * k)
                dve.wait_ge(s("xw_used"), used)
                to, frm = state[:, 2 * k - 1, :, :], state[:, 2 * k - 2, :, :]
                step(V_.tensor_tensor(to.rearrange("p g (h n) -> p (g h) n", n=S_HD),
                                      frm.rearrange("p g (h n) -> p (g h) n", n=S_HD),
                                      EX[:, 7 + k, :].unsqueeze(2).to_broadcast([P, S_HEADS, S_HD]), ALU.mult))
                for g in range(2):
                    ins = V_.tensor_tensor(state[:, 2 * k - 1, g, :], state[:, 2 * k - 1, g, :],
                                           stbank[4 * k - 2 + g], ALU.add)
                ins.then_inc(s("state_dve"), 1)

            xw(2)
            xdt(0, 0)
            xw(3)
            xdt(1, 0)
            xw(4)
            join(1, 3)
            xw(5)
            xdt(1, 1)
            xdt(0, 1)
            join(2, 6)

            def segments(k):
                b, c, d = SEG[k]
                dve.wait_ge(s("R_mm"), k + 1)
                if k >= 4:
                    dve.wait_ge(s("intra_mm"), k - 3)
                for h in range(4):
                    col = PL[:, 2 * d + c, 4 * b + h:4 * b + h + 1]
                    ins = V_.tensor_scalar(seg[:, k % 4, h * P:(h + 1) * P], RB[k % 3][:, h * P:(h + 1) * P], col, 0.0,
                                           ALU.subtract, ALU.min)
                ins.then_inc(s("seg_ready"), 1)

            def gate_y(b):
                dve.wait_ge(s("intra_mm"), 4 * b + 4)
                dve.wait_ge(s("inter_mm"), 4 * b + 4)
                for i in range(2):
                    f = 2 * b + i
                    y = XC[:, f, 0:LAT]
                    step(V_.scalar_tensor_tensor(out=y, in0=y, scalar=Dcol[:, f:f + 1],
                                                 in1=acc[:, b, i * LAT:(i + 1) * LAT], op0=ALU.mult, op1=ALU.add))
                    V_.tensor_tensor(y, y, Z[:, f, :], ALU.mult).then_inc(s("yg_ready"), 1)

            segments(0)
            segments(1)
            for k in range(16):
                b, c, d = SEG[k]
                heads4 = lambda x: x.rearrange("p (h i) -> p h i", h=4)
                dve.wait_ge(s("decay_ready"), k + 1)
                sv = heads4(seg[:, k % 4, :])
                V_.tensor_tensor(sv, sv, CB[:, 4 * d + 2 * c + b // 2, :].unsqueeze(1).to_broadcast([P, 4, P]), ALU.mult)\
                    .then_inc(s("m_ready"), 1)
                if k % 2 == 0 or k == 15:
                    dve.wait_ge(s("cexp_ready"), k + 1)
                    decayed_C(V_, k).then_inc(s("cd_dve"), 1)
                if k + 2 < 16:
                    segments(k + 2)
                if k % 4 == 0 and k:
                    gate_y(k // 4 - 1)
            gate_y(3)
            dve.wait_ge(s("qsc_root"), 2)
            step(V_.reciprocal(qsc[:, 0:LT, :], qsc[:, 0:LT, :]))
            step(V_.tensor_scalar(qsc[:, 0:LT, :], qsc[:, 0:LT, :], C_HD ** -0.5, None, ALU.mult))

            def gated_norm(u):
                if u == 1:
                    dve.wait_ge(s("yrt_ready"), 1)
                    step(V_.reciprocal(yrs[:, :], yrs[:, :]))
                if 3 <= u < 3 + KD:
                    f = u - 3
                    dve.wait_ge(s("mixC_hi_done"), f + 1)
                    V_.tensor_tensor(mixC_lo[:, 8 + f, :], yN[:, f % 2, :], mixC_hi[:, 8 + f, :].bitcast(F32),
                                     ALU.subtract).then_inc(s("mixC_lo_done"), 1)
                    dve.wait_ge(s("mixC_lo_done"), f + 1)
                if 1 <= u < 1 + KD:
                    f = u - 1
                    V_.scalar_tensor_tensor(out=yN[:, f % 2, :], in0=XC[:, f, 0:LAT], scalar=vec[:, GNG + f:GNG + f + 1],
                                            in1=yrs[:, :], op0=ALU.mult, op1=ALU.mult).then_inc(s("yn_C"), 1)
                    dve.wait_ge(s("yn_C"), u)

            attention(1, mixC_hi, mixC_lo, probC, lambda u: (0, 4),
                      lambda u: qsc[:, (u // 2) % 2, 2 * (u // 4) + u % 2:2 * (u // 4) + u % 2 + 1],
                      lambda: split(C_OUT + 1), lambda u: SINK[:, 2 * (u // 4) + u % 2:2 * (u // 4) + u % 2 + 1],
                      gated_norm)
            out_projection(C_OUT, 1, LAT, 1)
            norm(3, LAT)
            split(FF[1][1] + 1)
            ffn(1, LAT)
            dve.wait_ge(s("oT_done1"), 4 * LT)
            V_.tensor_copy(otile[:, 0, 512:1024], OUT_BANK[1][0][:, :]).then_inc(s("out_ready0"), 1)

        @block.tensor
        def _(pe):
            mm = nc.tensor.matmul
            ident = cst("ident")

            def T_(o, x, n=P):
                return nc.tensor.transpose(o, x, cst("ident", 0, n, 0, n))

            pe.wait_ge(s("const_loaded"), 16)
            pe.wait_ge(s("small_loaded"), 16 * (len(VECTORS) + 4))
            T_(p7[:, 0:128], vrow[:, 0, :])
            T_(p7[:, 128:240], vrow[0:112, 1, :], 112)
            T_(p7[:, 240:364], vrow[0:124, 2, :], 124).then_inc(s("vec_T"), 1)
            pe.wait_ge(s("x_loaded"), 32)
            for f in range(KD):
                if f >= 4:
                    pe.wait_ge(s("xT_act") if f % 2 else s("xT_dve"), (f - 4) // 2 + 1)
                for t in range(TT):
                    ins = T_(acc[:, f % 4, t * P:(t + 1) * P], xin[:, t, f * P:(f + 1) * P])
                ins.then_inc(s("xT_done"), 1)

            def mod_unit(m):
                n, k = m // KD, m % KD
                r = m_raw[m]
                pe.wait_ge(raw_loaded[r % RAW_SLOTS], 16 * (r // RAW_SLOTS + 1))
                if m == 0:
                    pe.wait_ge(s("cvec_ready"), 1)
                if k == 0 and n:
                    pe.wait_ge(s("mod_ready"), n)
                if k == 0 and n == 4:
                    pe.wait_ge(s("yrt_ready"), 1)
                for g in range(4):
                    ins = mm(pmod[32 * g:32 * g + 32, :], cvec[:, k, :], raw[:, r % RAW_SLOTS, g * 512:(g + 1) * 512],
                             start=(k == 0), stop=(k == KD - 1))
                ins.then_inc(mod_used, 1)

            def mod_T(n):
                pe.wait_ge(s("modc_ready"), n + 1)
                for b in range(4):
                    ins = T_(pmod[:, b * P:(b + 1) * P], modc[:, b * P:(b + 1) * P])
                ins.then_inc(s("modT_done"), 1)

            def sum_square(n, f, t):
                pe.wait_ge(s("sq_ready"), KD * n + f + 1)
                for g in range(t // P):
                    ins = mm(p5[32 * g:32 * g + 32, 0:P], cst("ones", 0, 32), n_sq[:, f % 2, g * P:(g + 1) * P],
                             start=(f == 0), stop=(f == KD - 1))
                ins.then_inc(s("ss_mm"), 1)

            def spread_roots(n, t):
                pe.wait_ge(s("rs_ready"), n + 1)
                for g in range(t // P):
                    ins = mm(p6[:, g * P:(g + 1) * P], cst("spread", g * P, (g + 1) * P, 0, 32 * (t // P)),
                             n_rs[0:32 * (t // P), :], start=True, stop=True)
                ins.then_inc(s("rs_spread"), 1)

            for f in range(KD):
                sum_square(0, f, T)
                if f in (1, 3, 5):
                    mod_unit(f // 2)
            for m in range(3, KD):
                mod_unit(m)
                if m == 4:
                    spread_roots(0, T)
            mod_T(0)

            def product(outs, hi, lo, rhs, kts, first=True, last=True, ready=None):
                order = [(m, j) for m in range(len(outs)) for j in range(kts)]
                if ready is not None:
                    order.sort(key=lambda mj: mj[1])
                for m, j in order:
                    if ready is not None and m == 0:
                        ready(j)
                    cols = slice(m * P, (m + 1) * P)
                    xh, xl = rhs(j)
                    mm(outs[m], hi[:, j, cols], xh, start=(first and j == 0), stop=False)
                    mm(outs[m], hi[:, j, cols], xl, start=False, stop=False)
                    ins = mm(outs[m], lo[:, j, cols], xh, start=False, stop=(last and j == kts - 1))
                return ins

            def token_product(o, hi, lo, tt, cols):
                for j in range(KD):
                    xh, xl = (h[:, j, tt * P:(tt + 1) * P] for h in (Hhi, Hlo))
                    mm(o, xh, hi[:, j, cols], start=(j == 0), stop=False)
                    mm(o, xl, hi[:, j, cols], start=False, stop=False)
                    ins = mm(o, xh, lo[:, j, cols], start=False, stop=(j == KD - 1))
                return ins

            def stream_in(n):
                return lambda j: pe.wait_ge(s("h_lo"), KD * n + j + 1)

            H = lambda t: (lambda j: (Hhi[:, j, 0:t], Hlo[:, j, 0:t]))

            def auxA(m):
                n = (4, 6, 7, 8, 9)[m]
                pe.wait_ge(read_act, A_READS[n][1])
                if m == 0:
                    mm(p5[:, :], cst("ones"), sqA[:, 0, 0, :], start=True, stop=True)
                    mm(p7[:, :], cst("ones"), sqA[:, 0, 1, :], start=True, stop=True)
                else:
                    if m == 1:
                        pe.wait_ge(s("krt_ready"), 2)
                    for i in range(2):
                        h = 2 * (m - 1) + i
                        mm(p7[0:16, :], cst("headA", 15 - h, 31 - h), sqA[:, m % 2, i, :], start=(h == 0),
                           stop=(h == A_HEADS - 1))
                if m >= 2:
                    pe.wait_ge(s("rope_done"), m - 1)
                for i in range(2):
                    ins = mm(ROT_BANK[m % 2][:, i * LAT:(i + 1) * LAT], cst("rotA"), QK[:, 2 * m + i, 0:LAT], start=True, stop=True)
                ins.then_inc(s("aux_done"), 1)

            for n, (kind, _, _) in enumerate(blocksA):
                lo = 2 * (n % 2)
                if n >= 2:
                    who, count = A_READS[n - 2]
                    pe.wait_ge(read_act if who == "act" else read_dve, count)
                pe.wait_ge(lo_split, n + 1)
                w_h, w_l = split_block(n, KD)
                if kind == "v":
                    for t in range(TT):
                        ins = token_product(acc[:, lo + t // 2, (t % 2) * BC:(t % 2 + 1) * BC], w_h, w_l, t, slice(0, BC))
                else:
                    ins = product([acc[:, lo + m, :] for m in range(2)], w_h, w_l, H(T), KD,
                                  ready=stream_in(0) if n == 0 else None)
                ins.then_inc(block_done, 1)
                if 1 <= n <= 8:
                    mod_unit(KD + n - 1)
                if n == 5:
                    pe.wait_ge(s("tables_loaded"), 16)
                    auxA(0)
                if 7 <= n <= 9:
                    auxA(n - 6)
            auxA(4)
            pe.wait_ge(s("qrow_ready"), 1)
            pe.wait_ge(s("rope_done"), 4)
            for t in range(TT):
                ins = T_(p5[:, 16 * t:16 * t + 16], qrow[0:16, t * P:(t + 1) * P], 16)
            ins.then_inc(s("qrow_T"), 1)
            mod_T(1)
            pe.wait_ge(s("qsc_root"), 1)
            pe.wait_ge(s("k_scaled"), 2)
            pe.wait_ge(s("rope_done"), 5)

            def conv_sums(u):
                if u == 20:
                    pe.wait_ge(s("conv_dve"), CONV_DVE)
                    pe.wait_ge(s("conv_pool"), 1)
                    pe.wait_ge(s("mod_ready"), 4)
                    for i in range(BT):
                        ins = mm(pmod[:, :], cst("ones"), Y[:, i, :], start=(i == 0), stop=(i == BT - 1))
                    ins.then_inc(s("mu_mm"), 1)
                for i in {23: (0, 1), 25: (2, 3)}.get(u, ()):
                    pe.wait_ge(s("yc_ready"), BT)
                    pe.wait_ge(s("yq_ready"), i + 1)
                    mm(pmod[:, :], cst("ones"), yq[:, i % 2, :], start=(i == 0), stop=(i == BT - 1)).then_inc(s("var_mm"), 1)

            def attention(layer, nk_of, scores, value, pr, prT, out_of):
                n0 = 32 * layer

                def S_(u):
                    if u >= 3:
                        pe.wait_ge(s("exp_done"), n0 + u - 2)
                    scores(u).then_inc(s("s_done"), 1)

                def turn(u):
                    pe.wait_ge(s("p_norm"), n0 + u + 1)
                    if u >= 2:
                        pe.wait_ge(s("pT_copied"), n0 + u - 1)
                    c0, nkt = nk_of(u)
                    for j in range(nkt):
                        ins = T_(acc[:, 2 + u % 2, j * P:(j + 1) * P], pr[:, u % 3, (c0 + j) * P:(c0 + j + 1) * P])
                    ins.then_inc(s("pT_done"), 1)

                def pv(u):
                    pe.wait_ge(s("pT_copied"), n0 + u + 1)
                    tile = u // 4
                    if u % 4 == 0 and tile >= 2:
                        pe.wait_ge(s("o_lo"), 8 * layer + tile - 1)
                    c0, nkt = nk_of(u)
                    for j in range(nkt):
                        ins = mm(out_of(u), value(u, c0 + j), prT[:, u % 2, j * P:(j + 1) * P], start=(j == 0),
                                 stop=(j == nkt - 1))
                    ins.then_inc(s("pv_done"), 1)

                S_(0)
                S_(1)
                for u in range(32):
                    if u + 2 < 32:
                        S_(u + 2)
                    if u in MOD_STEPS[layer]:
                        mod_unit(KD * (2 + 2 * layer) + MOD_STEPS[layer][u])
                    turn(u)
                    if u:
                        pv(u - 1)
                    if u in MOD_TURN[layer]:
                        mod_T(2 + 2 * layer + MOD_TURN[layer].index(u))
                    if layer == 0:
                        conv_sums(u)
                out_block(layer, 0)
                pv(31)

            def scoresA(u):
                h, t = u // 4, u % 4
                cols = slice(0, T) if t < LT else slice(LAT, T)
                return mm(sbank[u % 3][:, cols], QK[:, A_KV + h, t * P:(t + 1) * P], QK[:, h // 4, cols], start=True,
                          stop=True)

            def square_sums(n, q, t):
                if q in (3, 5, 7):
                    for f in range(q - 3, KD if q == 7 else q - 1):
                        sum_square(n, f, t)
                if q == 7:
                    spread_roots(n, t)

            def out_block(l, n):
                w, kt, hi, lo, t, reads0, waits, norm = OUT[l]
                pair, part = OUT_ORDER[l][n]
                for sem_, count in waits.get(n, ()):
                    pe.wait_ge(sem_, count)
                if n in (4, 6):
                    pe.wait_ge(read_dve, reads0 + pair - 1)
                pe.wait_ge(lo_split, w + n + 1)
                w_h, w_l = split_block(w + n, kt)
                second = n in (2, 3, 5, 7)
                product([acc[:, 2 * (pair % 2) + m, 0:t] for m in range(2)], w_h, w_l,
                        lambda j: (hi[:, kt * part + j, 0:t], lo[:, kt * part + j, 0:t]), kt,
                        first=not second, last=second).then_inc(block_done, 1)
                square_sums(norm, n, t)

            OUT = ((A_OUT, 6, hid_hi, hid_lo, T, after_A_in["dve"],
                    {0: ((s("exp_done"), 32), (s("o_lo"), 6)), 1: ((s("pT_copied"), 32),),
                     2: ((s("o_lo"), 8), (s("mixA_lo"), 4))}, 1),
                   (C_OUT, 8, mixC_hi, mixC_lo, LAT, after_C_in["dve"],
                    {0: ((s("exp_done"), 64), (s("mixC_lo_done"), 8)), 1: ((s("pT_copied"), 64),),
                     2: ((s("o_lo"), 16),)}, 3))

            attention(0, lambda u: (0, 4) if u % 4 < 2 else (2, 2), scoresA,
                      lambda u, j: V[:, j, (u // 16) * P:(u // 16 + 1) * P], prob, probT,
                      lambda u: po[(u // 4) % 2][:, (u % 4) * P:(u % 4 + 1) * P])
            for n in range(1, 8):
                out_block(0, n)

            def out_turn(half):
                for b in range(4):
                    f = 4 * half + b
                    if b % 2 == 0:
                        pe.wait_ge(read_dve, FFN_READS[1][3]["dve"] + f // 2 + 1)
                    for c in range(LT):
                        T_(OUT_BANK[half][c][:, b * P:(b + 1) * P], X[:, f, c * P:(c + 1) * P])\
                            .then_inc(s(f"oT_done{half}"), 1)

            def ffn(l, t):
                w = FF[l][1]
                hid = sum(HALF) // 2 * l
                for half, nt in enumerate(HALF):
                    R, R2 = FFN_READS[l][2 * half], FFN_READS[l][2 * half + 1]
                    pe.wait_ge(read_act, R["act"])
                    pe.wait_ge(read_dve, R["dve"] - 1)

                    def up_or_gate(w, q, it, pair, per):
                        side = q % 2
                        pe.wait_ge(read_dve if side else read_act, at(R["dve" if side else "act"] + pair, it, per))
                        pe.wait_ge(lo_split, at(w + q + 1, it, 4))
                        w_h, w_l = split_block(w + q, KD)
                        product([acc[:, 2 * side + m, 0:t] for m in range(2)], w_h, w_l, H(t), KD,
                                ready=stream_in(2 * l + 1) if half == 0 and q == 0 else None).then_inc(block_done, 1)

                    n_in = nt // 4
                    with pe.Fori(0, n_in) as it:
                        for q in range(4):
                            up_or_gate(w, q, it, q // 2, 2)
                    w += 4 * n_in
                    for q in range(nt % 4):
                        up_or_gate(w, q, None, nt // 2 - 1, 0)
                    w += nt % 4
                    hid += nt // 2
                    pe.wait_ge(read_act, R2["act"])
                    kt = nt // 2

                    def ffn_out(w, q, it, per, pair_use):
                        if q == 0:
                            pe.wait_ge(s("hid_lo_done"), hid - nt // 2 + (kt + 1) // 2)
                        if q == 1:
                            pe.wait_ge(s("hid_lo_done"), hid)                          
                        if q % 2 == 0:
                            pe.wait_ge(read_dve, at(R2["dve"] + pair_use - 1, it, per))  
                        pe.wait_ge(lo_split, at(w + q + 1, it, 2 * per))
                        w_h, w_l = split_block(w + q, kt)                          
                        product([acc[:, q // 2 % 2 * 2 + m, 0:t] for m in range(2)], w_h, w_l,
                                lambda j: (hid_hi[:, kt * (q % 2) + j, 0:t], hid_lo[:, kt * (q % 2) + j, 0:t]),
                                kt, first=(q % 2 == 0), last=(q % 2 == 1)).then_inc(block_done, 1)             

                    if half == 0:
                        with pe.Fori(0, 2) as it:
                            for q in range(4):
                                ffn_out(w, q, it, 2, q // 2)
                    else:
                        for q in range(8):
                            ffn_out(w, q, None, 0, q // 2)
                            if l == 1 and q == 5:
                                out_turn(0)
                            if l == 0:
                                square_sums(2, q, t)
                    w += 8

            ffn(0, T)

            def auxC(m):
                if m == 0:
                    pe.wait_ge(read_act, C_READS[7][1])
                    mm(p5[:, :], cst("pair"), sqK, start=True, stop=True)
                    mm(p6[:, 0:LAT], cst("rotC"), Kc[:, 0:LAT], start=True, stop=True).then_inc(s("aux_done"), 1)
                    return
                pe.wait_ge(read_act, C_READS[7 + m][1])
                for i in range(2):
                    tile = 2 * (m - 1) + i
                    mm(p7[0:16, 0:LAT], cst("headC", 15 - 2 * tile, 31 - 2 * tile), sqQ[(m - 1) % 2][:, i, :],
                       start=(tile == 0), stop=(tile == KD - 1))
                pe.wait_ge(s("rope_done"), 5 + m)
                for i in range(2):
                    ins = mm(p6[:, i * LAT:(i + 1) * LAT], cst("rotC"), Q[:, 2 * (m - 1) + i, :], start=True, stop=True)
                ins.then_inc(s("aux_done"), 1)

            def xs_turn(k):
                t = XS_TILES[k // 2]
                pe.wait_ge(s("xc_ready"), 4 * (k % 2) + 4)
                for b in range(4):
                    f = 4 * (k % 2) + b
                    ins = T_(XS_BANK[k][:, b * P:(b + 1) * P], XC[:, f, t * P:(t + 1) * P])
                ins.then_inc(s("xsT_done"), 1)

            def b_turn(k):
                pe.wait_ge(s("xc_ready"), XBC_T)
                for b in range(4):
                    t, g = XS_TILES[2 * k] + b // 2, b % 2
                    ins = T_((p6, p5)[k][:, b * P:(b + 1) * P], XC[:, 8 + g, t * P:(t + 1) * P])
                ins.then_inc(s("bT_done"), 1)

            w = C_IN
            pe.wait_ge(read_dve, FFN_READS[0][3]["dve"] + 4)
            for n, (kind, _, _) in enumerate(blocksC):
                lo = 2 * (n % 2)
                if n >= 2:
                    who, count = C_READS[n - 2]
                    pe.wait_ge(read_act if who == "act" else read_dve, count)
                pe.wait_ge(lo_split, w + n + 1)
                w_h, w_l = split_block(w + n, KD, 32 if kind == "dt" else BC)
                if kind == "dt":
                    for k in range(KD):
                        xh, xl = H(T)(k)
                        for p_, (wt, xt) in enumerate(((w_h, xh), (w_h, xl), (w_l, xh))):
                            ins = mm(acc[0:32, lo, :], wt[:, k, :], xt, start=(k == 0 and p_ == 0),
                                     stop=(k == KD - 1 and p_ == 2))
                else:
                    t = T if kind == "kv" or kind == "x" and n < 6 else LAT
                    ins = product([acc[:, lo + m, 0:t] for m in range(2)], w_h, w_l, H(t), KD,
                                  ready=stream_in(2) if n == 0 else None)
                ins.then_inc(block_done, 1)
                if n == 2:
                    pe.wait_ge(read_act, C_READS[1][1])
                    for t in range(TT):
                        ins = T_(p7[:, 32 * t:32 * t + 32], dtT[0:32, t * P:(t + 1) * P], 32)
                    ins.then_inc(s("dtT_done"), 1)
                if 8 <= n <= 12:
                    if n == 9:
                        pe.wait_ge(s("dt_ready"), 1)
                    auxC(n - 8)
                if n == 8:
                    for t in range(TT):
                        ins = T_(pmod[:, t * P:(t + 1) * P], vT[:, t * P:(t + 1) * P])
                    ins.then_inc(s("vT_done"), 1)
                if n == 9:
                    pe.wait_ge(s("da_ready"), 1)
                    pe.wait_ge(s("v_ready"), 1)
                    da_of = lambda t, d: dts[:, 7, 32 * t + 16 * d:32 * t + 16 * d + 16]
                    for k, parts in enumerate(CUM):
                        for i, (tri, t, d) in enumerate(parts):
                            ins = mm(pmod[:, 16 * k:16 * k + 16], cst(tri), da_of(t, d), start=(i == 0),
                                     stop=(i == len(parts) - 1))
                    ins.then_inc(s("cum_mm"), 1)
                if n == 12:
                    pe.wait_ge(s("krt_ready"), 3)
                    pe.wait_ge(s("ex_ready"), 1)
                    xs_turn(0)
                    xs_turn(1)
                if n == 13:
                    pe.wait_ge(s("qrow_ready"), 2)
                    pe.wait_ge(s("rope_done"), 10)
                    for t in range(LT):
                        ins = T_(p6[:, 16 * t:16 * t + 16], qrowC[:, t * P:(t + 1) * P], 16)
                    ins.then_inc(s("qrow_T"), 1)
                    pe.wait_ge(s("xs_dve"), 1)
                    xs_turn(2)
                    pe.wait_ge(s("xs_act"), 1)
                    xs_turn(3)
                    xs_turn(4)
                if n == 14:
                    pe.wait_ge(s("xs_dve"), 2)
                    xs_turn(5)
                    pe.wait_ge(s("xs_act"), 2)
                    xs_turn(6)
                    pe.wait_ge(s("xs_dve"), 3)
                    xs_turn(7)
                    pe.wait_ge(s("qsc_copied"), 1)
                    b_turn(0)

            pe.wait_ge(s("xs_act"), 3)
            b_turn(1)
            pe.wait_ge(s("xs_dve"), 4)
            for n in range(4):
                c, g = n // 2, n % 2
                ins = mm(pmod[:, n * P:(n + 1) * P], XC[:, 8 + g, c * P:(c + 1) * P], Cc[:, g, c * P:(c + 1) * P],
                         start=True, stop=True)
            ins.then_inc(s("cb_mm"), 1)
            pe.wait_ge(read_act, after_C_in["act"])
            pe.wait_ge(read_dve, after_C_in["dve"])
            pe.wait_ge(s("btok_ready"), 2)
            for n, (t, k, first, last) in enumerate(((2, 0, 1, 0), (3, 0, 0, 1), (0, 1, 1, 1), (2, 2, 1, 0), (3, 2, 0, 1),
                                                     (1, 3, 1, 1))):
                pe.wait_ge(s("xw_ready"), n + 1)
                if n == 5:
                    pe.wait_ge(s("cb_ready"), 2)
                    pe.wait_ge(s("xs_act"), 4)
                for g in range(2):
                    ins = mm(stbank[2 * k + g], Btok[:, t, g * P:(g + 1) * P], XW[:, n % 2, g * 512:(g + 1) * 512],
                             start=bool(first), stop=bool(last))
                ins.then_inc(s("xw_used"), 1)

            def decays(k):
                if k >= 3:
                    pe.wait_ge(s("cexp_ready"), k - 2)
                pe.wait_ge(s("rx_ready"), k + 1)
                mm(RB[k % 3][:, :], cst("ones"), rx[:, k % 4, :], start=True, stop=True).then_inc(s("R_mm"), 1)

            def sum_y(b):
                for f in (2 * b, 2 * b + 1):
                    pe.wait_ge(s("ysq_ready"), f + 1)
                    mm(pmod[:, 0:LAT], cst("ones"), ysq[:, f % 2, :], start=(f == 0), stop=(f == KD - 1))\
                        .then_inc(s("ssy_mm"), 1)

            pe.wait_ge(s("state_act"), 4)
            decays(0)
            decays(1)
            pe.wait_ge(s("state_dve"), 2)
            decays(2)
            for k in range(16):
                b, c, d = SEG[k]
                if k < 4:
                    pe.wait_ge(s("xdt_ready"), k + 1)
                st = SEG_STATE[(c, d)]
                outs = [acc[64 * (h % 2):64 * (h % 2) + 64, b, h // 2 * LAT + c * P:h // 2 * LAT + (c + 1) * P]
                        for h in range(4)]
                pe.wait_ge(s("m_ready"), k + 1)
                for h in range(4):
                    ins = mm(outs[h], XDT[c][d][:, b, h * S_HD:(h + 1) * S_HD], seg[:, k % 4, h * P:(h + 1) * P],
                             start=(k % 4 == 0 and h < 2), stop=False, skip_group_check=True)
                ins.then_inc(s("intra_mm"), 1)
                if k % 2 and k < 15:
                    pe.wait_ge(s("cd_pool"), k // 2 + 1)
                else:
                    pe.wait_ge(s("cd_dve"), (k + 1) // 2 + 1)
                for h in range(4):
                    hh = 4 * (b % 2) + h
                    ins = mm(outs[h], state[:, st, b // 2, hh * S_HD:(hh + 1) * S_HD], Cd[:, k % 4, h * P:(h + 1) * P],
                             start=False, stop=(k % 4 == 3), skip_group_check=True)
                ins.then_inc(s("inter_mm"), 1)
                if k + 3 < 16:
                    decays(k + 3)
                if k % 4 == 2 and k > 4:
                    sum_y(k // 4 - 1)
            sum_y(3)

            pe.wait_ge(s("k2_ready"), 1)
            pe.wait_ge(s("yg_ready"), KD)
            pe.wait_ge(s("cexp_ready"), 16)

            def scoresC(u):
                tile, t, e = u // 4, (u // 2) % 2, u % 2
                rows_ = slice(64 * e, 64 * e + 64)
                mm(sbank[u % 3], Q[rows_, tile, t * P:(t + 1) * P], K2[rows_, tile // 4, :], start=True, stop=False,
                   skip_group_check=True)
                o = 1 - t
                return mm(sbank[u % 3][:, o * P:(o + 1) * P], ident, cst("mask", t * P, (t + 1) * P), start=False,
                          stop=True, skip_group_check=True)

            attention(1, lambda u: (0, 4), scoresC, lambda u, j: Vc[:, j, (u // 16) * C_HD:(u // 16 + 1) * C_HD], probC,
                      probTC, lambda u: po[(u // 4) % 2][64 * (u % 2):64 * (u % 2) + 64,
                                                       ((u // 2) % 2) * P:((u // 2) % 2 + 1) * P])
            for n in range(1, 8):
                out_block(1, n)
            ffn(1, LAT)
            out_turn(1)


SEG = [(b, c, d) for b in range(4) for c, d in ((0, 0), (1, 0), (1, 1), (0, 1))]
SEG_STATE = {(0, 0): 0, (1, 0): 1, (1, 1): 2, (0, 1): 3}
XS_TILES = (2, 3, 0, 1)
CUM = [
    (("after", 2, 0), ("ones", 3, 0)), (("after", 3, 0),),
    (("before", 2, 1),), (("before", 3, 1), ("ones", 2, 1)),
    (("upto", 0, 0),), (("upto", 1, 0),),
    (("from", 0, 1),), (("from", 1, 1),),
    (("ones", 0, 0),), (("ones", 1, 1),),
    (("after", 0, 0),), (("before", 1, 1),),
]
POOL_TAPS = 21
CONV_DVE = (BT - 1) * B_CONV - (B_CONV - POOL_TAPS) + 1
OUT_ORDER = ([(0, 0), (1, 0), (0, 1), (1, 1), (2, 0), (2, 1), (3, 0), (3, 1)],
             [(0, 1), (1, 1), (0, 0), (1, 0), (2, 1), (2, 0), (3, 1), (3, 0)])
CONV_ORDER = (2, 3, 0, 1)
MOD_STEPS = ({**{u: u for u in range(8)}, **{u: u - 2 for u in range(10, 18)}},
             {16 * g + u: 8 * g + k for g in range(2) for k, u in enumerate((1, 2, 4, 6, 8, 10, 12, 13))})
MOD_TURN = ((8, 18), (14, 30))

INPUTS = ["x", "c", "ctx", "c_ctx", "mod_w", "mod_b", "norm1_g", "norm2_g", "ffn_w_in", "ffn_w_out", "ev_w_in",
          "ev_w_out", "ev_q_g", "ev_k_g", "ev_dw_w", "ev_dw_b", "ev_cn_g", "ev_cn_b", "od_w_in", "od_w_out",
          "od_q_g", "od_k_g", "od_sink", "od_conv_w", "od_conv_b", "od_dt_bias", "od_A_log", "od_D", "od_gnorm_g"]


def kernel(**inputs):
    import concourse.bacc as bacc
    from concourse.bass_utils import run_bass_kernel_spmd

    nc = bacc.Bacc("TRN2", target_bir_lowering=False, num_devices=1)
    arrays, aps = {}, {}
    for name in INPUTS + ["const"]:
        arr = constants() if name == "const" else np.ascontiguousarray(inputs[name])
        arrays[f"in_{name}"] = arr
        aps[name] = nc.dram_tensor(f"in_{name}", arr.shape, mybir.dt.from_np(arr.dtype), kind="ExternalInput").ap()
    out = nc.dram_tensor("out", (1, LAT, D), F32, kind="ExternalOutput").ap()
    build_trunk(nc, aps, out)
    r = run_bass_kernel_spmd(nc, [arrays], core_ids=[0])
    return r.results[0]["out"]
```
